# Optimizing a Trainium2 kernel written in Bass

```python
import jax, jax.numpy as jnp
from jax import lax
import numpy as np

D_MODEL = 1024
BATCH = 1
SEQ = 1024
DEPTH = 2

PLE_DIM = 256
RET_HEADS = 4
RET_HEAD_DIM = 128
SB_HEADS = 4
SB_HEAD_DIM = 128
RET_WIDTH = RET_HEADS * RET_HEAD_DIM
SB_WIDTH = SB_HEADS * SB_HEAD_DIM
EVEN_WIDTH = RET_WIDTH + SB_WIDTH
EVEN_PROJ = 4 * RET_WIDTH + 4 * SB_WIDTH
RET_CHUNK = 128
SB_BLOCK = 128
ROPE_BASE = 10000.0
RWKV_HEAD_DIM = 64
RWKV_HEADS = D_MODEL // RWKV_HEAD_DIM
DECAY_LORA = 64
ICLR_LORA = 64
VRES_LORA = 32
N_EVEN = (DEPTH + 1) // 2
N_ODD = DEPTH // 2
N_VRES = max(N_ODD - 1, 0)
RMS_EPS = 1e-6
GN_EPS = 1e-5
LNX_EPS = 64e-5


def rmsnorm(x, gain):
    xf = x.astype(jnp.float32)
    y = xf * lax.rsqrt(jnp.mean(xf * xf, axis=-1, keepdims=True) + RMS_EPS)
    return (y * gain).astype(x.dtype)

def head_norm(y, eps):
    yf = y.astype(jnp.float32)
    mu = jnp.mean(yf, axis=-1, keepdims=True)
    var = jnp.mean(jnp.square(yf - mu), axis=-1, keepdims=True)
    out = (yf - mu) * lax.rsqrt(var + eps)
    return out.reshape(*y.shape[:-2], -1)

def rotary(x, pos):
    half = x.shape[-1] // 2
    inv_freq = ROPE_BASE ** (-jnp.arange(half, dtype=jnp.float32) / half)
    ang = pos.astype(jnp.float32)[:, None] * inv_freq[None, :]
    cos = jnp.cos(ang)[None, :, None, :]
    sin = jnp.sin(ang)[None, :, None, :]
    x1 = x[..., :half].astype(jnp.float32)
    x2 = x[..., half:].astype(jnp.float32)
    return jnp.concatenate([x1 * cos - x2 * sin, x1 * sin + x2 * cos], axis=-1).astype(x.dtype)

def retention(q, k, v, gn_gain):
    B, S, H, Dh = q.shape
    C = RET_CHUNK
    N = S // C
    pos = jnp.arange(S)
    q = rotary(q, pos)
    k = rotary(k, pos) * (Dh ** -0.5)
    lg = jnp.log(1.0 - 2.0 ** (-5.0 - jnp.arange(H, dtype=jnp.float32)))
    c = jnp.arange(C, dtype=jnp.float32)
    diff = c[:, None] - c[None, :]
    intra = jnp.where(diff[None] >= 0, jnp.exp(jnp.maximum(diff, 0.0)[None] * lg[:, None, None]), 0.0).astype(q.dtype)
    qc = q.reshape(B, N, C, H, Dh)
    kc = k.reshape(B, N, C, H, Dh)
    vc = v.reshape(B, N, C, H, Dh)
    scores = jnp.einsum('bnihd,bnjhd->bnhij', qc, kc) * intra
    out = jnp.einsum('bnhij,bnjhe->bnihe', scores, vc)
    k_dec = kc * jnp.exp((C - 1 - c)[:, None] * lg[None, :]).astype(q.dtype)[:, :, None]
    kv = jnp.einsum('bnjhd,bnjhe->nbhde', k_dec, vc)
    chunk_decay = jnp.exp(C * lg).astype(kv.dtype)[None, :, None, None]

    def carry_step(state, kv_n):
        return state * chunk_decay + kv_n, state

    _, prev = lax.scan(carry_step, jnp.zeros_like(kv[0]), kv)
    q_dec = qc * jnp.exp((c + 1)[:, None] * lg[None, :]).astype(q.dtype)[:, :, None]
    out = out + jnp.einsum('bnihd,nbhde->bnihe', q_dec, prev)
    out = out.reshape(B, S, H, Dh)
    return head_norm(out, GN_EPS) * gn_gain

def stick_breaking(q, k, v):
    B, S, H, Dh = q.shape
    nb = S // SB_BLOCK
    scale = Dh ** -0.5
    key_pos = jnp.arange(S)
    qb = q.reshape(B, nb, SB_BLOCK, H, Dh).transpose(1, 0, 2, 3, 4)

    def block(args):
        q_blk, b_idx = args
        z = jnp.einsum('bqhd,bkhd->bhqk', q_blk, k).astype(jnp.float32) * scale
        q_pos = b_idx * SB_BLOCK + jnp.arange(SB_BLOCK)
        mask = key_pos[None, :] < q_pos[:, None]
        log_1mb = jnp.where(mask, jax.nn.log_sigmoid(-z), 0.0)
        after = lax.cumsum(log_1mb, axis=3, reverse=True) - log_1mb
        w = jnp.where(mask, jnp.exp(jax.nn.log_sigmoid(z) + after), 0.0)
        return jnp.einsum('bhqk,bkhd->bqhd', w.astype(v.dtype), v)

    out = lax.map(block, (qb, jnp.arange(nb)))
    return out.transpose(1, 0, 2, 3, 4).reshape(B, S, H * Dh)

def even_mixer(hn, w_in, w_out, ret_gn_gain):
    B, S, _ = hn.shape
    z = jnp.einsum('bsd,df->bsf', hn, w_in)
    qa, ka, va, ga, qb, kb, vb, gb = jnp.split(z, 8, axis=-1)
    ra = lambda t: t.reshape(B, S, RET_HEADS, RET_HEAD_DIM)
    rb = lambda t: t.reshape(B, S, SB_HEADS, SB_HEAD_DIM)
    o_a = retention(ra(qa), ra(ka), ra(va), ret_gn_gain).astype(hn.dtype)
    o_b = stick_breaking(rb(qb), rb(kb), rb(vb))
    mixed = jnp.concatenate([o_a * jax.nn.silu(ga), o_b * jax.nn.silu(gb)], axis=-1)
    return jnp.einsum('bsf,fd->bsd', mixed, w_out)

def token_shift(x):
    return jnp.pad(x, ((0, 0), (1, 0), (0, 0)))[:, :-1]

def rwkv7_mixer(hn, mu, w_in, w_out, w0, w1, w2, a0, a1, a2, k_k, k_a, r_k, lnx_g, lnx_b, v_first, vres):
    B, S, D = hn.shape
    H, N = RWKV_HEADS, RWKV_HEAD_DIM
    xx = token_shift(hn) - hn
    xs = hn[None] + xx[None] * mu[:, None, None, :]
    r, k, v, g = jnp.einsum('pbsd,pdf->pbsf', xs[:4], w_in)
    xv, xw, xa = xs[2], xs[4], xs[5]
    w_log = -jax.nn.softplus(-(w0 + jnp.tanh(xw @ w1) @ w2)) - 0.5
    decay = jnp.exp(-jnp.exp(w_log.astype(jnp.float32)))
    a = jax.nn.sigmoid(a0 + (xa @ a1) @ a2)
    if v_first is None:
        v_first = v
    else:
        v0, v1, v2 = vres
        v = v + (v_first - v) * jax.nn.sigmoid(v0 + (xv @ v1) @ v2)
    kk = (k * k_k).reshape(B, S, H, N).astype(jnp.float32)
    kk = kk / jnp.maximum(jnp.linalg.norm(kk, axis=-1, keepdims=True), 1e-12)
    k = k * (1.0 + (a - 1.0) * k_a)
    heads = lambda t: t.reshape(B, S, H, N).astype(jnp.float32)
    rh, kh, vh, ah, wh = heads(r), heads(k), heads(v), heads(a), heads(decay)
    tm = lambda t: t.transpose(1, 0, 2, 3)

    def step(state, inp):
        r_t, w_t, k_t, v_t, kk_t, a_t = inp
        sk = jnp.einsum('bhvk,bhk->bhv', state, kk_t)
        state = state * w_t[:, :, None, :] - sk[..., None] * (kk_t * a_t)[:, :, None, :] + v_t[..., None] * k_t[:, :, None, :]
        return state, jnp.einsum('bhvk,bhk->bhv', state, r_t)

    s0 = jnp.zeros((B, H, N, N), jnp.float32)
    _, ys = lax.scan(step, s0, (tm(rh), tm(wh), tm(kh), tm(vh), tm(kk), tm(ah)))
    y = ys.transpose(1, 0, 2, 3)
    y = head_norm(y, LNX_EPS) * lnx_g + lnx_b
    bonus = jnp.sum(rh * kh * r_k, axis=-1, keepdims=True) * vh
    y = (y + bonus.reshape(B, S, D)).astype(hn.dtype)
    out = jnp.einsum('bsf,fd->bsd', y * jax.nn.silu(g), w_out)
    return out, v_first

def first_inputs(seed: int = 0) -> dict:
    key = jax.random.key(seed)
    ks = jax.random.split(key, 32)
    nrm = lambda kk, shape, s: jax.random.normal(kk, shape, jnp.float32) * s
    uni = lambda kk, shape: jax.random.uniform(kk, shape, jnp.float32)
    D = D_MODEL
    return {
        "x": nrm(ks[0], (BATCH, SEQ, D), 1.0),
        "p": nrm(ks[1], (DEPTH, BATCH, SEQ, PLE_DIM), 1.0),
        "norm_gain": 1.0 + nrm(ks[2], (DEPTH, D), 0.1),
        "final_gain": 1.0 + nrm(ks[3], (D,), 0.1),
        "ple_proj": nrm(ks[4], (DEPTH, PLE_DIM, D), PLE_DIM ** -0.5),
        "ple_gate": nrm(ks[5], (DEPTH, D, D), D ** -0.5),
        "even_w_in": nrm(ks[6], (N_EVEN, D, EVEN_PROJ), D ** -0.5),
        "even_w_out": nrm(ks[7], (N_EVEN, EVEN_WIDTH, D), EVEN_WIDTH ** -0.5),
        "ret_gn_gain": 1.0 + nrm(ks[8], (N_EVEN, RET_WIDTH), 0.1),
        "odd_mu": uni(ks[9], (N_ODD, 6, D)),
        "odd_w_in": nrm(ks[10], (N_ODD, 4, D, D), D ** -0.5),
        "odd_w_out": nrm(ks[11], (N_ODD, D, D), D ** -0.5),
        "rwkv_w0": -6.0 + 5.0 * uni(ks[12], (N_ODD, D)),
        "rwkv_w1": nrm(ks[13], (N_ODD, D, DECAY_LORA), D ** -0.5),
        "rwkv_w2": nrm(ks[14], (N_ODD, DECAY_LORA, D), 0.1 * DECAY_LORA ** -0.5),
        "rwkv_a0": nrm(ks[15], (N_ODD, D), 0.1),
        "rwkv_a1": nrm(ks[16], (N_ODD, D, ICLR_LORA), D ** -0.5),
        "rwkv_a2": nrm(ks[17], (N_ODD, ICLR_LORA, D), 0.1 * ICLR_LORA ** -0.5),
        "rwkv_v0": 1.0 + nrm(ks[18], (N_VRES, D), 0.1),
        "rwkv_v1": nrm(ks[19], (N_VRES, D, VRES_LORA), D ** -0.5),
        "rwkv_v2": nrm(ks[20], (N_VRES, VRES_LORA, D), 0.1 * VRES_LORA ** -0.5),
        "rwkv_k_k": 0.85 + nrm(ks[21], (N_ODD, D), 0.1),
        "rwkv_k_a": 1.0 + nrm(ks[22], (N_ODD, D), 0.1),
        "rwkv_r_k": nrm(ks[23], (N_ODD, RWKV_HEADS, RWKV_HEAD_DIM), 0.1),
        "rwkv_lnx_gain": 1.0 + nrm(ks[24], (N_ODD, D), 0.1),
        "rwkv_lnx_bias": nrm(ks[25], (N_ODD, D), 0.02),
    }

def first_block(x, p, norm_gain, final_gain, ple_proj, ple_gate, even_w_in, even_w_out, ret_gn_gain,
              odd_mu, odd_w_in, odd_w_out, rwkv_w0, rwkv_w1, rwkv_w2, rwkv_a0, rwkv_a1, rwkv_a2,
              rwkv_v0, rwkv_v1, rwkv_v2, rwkv_k_k, rwkv_k_a, rwkv_r_k, rwkv_lnx_gain, rwkv_lnx_bias):
    h = x
    v_first = None
    for i in range(DEPTH):
        hn = rmsnorm(h, norm_gain[i])
        if i % 2 == 0:
            e = i // 2
            h = h + even_mixer(hn, even_w_in[e], even_w_out[e], ret_gn_gain[e])
        else:
            o = i // 2
            vres = None if v_first is None else (rwkv_v0[o - 1], rwkv_v1[o - 1], rwkv_v2[o - 1])
            y, v_first = rwkv7_mixer(hn, odd_mu[o], odd_w_in[o], odd_w_out[o], rwkv_w0[o], rwkv_w1[o], rwkv_w2[o],
                                     rwkv_a0[o], rwkv_a1[o], rwkv_a2[o], rwkv_k_k[o], rwkv_k_a[o], rwkv_r_k[o],
                                     rwkv_lnx_gain[o], rwkv_lnx_bias[o], v_first, vres)
            h = h + y
        gate = jax.nn.sigmoid(jnp.einsum('bsd,de->bse', h, ple_gate[i]))
        h = h + gate * jnp.einsum('bsp,pd->bsd', p[i], ple_proj[i])
    return rmsnorm(h, final_gain)


N_MIXERS = 2
ATT_HEADS = 16
ATT_HEAD_DIM = 64
ATT_WIDTH = ATT_HEADS * ATT_HEAD_DIM
QUERY_BLOCK = 128
REC_HEADS = 8
REC_KEY_DIM = 128
REC_VAL_DIM = 128
REC_WIDTH = REC_HEADS * REC_KEY_DIM
REC_VWIDTH = REC_HEADS * REC_VAL_DIM
CHUNK = 64
N_ATT_LAYERS = (DEPTH + 1) // 2
N_REC_LAYERS = DEPTH // 2
EPS = 1e-6


def rms_norm(x, gain):
    xf = x.astype(jnp.float32)
    y = xf * lax.rsqrt(jnp.mean(xf * xf, axis=-1, keepdims=True) + EPS)
    return (y * gain.astype(jnp.float32)).astype(x.dtype)

def fox_attention(q, k, v, c):
    B, H, S, hd = q.shape
    scale = hd ** -0.5
    kpos = jnp.arange(S)

    def block(i):
        start = i * QUERY_BLOCK
        qb = lax.dynamic_slice_in_dim(q, start, QUERY_BLOCK, axis=2)
        cb = lax.dynamic_slice_in_dim(c, start, QUERY_BLOCK, axis=2)
        s = jnp.einsum('bhqd,bhkd->bhqk', qb, k).astype(jnp.float32) * scale
        s = s + (cb[..., :, None] - c[..., None, :])
        qpos = start + jnp.arange(QUERY_BLOCK)
        s = jnp.where(kpos[None, :] <= qpos[:, None], s, -jnp.inf)
        w = jax.nn.softmax(s, axis=-1)
        return jnp.einsum('bhqk,bhkd->bhqd', w.astype(v.dtype), v)

    out = lax.map(block, jnp.arange(S // QUERY_BLOCK))
    return out.transpose(1, 0, 3, 2, 4).reshape(B, S, H * hd)

def fox_mixer(u, w_in, b_f, w_out):
    B, S, _ = u.shape
    proj = u @ w_in
    q, k, v, g, fl = jnp.split(proj, [ATT_WIDTH, 2 * ATT_WIDTH, 3 * ATT_WIDTH, 4 * ATT_WIDTH], axis=-1)
    heads = lambda t: t.reshape(B, S, ATT_HEADS, ATT_HEAD_DIM).transpose(0, 2, 1, 3)
    log_f = jax.nn.log_sigmoid(fl.astype(jnp.float32) + b_f.astype(jnp.float32))
    c = jnp.cumsum(log_f, axis=1).transpose(0, 2, 1)
    attn = fox_attention(heads(q), heads(k), heads(v), c)
    return (attn * jax.nn.silu(g)) @ w_out

def hgrn2_mixer(u, w_in, lb, out_gain, w_out):
    B, S, _ = u.shape
    proj = u @ w_in
    q, fl, inp, g = jnp.split(proj, [REC_WIDTH, 2 * REC_WIDTH, 2 * REC_WIDTH + REC_VWIDTH], axis=-1)
    lbf = lb.astype(jnp.float32)
    log_f = jnp.logaddexp(jnp.log(lbf), jnp.log1p(-lbf) + jax.nn.log_sigmoid(fl.astype(jnp.float32)))
    k = -jnp.expm1(log_f)

    def chunks(t, dh):
        return t.astype(jnp.float32).reshape(B, S // CHUNK, CHUNK, REC_HEADS, dh).transpose(1, 0, 3, 2, 4)

    qc, kc, gc = chunks(q, REC_KEY_DIM), chunks(k, REC_KEY_DIM), chunks(log_f, REC_KEY_DIM)
    ic = chunks(inp, REC_VAL_DIM)
    causal = jnp.tril(jnp.ones((CHUNK, CHUNK), dtype=bool))

    def step(state, xs):
        qb, kb, gb, ib = xs
        b = jnp.cumsum(gb, axis=-2)
        diff = b[..., :, None, :] - b[..., None, :, :]
        decay = jnp.exp(jnp.where(causal[:, :, None], diff, -jnp.inf))
        scores = jnp.einsum('bhtd,bhsd,bhtsd->bhts', qb, kb, decay)
        o = scores @ ib + jnp.einsum('bhtd,bhdv->bhtv', qb * jnp.exp(b), state)
        b_last = b[..., -1:, :]
        state = jnp.exp(b_last[..., 0, :])[..., None] * state + \
            jnp.einsum('bhsd,bhsv->bhdv', kb * jnp.exp(b_last - b), ib)
        return state, o

    state0 = jnp.zeros((B, REC_HEADS, REC_KEY_DIM, REC_VAL_DIM), jnp.float32)
    _, o = lax.scan(step, state0, (qc, kc, gc, ic))
    o = o.transpose(1, 0, 3, 2, 4).reshape(B, S, REC_HEADS, REC_VAL_DIM)
    o = o * lax.rsqrt(jnp.mean(o * o, axis=-1, keepdims=True) + EPS) * out_gain.astype(jnp.float32)
    gh = g.astype(jnp.float32).reshape(B, S, REC_HEADS, REC_VAL_DIM)
    y = (o * jax.nn.silu(gh)).reshape(B, S, REC_VWIDTH).astype(u.dtype)
    return y @ w_out

def second_inputs(seed: int = 0) -> dict:
    key = jax.random.key(seed)
    ks = jax.random.split(key, 14)
    nrm = jax.random.normal
    D = D_MODEL
    return {
        "x": nrm(ks[0], (BATCH, SEQ, D), jnp.float32),
        "p": nrm(ks[1], (DEPTH, BATCH, SEQ, PLE_DIM), jnp.float32),
        "norm_pre": 1.0 + 0.05 * nrm(ks[2], (DEPTH, D), jnp.float32),
        "norm_post": 1.0 + 0.05 * nrm(ks[3], (DEPTH, D), jnp.float32),
        "att_w_in": nrm(ks[4], (N_ATT_LAYERS, D, 4 * ATT_WIDTH + ATT_HEADS), jnp.float32) * D ** -0.5,
        "att_b_f": jax.random.uniform(ks[5], (N_ATT_LAYERS, ATT_HEADS), jnp.float32, 1.0, 6.0),
        "att_w_out": nrm(ks[6], (N_ATT_LAYERS, ATT_WIDTH, D), jnp.float32) * ATT_WIDTH ** -0.5,
        "rec_w_in": nrm(ks[7], (N_REC_LAYERS, D, 2 * REC_WIDTH + 2 * REC_VWIDTH), jnp.float32) * D ** -0.5,
        "rec_lb": 1.0 + 0.1 * nrm(ks[8], (DEPTH, REC_WIDTH), jnp.float32),
        "rec_out_norm": 1.0 + 0.05 * nrm(ks[9], (N_REC_LAYERS, REC_VAL_DIM), jnp.float32),
        "rec_w_out": nrm(ks[10], (N_REC_LAYERS, REC_VWIDTH, D), jnp.float32) * REC_VWIDTH ** -0.5,
        "ple_w_proj": nrm(ks[11], (DEPTH, PLE_DIM, D), jnp.float32) * PLE_DIM ** -0.5,
        "ple_w_gate": nrm(ks[12], (DEPTH, D, D), jnp.float32) * D ** -0.5,
    }

def second_block(x, p, norm_pre, norm_post, att_w_in, att_b_f, att_w_out, rec_w_in, rec_lb,
              rec_out_norm, rec_w_out, ple_w_proj, ple_w_gate):
    sm = jax.nn.softmax(rec_lb.astype(jnp.float32), axis=0)
    lower_bounds = jnp.cumsum(sm, axis=0) - sm[0:1]
    h = x
    for layer in range(DEPTH):
        u = rms_norm(h, norm_pre[layer])
        j = layer // N_MIXERS
        if layer % N_MIXERS == 0:
            y = fox_mixer(u, att_w_in[j], att_b_f[j], att_w_out[j])
        else:
            y = hgrn2_mixer(u, rec_w_in[j], lower_bounds[layer], rec_out_norm[j], rec_w_out[j])
        h = h + rms_norm(y, norm_post[layer])
        gate = jax.nn.sigmoid((h @ ple_w_gate[layer]).astype(jnp.float32)).astype(h.dtype)
        h = h + (p[layer] @ ple_w_proj[layer]) * gate
    return h


def setup_inputs(seed=0):
    out = dict(first_inputs(seed))
    for name, value in second_inputs(seed + 1).items():
        if name != "x":
            out[name + "_2"] = value
    return out


def reference(
    x, p, norm_gain, final_gain, ple_proj, ple_gate, even_w_in, even_w_out, ret_gn_gain, odd_mu,
    odd_w_in, odd_w_out, rwkv_w0, rwkv_w1, rwkv_w2, rwkv_a0, rwkv_a1, rwkv_a2, rwkv_v0, rwkv_v1,
    rwkv_v2, rwkv_k_k, rwkv_k_a, rwkv_r_k, rwkv_lnx_gain, rwkv_lnx_bias, p_2, norm_pre_2,
    norm_post_2, att_w_in_2, att_b_f_2, att_w_out_2, rec_w_in_2, rec_lb_2, rec_out_norm_2,
    rec_w_out_2, ple_w_proj_2, ple_w_gate_2,
):
    x = first_block(
        x, p, norm_gain, final_gain, ple_proj, ple_gate, even_w_in, even_w_out, ret_gn_gain,
        odd_mu, odd_w_in, odd_w_out, rwkv_w0, rwkv_w1, rwkv_w2, rwkv_a0, rwkv_a1, rwkv_a2,
        rwkv_v0, rwkv_v1, rwkv_v2, rwkv_k_k, rwkv_k_a, rwkv_r_k, rwkv_lnx_gain, rwkv_lnx_bias,
    )
    return second_block(
        x, p_2, norm_pre_2, norm_post_2, att_w_in_2, att_b_f_2, att_w_out_2, rec_w_in_2,
        rec_lb_2, rec_out_norm_2, rec_w_out_2, ple_w_proj_2, ple_w_gate_2,
    )


_drawn_inputs = setup_inputs


def setup_inputs(seed=0):
    import zlib

    import numpy as np

    out = dict(_drawn_inputs(seed))
    spreads = {}
    factors = {'rwkv_w1': 8.0, 'rwkv_w2': 8.0, 'rwkv_lnx_bias': 3.798}
    for name, (base, spread) in spreads.items():
        noise = np.random.default_rng([zlib.crc32(name.encode()), seed]).standard_normal(out[name].shape)
        drawn = base * np.exp(spread * noise) if base else spread * noise
        out[name] = __import__('jax').numpy.asarray(drawn.astype(out[name].dtype))
    for name, factor in factors.items():
        out[name] = (out[name] * factor).astype(out[name].dtype)
    return out
```

```python
from contextlib import ExitStack

import numpy as np

import concourse.bass as bass
from concourse import mybir

P = 128
S = 1024
D = 1024
NS = S // P
NK = D // P
F32 = mybir.dt.float32
R32 = mybir.dt.float32r
I32 = mybir.dt.int32
ALU = mybir.AluOpType
ACT = mybir.ActivationFunctionType
AX = mybir.AxisListType.X
RMS_EPS = 1e-6
GN_EPS = 1e-5
LNX_EPS = 64e-5
RSQRT_CAP = 1e12
NEG = -1.0e30
SQRT_E_INV = float(np.exp(-0.5))


def shape_constants():
    half = 64
    inv = np.float32(10000.0) ** (-np.arange(half, dtype=np.float32) / np.float32(half))
    ang = (np.arange(S, dtype=np.float32)[:, None] * inv[None, :]).astype(np.float32).astype(np.float64)
    cos = np.cos(ang).reshape(NS, P, half).transpose(1, 0, 2)
    sin = np.sin(ang).reshape(NS, P, half).transpose(1, 0, 2)
    lg = np.log(1.0 - 2.0 ** (-5.0 - np.arange(4, dtype=np.float64)))
    c = np.arange(P, dtype=np.float64)
    scale = 128.0 ** -0.5
    diff = c[None, :] - c[:, None]
    intra = np.where(diff[:, None, :] >= 0, np.exp(np.maximum(diff, 0.0)[:, None, :] * lg[None, :, None]), 0.0) * scale
    kdec = np.exp((P - 1 - c)[:, None] * lg[None, :]) * scale
    qdec = np.exp((c + 1)[:, None] * lg[None, :])
    after = (c[None, :] > c[:, None]).astype(np.float64)
    upto = (c[None, :] >= c[:, None]).astype(np.float64)
    levels = []
    for m in (64, 32, 16, 8, 4, 2, 1):
        blk = np.floor(c / (2 * m))
        first = np.floor(c / m) % 2 == 0
        levels.append(((blk[:, None] == blk[None, :]) & first[:, None] & ~first[None, :]).astype(np.float64))
    levels.append(np.eye(P))
    heads2 = (np.floor(c / 64)[:, None] == np.floor(c / 64)[None, :]).astype(np.float64)
    reset = np.ones((P, S))
    reset[:, ::P] = 0.0
    f = lambda a: np.ascontiguousarray(np.asarray(a, np.float32).reshape(P, -1))
    parts = {
        "ident": f(np.eye(P)), "cos": f(cos), "sin": f(sin), "intra": f(intra), "kdec": f(kdec), "qdec": f(qdec),
        "after": f(after), "upto": f(upto), "before": f(after.T),
        "ntri": f(-upto.T), "nones": f(-np.ones((P, P))), "neg": f(np.where(after > 0, NEG, 0.0)),
        "levels": f(np.stack(levels, 1)), "heads2": f(heads2), "cols2": f(heads2[:, ::64]), "reset": f(reset),
    }
    where, at = {}, 0
    for name, a in parts.items():
        where[name] = (at, a.shape[1])
        at += a.shape[1]
    return np.concatenate(list(parts.values()), 1), where


class Line:

    def __init__(self, sem):
        self.todo, self.sem, self.n, self.seen = [], sem, 0, {}

    @property
    def last(self):
        return (self.sem, self.n)

    def wait(self, *tokens):
        for t in tokens:
            if t is None:
                continue
            if isinstance(t, list):
                self.wait(*t)
                continue
            sem, value = t
            if value > self.seen.get(id(sem), 0):
                self.seen[id(sem)] = value
                self.todo.append(lambda e, sem=sem, value=value: e.wait_ge(sem, value))

    def do(self, fn, *tokens):
        self.wait(*tokens)
        self.n += 1
        self.todo.append(lambda e: fn(e).then_inc(self.sem, 1))
        return (self.sem, self.n)

    def go(self, fn, *tokens):
        self.wait(*tokens)
        self.todo.append(fn)

    def run(self, e):
        for fn in self.todo:
            fn(e)


class Chan:

    def __init__(self, sem):
        self.sem, self.n = sem, 0

    @property
    def last(self):
        return (self.sem, 16 * self.n)

    def dma(self, line, out, in_, *tokens):
        line.wait(*tokens)
        self.n += 1
        line.todo.append(lambda e: e.dma_start(out, in_).then_inc(self.sem, 16))
        return (self.sem, 16 * self.n)


class Slot:

    def __init__(self, v, chan=None):
        self.v, self.chan, self.busy = v, chan, []


class Ring:
    def __init__(self, slots):
        self.slots, self.i = slots, 0

    def take(self):
        s = self.slots[self.i % len(self.slots)]
        self.i += 1
        return s


class Ctx:
    def __init__(self, nc, ctx, consts, where, scratch):
        self.nc, self.ctx, self.consts, self.where, self.scratch = nc, ctx, consts, where, scratch
        sem = lambda n: ctx.enter_context(nc.semaphore(n))
        self.pe, self.ve, self.ac, self.po, self.sp = (Line(sem(n)) for n in ("s_pe", "s_ve", "s_ac", "s_po", "s_sp"))
        self.lines = [self.pe, self.ve, self.ac, self.po, self.sp]
        self.chans = [Chan(sem(f"d{i}")) for i in range(80)]
        self.nch = 0
        self.banks = [ctx.enter_context(nc.psum_tensor(f"bank{i}", [P, 512], F32)) for i in range(8)]
        self.bank_slots = [Slot(b) for b in self.banks]
        self.XH = ctx.enter_context(nc.sbuf_tensor("XH", [P, NK, S], R32))
        self.XL = ctx.enter_context(nc.sbuf_tensor("XL", [P, NK, S], R32))
        self.ident = ctx.enter_context(nc.sbuf_tensor("ident", [P, P], F32))
        self.xt = [[] for _ in range(NS)]
        self.xk = [[] for _ in range(NK)]
        self.nph, self.drop = 0, None
        self.tid = self.chan().dma(self.sp, self.ident[:, :], self.const_in("ident"))

    def const_in(self, name):
        a, n = self.where[name]
        return self.consts[:, a:a + n]

    def chan(self):
        c = self.chans[self.nch]
        self.nch += 1
        return c

    def phase(self):
        if self.nph:
            self.stack.close()
            if self.drop is not None:
                self.drop.close()
                self.drop = None
            marks = [l.last for l in self.lines] + [c.last for c in self.chans if c.n]
            for l in self.lines:
                l.wait([m for m in marks if m[1] and m[0] is not l.sem or l in (self.ve, self.ac, self.po, self.pe) and m[1]])
        self.nph += 1
        self.nch = 1
        self.stack = ExitStack()

    def sb(self, name, shape, dt=F32):
        return self.stack.enter_context(self.nc.sbuf_tensor(f"{name}_{self.nph}", shape, dt))

    def psum(self, ids):
        return Ring([self.bank_slots[i] for i in ids])

    def const(self, name, shape=None):
        n = self.where[name][1]
        t = self.sb(name, [P, n])
        tok = self.chan().dma(self.sp, t[:, :], self.const_in(name))
        return t, tok

    def buf(self, name, shape, n, dt=F32):
        return Ring([Slot(self.sb(f"{name}{i}", shape, dt), self.chan()) for i in range(n)])


def f32(ap):
    return ap.bitcast(F32)


class Weights:

    def __init__(self, c, srcs, raw=4, ahead=1, pad=False):
        self.c, self.srcs, self.ahead = c, srcs, ahead
        self.raw = c.buf("wraw", [P, 2, 512], raw)
        self.slots = Ring([Slot((c.sb(f"wh{i}", [P, NK, 512], R32), c.sb(f"wl{i}", [P, NK, 512], R32)))
                           for i in range(2)])
        self.got = []

    def prepare(self, upto):
        c = self.c
        while len(self.got) < min(upto, len(self.srcs)):
            src = self.srcs[len(self.got)]
            n = src.shape[1]
            slot = self.slots.take()
            h, l = slot.v
            toks = []
            for j in range(NK // 2):
                r = self.raw.take()
                t = r.chan.dma(c.sp, r.v[:, :, 0:n], src[256 * j:256 * (j + 1), :].rearrange("(a p) n -> p a n", p=P),
                               *r.busy)
                hj, lj, rj = h[:, 2 * j:2 * j + 2, 0:n], l[:, 2 * j:2 * j + 2, 0:n], r.v[:, :, 0:n]
                th = c.po.do(lambda e, hj=hj, rj=rj: e.tensor_copy(hj, rj), t, *slot.busy)
                tl = c.ve.do(lambda e, hj=hj, lj=lj, rj=rj: e.tensor_tensor(lj, rj, f32(hj), ALU.subtract),
                             th, t, *slot.busy)
                r.busy = [tl]
                toks.append([th, tl])
            slot.busy = []
            self.got.append((slot, toks))

    def get(self, i, more=None):
        self.prepare(i + 1 + (self.ahead if more is None else more))
        return self.got[i]


def mm_group(c, bank, terms, *tokens):
    for i, (out, lhsT, rhs) in enumerate(terms):
        fn = lambda e, out=out, lhsT=lhsT, rhs=rhs, i=i: e.matmul(
            out, lhsT, rhs, start=(i == 0), stop=(i == len(terms) - 1))
        if i < len(terms) - 1:
            c.pe.go(fn, *(tokens if i == 0 else ()))
        else:
            return c.pe.do(fn, *(tokens if i == 0 else ()))


def big_product(c, bank, out, xs, w, wtoks, xtoks, x_is_lhs):
    last = None
    for k in range(NK):
        (xh, xl), (wh, wl) = xs(k), w(k)
        for j, (a, b) in enumerate(((xh, wh), (xl, wh), (xh, wl))):
            lhsT, rhs = (a, b) if x_is_lhs else (b, a)
            first, stop = k == 0 and j == 0, k == NK - 1 and j == 2
            fn = lambda e, lhsT=lhsT, rhs=rhs, first=first, stop=stop: e.matmul(
                out, lhsT, rhs, start=first, stop=stop)
            tokens = ([bank.busy, xtoks] if first else []) + ([wtoks[k // 2], c.xk[k]] if j == 0 else [])
            if stop:
                last = c.pe.do(fn, *tokens)
            else:
                c.pe.go(fn, *tokens)
    bank.busy = [last]
    return last


def seq_tile(c, bank, s, w, n=512, off=0):
    slot, toks = w
    h, l = slot.v
    t = big_product(c, bank, bank.v[:, off:off + n],
                    lambda k: (c.XH[:, k, s * P:(s + 1) * P], c.XL[:, k, s * P:(s + 1) * P]),
                    lambda k: (h[:, k, 0:n], l[:, k, 0:n]), toks, c.xt[s], True)
    slot.busy = [t]
    return t


def feat_tile(c, bank, f, sh, w):
    slot, toks = w
    h, l = slot.v
    t = big_product(c, bank, bank.v[:, :],
                    lambda k: (c.XH[:, k, sh * 512:(sh + 1) * 512], c.XL[:, k, sh * 512:(sh + 1) * 512]),
                    lambda k: (h[:, k, f * P:(f + 1) * P], l[:, k, f * P:(f + 1) * P]), toks,
                    [t for s in range(4 * sh, 4 * sh + 4) for t in c.xt[s]], False)
    slot.busy = [t]
    return t


def to_xt(c, rows, s, tbanks, *tokens):
    out = []
    for half in range(2):
        b = tbanks.take()
        for j in range(4):
            k = 4 * half + j
            fn = lambda e, b=b, j=j, k=k: e.transpose(b.v[:, j * P:(j + 1) * P], rows[:, k * P:(k + 1) * P],
                                                      c.ident[:, :])
            if j < 3:
                c.pe.go(fn, *tokens, c.tid, *b.busy)
            else:
                tt = c.pe.do(fn, *tokens)
        out += split_out(c, b, lambda t, half=half: t[:, 4 * half:4 * half + 4, s * P:(s + 1) * P], tt)
    c.xt[s] = out
    return tt


def split_out(c, bank, part, *tokens):
    src = bank.v[:, :].rearrange("p (a b) -> p a b", a=4)
    th = c.ac.do(lambda e: e.activation(part(c.XH), src, ACT.Copy), *tokens)
    tl = c.ve.do(lambda e: e.tensor_tensor(part(c.XL), src, f32(part(c.XH)), ALU.subtract), th, *tokens)
    bank.busy = [th, tl]
    return [th, tl]


def rsqrt(c, ap, *tokens):
    t = c.ac.do(lambda e: e.activation(ap, ap, ACT.Sqrt), *tokens)
    return c.ve.do(lambda e: e.reciprocal(ap, ap), t)


def rms_scale(c, sq, st, srcs, width, eps, *tokens):
    toks = []
    for i, a in enumerate(srcs):
        toks.append(c.ac.do(lambda e, a=a, i=i: e.activation(sq[:, 0:a.shape[1]], a, ACT.Square,
                                                             accum_out=st[:, i:i + 1]), *tokens, c.ac.last))
    if len(srcs) == 2:
        t = c.ve.do(lambda e: e.tensor_tensor(st[:, 0:1], st[:, 0:1], st[:, 1:2], ALU.add), *toks)
    else:
        t = toks[0]
    t = c.ve.do(lambda e: e.tensor_scalar(st[:, 2:3], st[:, 0:1], 1.0 / width, eps, ALU.mult, ALU.add), t)
    return rsqrt(c, st[:, 2:3], t), toks


def row_gain(c, name, src):
    t = c.sb(name, [P, D])
    return t, c.chan().dma(c.sp, t[:, :], src.rearrange("(a n) -> a n", a=1).to_broadcast([P, D]))


def start(c, x, gain):
    c.phase()
    g, tg = row_gain(c, "g", gain)
    rows, tmp = c.buf("h", [P, D], 2), c.buf("tmp", [P, D], 2)
    sq = c.sb("sq", [P, D])
    sts = c.buf("st", [P, 4], 2)
    tb = c.psum(range(4))
    for s in range(NS):
        r, m, st = rows.take(), tmp.take(), sts.take()
        t = r.chan.dma(c.sp, r.v[:, :], x[s * P:(s + 1) * P, :], *r.busy)
        tr, _ = rms_scale(c, sq, st.v, [r.v[:, :]], D, RMS_EPS, t, *st.busy)
        tm = c.ve.do(lambda e, r=r, m=m, st=st: e.scalar_tensor_tensor(
            out=m.v[:, :], in0=r.v[:, :], scalar=st.v[:, 2:3], in1=g[:, :], op0=ALU.mult, op1=ALU.mult),
            tr, tg, *m.busy)
        r.busy, st.busy = [tm], [tm]
        m.busy = [to_xt(c, m.v, s, tb, tm)]
    c.h = x
    c.h_tok = [None] * NS


def project(c, srcs, modes, dst, w=None, first=0, silu=()):
    w = w or Weights(c, srcs)
    mm = c.psum(range(8))
    stage = c.stage
    toks = []
    for i, mode in enumerate(modes):
        ready = w.get(first + i)
        for j in range(8):
            b, st = mm.take(), stage.take()
            if mode == "seq":
                t = seq_tile(c, b, j, ready)
            else:
                t = feat_tile(c, b, j // 2, j % 2, ready)
            f = ACT.Sigmoid if i in silu else ACT.Copy
            t = c.ac.do(lambda e, b=b, st=st, f=f: e.activation(st.v[:, :], b.v[:, :], f), t, *st.busy)
            if i in silu:
                t = c.ve.do(lambda e, b=b, st=st: e.tensor_tensor(st.v[:, :], b.v[:, :], st.v[:, :], ALU.mult), t)
            b.busy = [t]
            out = dst[i](j)
            st.busy = [st.chan.dma(c.sp, out, st.v[:, :], t)]
            toks += st.busy
    return toks


def layer_end(c, w_out, p, ple_w, gate_w, next_gain, post_gain=None, mid_gain=None, out=None):
    c.phase()
    w = Weights(c, [w_out[:, 0:512], w_out[:, 512:1024], gate_w[:, 0:512], gate_w[:, 512:1024]], raw=2)
    H = c.sb("H", [P, NS, D])
    pT = c.sb("pT", [P, 2, S])
    pw = c.sb("pw", [P, 2, D])
    tmp = c.buf("tmp", [P, D], 1)
    sg = c.buf("sg", [P, 512], 2)
    sts = c.buf("st", [P, 4], 2)
    tb = c.psum([6, 7])
    mm = c.psum(range(6))
    gains = []
    chans = [c.chan() for _ in range(NS)]
    th = [chans[s].dma(c.sp, H[:, s, :], c.h[s * P:(s + 1) * P, :], c.h_tok[s]) for s in range(NS)]
    if post_gain is not None:
        pg, tpg = row_gain(c, "pg", post_gain)
    w.get(0, more=1)
    tpw = c.chan().dma(c.sp, pw[:, :, :], ple_w.rearrange("(a p) n -> p a n", p=P))
    pt = tmp.take()
    tpt = []
    for q in range(2):
        t = pt.chan.dma(c.sp, pt.v[:, :].rearrange("p (a n) -> p a n", a=4),
                        p[512 * q:512 * (q + 1), :].rearrange("(a p) n -> p a n", p=P), *pt.busy)
        for k in range(2):
            b = tb.take()
            for a in range(4):
                fn = lambda e, b=b, a=a, k=k: e.transpose(b.v[:, a * P:(a + 1) * P],
                                                          pt.v[:, a * 256 + k * P:a * 256 + (k + 1) * P], c.ident[:, :])
                if a < 3:
                    c.pe.go(fn, t, c.tid, *b.busy)
                else:
                    tt = c.pe.do(fn)
            b.busy = [c.ac.do(lambda e, b=b, q=q, k=k: e.activation(pT[:, k, 512 * q:512 * (q + 1)], b.v[:, :], ACT.Copy), tt)]
            tpt += b.busy
            pt.busy = [tt]
    ready = [None] * NS
    w0, w1 = w.got[0], w.got[1]
    for s in range(NS + 1):
        if s < NS:
            bs = [mm.take(), mm.take()]
            ts = [seq_tile(c, bs[0], s, w0), seq_tile(c, bs[1], s, w1)]
            if post_gain is None:
                for half in range(2):
                    hs = H[:, s, 512 * half:512 * (half + 1)]
                    ts[half] = c.ve.do(lambda e, hs=hs, b=bs[half]: e.tensor_tensor(hs, b.v[:, :], hs, ALU.add),
                                       ts[half], th[s])
                    bs[half].busy = [ts[half]]
            else:
                st = sts.take()
                sq = sg.take()
                tr, tq = rms_scale(c, sq.v, st.v, [bs[0].v[:, :], bs[1].v[:, :]], D, RMS_EPS, *ts, *st.busy, *sq.busy)
                sq.busy = tq
                m = tmp.take()
                for half in range(2):
                    cs = slice(512 * half, 512 * (half + 1))
                    t = c.ve.do(lambda e, b=bs[half], st=st, cs=cs, m=m: e.scalar_tensor_tensor(
                        out=m.v[:, cs], in0=b.v[:, :], scalar=st.v[:, 2:3], in1=pg[:, cs], op0=ALU.mult, op1=ALU.mult),
                        tr, tpg, *m.busy)
                    bs[half].busy = [t, *tq]
                    ts[half] = c.ve.do(lambda e, s=s, cs=cs, m=m: e.tensor_tensor(H[:, s, cs], m.v[:, cs], H[:, s, cs], ALU.add),
                                       t, th[s])
                st.busy, m.busy = [t], [ts[1]]
            ready[s] = ts
        if s > 0:
            to_xt(c, H[:, s - 1, :], s - 1, tb, *ready[s - 1])
    w.get(2, more=1)
    w0, w1 = w.got[2], w.got[3]
    ng, tng = (pw, tpw) if next_gain is None else row_gain(c, "ng", next_gain)
    if mid_gain is not None:
        mg, tmg = row_gain(c, "mg", mid_gain)
    toks = [None] * NS
    pending = None
    for s in range(NS + 1):
        if s < NS:
            for half, wt in ((0, w0), (1, w1)):
                cs = slice(512 * half, 512 * (half + 1))
                gb, pb, g = mm.take(), mm.take(), sg.take()
                tg = seq_tile(c, gb, s, wt)
                tp = mm_group(c, pb, [(pb.v[:, :], pT[:, k, s * P:(s + 1) * P], pw[:, k, cs]) for k in range(2)],
                              *tpt, tpw, *pb.busy)
                tg = c.ac.do(lambda e, g=g, gb=gb: e.activation(g.v[:, :], gb.v[:, :], ACT.Sigmoid), tg, *g.busy)
                gb.busy = [tg]
                tp = c.ve.do(lambda e, g=g, pb=pb: e.tensor_tensor(g.v[:, :], pb.v[:, :], g.v[:, :], ALU.mult), tp, tg)
                pb.busy = [tp]
                t = c.ve.do(lambda e, g=g, s=s, cs=cs: e.tensor_tensor(H[:, s, cs], H[:, s, cs], g.v[:, :], ALU.add), tp)
                g.busy = [t]
            hs = H[:, s, :]
            if mid_gain is not None:
                st, m = sts.take(), tmp.take()
                tr, tq = rms_scale(c, m.v, st.v, [hs], D, RMS_EPS, t, *st.busy, *m.busy)
                m.busy = tq
                t = c.ve.do(lambda e, hs=hs, st=st: e.scalar_tensor_tensor(
                    out=hs, in0=hs, scalar=st.v[:, 2:3], in1=mg[:, :], op0=ALU.mult, op1=ALU.mult), tr, tmg, *tq)
                st.busy = [t]
            toks[s] = chans[s].dma(c.sp, (c.scratch["h"] if out is None else out)[s * P:(s + 1) * P, :], hs, t)
        if s > 0 and next_gain is not None:
            st, m = sts.take(), tmp.take()
            tr, tq = rms_scale(c, m.v, st.v, [H[:, s - 1, :]], D, RMS_EPS, pending, *st.busy, *m.busy)
            tm = c.ve.do(lambda e, s=s, m=m, st=st: e.scalar_tensor_tensor(
                out=m.v[:, :], in0=H[:, s - 1, :], scalar=st.v[:, 2:3], in1=ng[:, :], op0=ALU.mult, op1=ALU.mult),
                tr, tng, *tq)
            st.busy = [tm]
            m.busy = [to_xt(c, m.v, s - 1, tb, tm)]
        pending = t
    c.h, c.h_tok = c.scratch["h"], toks


def V(c, fn, *tokens):
    return c.ve.do(fn, *tokens)


def tt(out, a, b, op):
    return lambda e: e.tensor_tensor(out, a, b, op)


def stt(out, a, s, b, op0, op1):
    return lambda e: e.scalar_tensor_tensor(out=out, in0=a, scalar=s, in1=b, op0=op0, op1=op1)


def act(out, a, f, **kw):
    return lambda e: e.activation(out, a, f, **kw)


def ts(out, a, s1, s2, op0, op1=None):
    if op1 is None:
        return lambda e: e.tensor_scalar(out, a, s1, s2, op0)
    return lambda e: e.tensor_scalar(out, a, s1, s2, op0, op1)


def cp(out, a):
    return lambda e: e.tensor_copy(out, a)


def last_axis(ap, shape):
    return ap.unsqueeze(len(ap.shape)).to_broadcast(shape)


def mid_axis(ap, shape):
    return ap.unsqueeze(1).to_broadcast(shape)


def transposes(c, bank, srcs, *tokens):
    for i, a in enumerate(srcs):
        fn = lambda e, i=i, a=a: e.transpose(bank[:, i * P:(i + 1) * P], a, c.ident[:, :])
        if i < len(srcs) - 1:
            c.pe.go(fn, *tokens, c.tid)
        else:
            return c.pe.do(fn, *tokens, c.tid)


def part_matmuls(c, items, *tokens):
    for i, (out, lhsT, rhs) in enumerate(items):
        fn = lambda e, out=out, lhsT=lhsT, rhs=rhs: e.matmul(out, lhsT, rhs, start=True, stop=True)
        if i < len(items) - 1:
            c.pe.go(fn, *tokens)
        else:
            return c.pe.do(fn, *tokens)


def normed_heads(c, o, y, st, eps, *tokens):
    nh = o.shape[1]
    stats, mv = st
    for h in range(nh):
        t = V(c, lambda e, h=h: e.bn_stats(stats[:, h, :], o[:, h, :]), *tokens)
    for h in range(nh):
        t2 = V(c, lambda e, h=h: e.bn_aggr(mv[:, h, :], stats[:, h, :]), t)
    t = V(c, ts(mv[:, :, 1], mv[:, :, 1], eps, None, ALU.add), t2)
    t = rsqrt(c, mv[:, :, 1], t)
    for h in range(nh):
        t2 = V(c, ts(y[:, h, :], o[:, h, :], mv[:, h, 0:1], mv[:, h, 1:2], ALU.subtract, ALU.mult), t)
    return t2


def retention(c, z, ztok, gn_gain):
    c.phase()
    cos, t0 = c.const("cos")
    sin, t1 = c.const("sin")
    intra, t2 = c.const("intra")
    kdec, t3 = c.const("kdec")
    qdec, t4 = c.const("qdec")
    gn = c.sb("gn", [P, 512])
    t5 = c.chan().dma(c.sp, gn[:, :], gn_gain.rearrange("(a n) -> a n", a=1).to_broadcast([P, 512]))
    tk = [t0, t1, t2, t3, t4, t5]
    cos = cos[:, :].rearrange("p (n j) -> p n j", j=64)
    sin = sin[:, :].rearrange("p (n j) -> p n j", j=64)
    intra = intra[:, :]
    zs = c.buf("z", [P, 2048], 2)
    two = lambda n, shape: c.buf(n, shape, 2)
    As, Bs, kds, qkTs, scs, os_, ys, sgs = (two(n, s) for n, s in (
        ("A", [P, 1024]), ("B", [P, 1024]), ("kd", [P, 512]), ("qkT", [P, 1024]), ("sc", [P, 512]),
        ("o", [P, 512]), ("y", [P, 512]), ("sg", [P, 512])))
    stats, mv = c.sb("stats", [P, 4, 6]), c.sb("mv", [P, 4, 2])
    state = c.sb("state", [P, 4, P])
    lg = np.log(1.0 - 2.0 ** (-5.0 - np.arange(4, dtype=np.float64)))
    cd = [float(np.exp(P * x)) for x in lg]
    tb, sb_, ob, ib, kb, xb = (c.psum(x) for x in ([0, 1], [2], [3], [4], [5], [6, 7]))
    tstate = None
    ty = None
    for n in range(NS):
        zr, A, B, kd, qkT, sc, o, y, sg = (r.take() for r in (zs, As, Bs, kds, qkTs, scs, os_, ys, sgs))
        tz = zr.chan.dma(c.sp, zr.v[:, :], z[n * P:(n + 1) * P, 0:2048], ztok, *zr.busy)
        qk = zr.v[:, 0:1024].rearrange("p (h a j) -> p h a j", h=8, a=2)
        Av = A.v[:, :].rearrange("p (h a j) -> p h a j", h=8, a=2)
        Bv = B.v[:, :].rearrange("p (h a j) -> p h a j", h=8, a=2)
        b8 = lambda t: t[:, n, :].unsqueeze(1).to_broadcast([P, 8, 64])
        ta = V(c, tt(Av[:, :, 0, :], qk[:, :, 0, :], b8(cos), ALU.mult), tz, *tk, *A.busy)
        ta = V(c, tt(Av[:, :, 1, :], qk[:, :, 1, :], b8(cos), ALU.mult))
        tb1 = c.po.do(tt(Bv[:, :, 0, :], qk[:, :, 1, :], b8(sin), ALU.mult), tz, *tk, *B.busy)
        tb2 = c.po.do(tt(Bv[:, :, 1, :], qk[:, :, 0, :], b8(sin), ALU.mult))
        ta = V(c, tt(Av[:, :, 0, :], Av[:, :, 0, :], Bv[:, :, 0, :], ALU.subtract), ta, tb2)
        ta = V(c, tt(Av[:, :, 1, :], Av[:, :, 1, :], Bv[:, :, 1, :], ALU.add), ta, tb2)
        B.busy = [ta]
        v = zr.v[:, 1024:1536].rearrange("p (h e) -> p h e", h=4)
        kdv = kd.v[:, :].rearrange("p (h e) -> p h e", h=4)
        tkd = V(c, tt(kdv, A.v[:, 512:1024].rearrange("p (h e) -> p h e", h=4),
                      last_axis(kdec[:, :], [P, 4, P]), ALU.mult), ta, *kd.busy)
        tq = []
        for j in range(2):
            b = tb.take()
            t = transposes(c, b.v, [A.v[:, 512 * j + P * h:512 * j + P * (h + 1)] for h in range(4)], ta, *b.busy)
            b.busy = [c.ac.do(act(qkT.v[:, 512 * j:512 * (j + 1)], b.v[:, :], ACT.Copy), t, *qkT.busy)]
            tq += b.busy
        A.busy = [t, tkd]
        q = lambda h: qkT.v[:, h * P:(h + 1) * P]
        k = lambda h: qkT.v[:, 512 + h * P:512 + (h + 1) * P]
        b = sb_.take()
        t = part_matmuls(c, [(b.v[:, h * P:(h + 1) * P], k(h), q(h)) for h in range(4)], *tq, *b.busy)
        tsc = V(c, tt(sc.v[:, :], b.v[:, :], intra, ALU.mult), t, *sc.busy)
        b.busy = [tsc]
        bi = ib.take()
        ti = None
        if n:
            ti = part_matmuls(c, [(bi.v[:, h * P:(h + 1) * P], q(h), state[:, h, :]) for h in range(4)],
                              *tq, tstate, *bi.busy)
        bk = kb.take()
        tkv = part_matmuls(c, [(bk.v[:, h * P:(h + 1) * P], kdv[:, h, :], v[:, h, :]) for h in range(4)],
                           tkd, tz, *bk.busy)
        bo = ob.take()
        to = part_matmuls(c, [(bo.v[:, h * P:(h + 1) * P], sc.v[:, h * P:(h + 1) * P], v[:, h, :])
                              for h in range(4)], tsc, *bo.busy)
        qkT.busy, sc.busy, kd.busy = [to], [to], [to]
        for h in range(4):
            hs = slice(h * P, (h + 1) * P)
            if n:
                t = V(c, stt(state[:, h, :], state[:, h, :], cd[h], bk.v[:, hs], ALU.mult, ALU.add), tkv, ti, tstate)
            else:
                t = V(c, cp(state[:, h, :], bk.v[:, hs]), tkv)
        tstate = t
        bk.busy = [t]
        if n:
            t = V(c, tt(o.v[:, :].rearrange("p (h e) -> p h e", h=4), bi.v[:, :].rearrange("p (h e) -> p h e", h=4),
                        last_axis(qdec[:, :], [P, 4, P]), ALU.mult), ti, *o.busy)
            bi.busy = [t]
            t = V(c, tt(o.v[:, :], o.v[:, :], bo.v[:, :], ALU.add), to, t)
        else:
            t = V(c, cp(o.v[:, :], bo.v[:, :]), to, *o.busy)
        bo.busy = [t]
        ty = normed_heads(c, o.v[:, :].rearrange("p (h e) -> p h e", h=4), y.v[:, :].rearrange("p (h e) -> p h e", h=4),
                          (stats, mv), GN_EPS, t, ty, *y.busy)
        o.busy = [ty]
        tg = c.ac.do(act(sg.v[:, :], zr.v[:, 1536:2048], ACT.Sigmoid), tz, *sg.busy)
        t = c.po.do(tt(sg.v[:, :], sg.v[:, :], zr.v[:, 1536:2048], ALU.mult), tg)
        t = c.po.do(tt(sg.v[:, :], sg.v[:, :], gn[:, :], ALU.mult), t)
        zr.busy = [t, to, tkv, ta, tb2]
        t = V(c, tt(y.v[:, :], y.v[:, :], sg.v[:, :], ALU.mult), t, ty)
        sg.busy = [t]
        ty = t
        b = xb.take()
        t = transposes(c, b.v, [y.v[:, h * P:(h + 1) * P] for h in range(4)], t, *b.busy)
        y.busy = [t]
        c.xt[n] = split_out(c, b, lambda X, n=n: X[:, 0:4, n * P:(n + 1) * P], t)


def stick(c, z, zt, ztok):
    c.phase()
    ntri, t0 = c.const("ntri")
    nones, t1 = c.const("nones")
    after, t2 = c.const("after")
    tk = [t0, t1, t2]
    qs, ks, gs, vs, gg = (c.buf(n, [P, S], 2) for n in ("q", "k", "g", "v", "gg"))
    a_, l_, sp_, w_ = (c.buf(n, [P, 512], 3) for n in ("a", "l", "sp", "w"))
    R = c.buf("R", [P, 512], 2)
    mix = c.buf("mix", [P, 512], 2)
    zb, ob = c.psum([0, 1, 2, 3, 4, 5]), c.psum([6, 7])
    scale = 128.0 ** -0.5
    for h in range(4):
        q, k, g, v, gf = (r.take() for r in (qs, ks, gs, vs, gg))
        tq = q.chan.dma(c.sp, q.v[:, :], zt[h * P:(h + 1) * P, :], ztok, *q.busy)
        tkk = k.chan.dma(c.sp, k.v[:, :], zt[512 + h * P:512 + (h + 1) * P, :], *k.busy)
        tg = g.chan.dma(c.sp, g.v[:, :], zt[1024 + h * P:1024 + (h + 1) * P, :], *g.busy)
        tv = v.chan.dma(c.sp, v.v[:, :].rearrange("p (a e) -> p a e", a=NS),
                        z[:, 2048 + h * P:2048 + (h + 1) * P].rearrange("(a p) e -> p a e", p=P), *v.busy)
        tq = V(c, ts(q.v[:, :], q.v[:, :], scale, None, ALU.mult), tq)
        t = c.ac.do(act(gf.v[:, :], g.v[:, :], ACT.Sigmoid), tg, *gf.busy)
        tg = c.po.do(tt(gf.v[:, :], gf.v[:, :], g.v[:, :], ALU.mult), t)
        g.busy = [tg]
        for half in range(2):
            o, r, mx = ob.take(), R.take(), mix.take()
            tr = c.po.do(lambda e, r=r: e.memset(r.v[:, :], 0.0), *r.busy)
            top = 4 * half + 3
            to = None
            for kb in range(top, -1, -1):
                off = max(0, kb - 4 * half) * P
                cs, n = slice(off, 512), 512 - off
                qc = slice(512 * half + off, 512 * (half + 1))
                b, a, l, sp, w = (x.take() for x in (zb, a_, l_, sp_, w_))
                tz = c.pe.do(lambda e, b=b, k=k, q=q, kb=kb, n=n, qc=qc: e.matmul(
                    b.v[:, 0:n], k.v[:, kb * P:(kb + 1) * P], q.v[:, qc], start=True, stop=True), tq, tkk, *b.busy)
                t = c.ac.do(act(a.v[:, 0:n], b.v[:, 0:n], ACT.Abs), tz, *a.busy)
                t = c.ac.do(act(a.v[:, 0:n], a.v[:, 0:n], ACT.Exp, scale=-1.0), t)
                t = c.ac.do(act(l.v[:, 0:n], a.v[:, 0:n], ACT.Ln, bias=1.0), t, *l.busy)
                a.busy = [t]
                t = V(c, stt(sp.v[:, 0:n], b.v[:, 0:n], 0.0, l.v[:, 0:n], ALU.max, ALU.add), t, *sp.busy)
                l.busy = [t]
                if kb >= 4 * half:
                    t = V(c, tt(sp.v[:, 0:P], sp.v[:, 0:P], after[:, :], ALU.mult), t, *tk)
                c.pe.go(lambda e, b=b, sp=sp, n=n: e.matmul(b.v[:, 0:n], ntri[:, :], sp.v[:, 0:n], start=False,
                                                            stop=False, skip_group_check=True), t, *tk)
                tz = c.pe.do(lambda e, b=b, r=r, n=n, cs=cs: e.matmul(
                    b.v[:, 0:n], nones[:, :], r.v[:, cs], start=False, stop=True, skip_group_check=True), tr)
                if kb:
                    tr = c.po.do(tt(r.v[:, cs], r.v[:, cs], sp.v[:, 0:n], ALU.add), t, tz, tr)
                sp.busy = [tz, tr]
                t = c.ac.do(act(w.v[:, 0:n], b.v[:, 0:n], ACT.Exp), tz, *w.busy)
                b.busy = [t]
                if kb >= 4 * half:
                    t = c.po.do(tt(w.v[:, 0:P], w.v[:, 0:P], after[:, :], ALU.mult), t, *tk)
                to = c.pe.do(lambda e, o=o, v=v, w=w, kb=kb, n=n, cs=cs, top=top: e.matmul(
                    o.v[:, cs], v.v[:, kb * P:(kb + 1) * P], w.v[:, 0:n], start=(kb == top), stop=(kb == 0),
                    skip_group_check=True), t, tv, *o.busy)
                w.busy = [to]
            r.busy = [to]
            qc = slice(512 * half, 512 * (half + 1))
            t = V(c, tt(mx.v[:, :], o.v[:, :], gf.v[:, qc], ALU.mult), to, tg, *mx.busy)
            o.busy = [t]
            th = c.ac.do(act(c.XH[:, 4 + h, qc], mx.v[:, :], ACT.Copy), t)
            tl = V(c, tt(c.XL[:, 4 + h, qc], mx.v[:, :], f32(c.XH[:, 4 + h, qc]), ALU.subtract), th, t)
            mx.busy = [tl, th]
            for s in range(4 * half, 4 * half + 4):
                c.xt[s] = c.xt[s] + [th, tl]
        q.busy, k.busy, v.busy, gf.busy = [to], [to], [to], [t]


def layer_even(c, i, xt_stage=True):
    c.phase()
    z, zt = c.scratch["z"], c.scratch["zt"]
    c.stage = c.buf("stage", [P, 512], 4)
    win = i["even_w_in"][0]
    order = [(0, "seq", 0), (1, "seq", 512), (2, "seq", 1024), (3, "seq", 1536), (4, "feat", 0), (5, "feat", 512),
             (6, "seq", 2048), (7, "feat", 1024)]
    dst = []
    for blk, mode, at in order:
        if mode == "seq":
            dst.append(lambda j, at=at: z[j * P:(j + 1) * P, at:at + 512])
        else:
            dst.append(lambda j, at=at: zt[at + (j // 2) * P:at + (j // 2 + 1) * P, (j % 2) * 512:(j % 2 + 1) * 512])
    tok = project(c, [win[:, 512 * b:512 * (b + 1)] for b, _, _ in order], [m for _, m, _ in order], dst)
    retention(c, z, tok, i["ret_gn_gain"][0])
    stick(c, z, zt, tok)


VECS = {"mu": 0, "w0": 48, "a0": 56, "k_k": 64, "k_a": 72, "r_k": 80}


def per_feature(c, i, bank):
    rows, vt = c.sb("vrows", [88, P]), c.sb("vt", [P, 88])
    blk = lambda a: a.rearrange("(k q) -> k q", q=P)
    srcs = [i["odd_mu"][0].rearrange("p (k q) -> (p k) q", q=P), blk(i["rwkv_w0"][0]), blk(i["rwkv_a0"][0]),
            blk(i["rwkv_k_k"][0]), blk(i["rwkv_k_a"][0]), i["rwkv_r_k"][0].rearrange("(k a) q -> k (a q)", a=2)]
    at, toks = 0, []
    for a in srcs:
        n = a.shape[0]
        toks.append(c.chan().dma(c.sp, rows[at:at + n, :], a))
        at += n
    t = c.pe.do(lambda e: e.transpose(bank.v[:, 0:88], rows[:, :], c.ident[0:88, 0:88]), c.tid, *toks, *bank.busy)
    t = V(c, cp(vt[:, :], bank.v[:, 0:88]), t)
    bank.busy = [t]
    return vt, t


def shifted(c, n, HN, vt, omu, us, xs, tokens, last):
    for k in range(NK):
        u, x = us.take(), xs.take()
        t = c.ac.do(act(u.v[:, :], HN[:, k, 1:S + 1], ACT.Copy, scale=omu[:, 8 * n + k:8 * n + k + 1]), *tokens, *u.busy)
        t = V(c, stt(x.v[:, :], HN[:, k, 0:S], vt[:, 8 * n + k:8 * n + k + 1], u.v[:, :], ALU.mult, ALU.add), t, *x.busy)
        u.busy = [t]
        th = c.ac.do(act(c.XH[:, k, :], x.v[:, :], ACT.Copy), t, last)
        tl = V(c, tt(c.XL[:, k, :], x.v[:, :], f32(c.XH[:, k, :]), ALU.subtract), th, last)
        x.busy = [tl]
        c.xk[k] = [th, tl]


def layer_odd(c, i):
    c.phase()
    c.keep = ExitStack()
    z, zt = c.scratch["z"], c.scratch["zt"]
    c.stage = c.buf("stage", [P, 512], 4)
    win = i["odd_w_in"][0]
    tabs = [win[n][:, 512 * j:512 * (j + 1)] for n in range(4) for j in range(2)]
    w = Weights(c, tabs + [i["rwkv_w1"][0], i["rwkv_a1"][0]], raw=3)
    HN = c.sb("HN", [P, NK, S + 1])
    us, xs = c.buf("u", [P, S], 1), c.buf("x", [P, S], 2)
    lo = [c.keep.enter_context(c.nc.sbuf_tensor(f"lora{n}", [64, S], F32, side="right")) for n in range(2)]
    vt, tvt = per_feature(c, i, c.bank_slots[0])
    omu = c.sb("omu", [P, 48])
    to = V(c, ts(omu[:, :], vt[:, 0:48], -1.0, 1.0, ALU.mult, ALU.add), tvt)
    t0 = c.po.do(lambda e: e.memset(HN[:, :, 0:1], 0.0))
    hn = [V(c, tt(HN[:, k, 1:S + 1], f32(c.XH[:, k, :]), f32(c.XL[:, k, :]), ALU.add), *[c.xt[s] for s in range(NS)])
          for k in range(NK)]
    c.xt = [[] for _ in range(NS)]
    tokens = [t0, to, tvt, *hn]
    last, toks = None, []
    for n in range(4):
        shifted(c, n, HN, vt, omu, us, xs, tokens, last)
        dst = []
        for j in range(2):
            at = 1024 * n + 512 * j
            if n < 2:
                dst.append(lambda q, at=at: zt[at + (q // 2) * P:at + (q // 2 + 1) * P,
                                               (q % 2) * 512:(q % 2 + 1) * 512])
            else:
                dst.append(lambda q, at=at - 2048: z[q * P:(q + 1) * P, at:at + 512])
        toks += project(c, None, ["feat" if n < 2 else "seq"] * 2, dst, w, first=2 * n, silu=(0, 1) if n == 3 else ())
        last = c.pe.last
    mm = c.psum(range(8))
    for n in range(2):
        shifted(c, 4 + n, HN, vt, omu, us, xs, tokens, last)
        ready = w.get(8 + n)
        for sh in range(2):
            b = mm.take()
            t = feat_tile(c, b, 0, sh, ready)
            b.busy = [c.ac.do(act(lo[n][:, 512 * sh:512 * (sh + 1)], b.v[0:64, :], ACT.Copy if n else ACT.Tanh), t)]
        last = c.pe.last
    c.xk = [[] for _ in range(NK)]
    rwkv(c, i, z, zt, toks, lo)
    c.drop = c.keep


def alternate(*gens):
    gens = [g for g in gens if g is not None]
    while gens:
        for g in list(gens):
            try:
                next(g)
            except StopIteration:
                gens.remove(g)


def rwkv(c, i, z, zt, ztok, lo):
    c.phase()
    after, t0 = c.const("after")
    upto, t1 = c.const("upto")
    levels, t3 = c.const("levels")
    heads2, t4 = c.const("heads2")
    cols2, t5 = c.const("cols2")
    tk = [t0, t1, t3, t4, t5]
    vt, tvt = per_feature(c, i, c.bank_slots[0])
    vec = lambda n, p: vt[:, VECS[n] + p:VECS[n] + p + 1]
    mask4 = c.sb("mask4", [P, 4, P])
    tm4 = [V(c, ts(mask4[:, 0, :], after[:, :], -1.0, None, ALU.mult), *tk),
           V(c, ts(mask4[:, 1, :], upto[:, :], -1.0, None, ALU.mult)),
           V(c, cp(mask4[:, 2, :], after[:, :])), V(c, cp(mask4[:, 3, :], upto[:, :]))]
    eye = c.ident
    wab = c.buf("wab", [64, 2, P], 2)
    lnr = c.buf("ln", [P, 2, P], 2)
    one = lambda n, shape, k=1: c.buf(n, shape, k)
    rb, kb = one("r", [P, S]), one("k", [P, S])
    gb = one("g", [P, P], 3)
    vz = one("vz", [P, NS, 2, P], 2)
    ab, lb, bb, t1b, t2b = (one(n, [P, S]) for n in ("a", "lw", "b", "t1", "t2"))
    arb = one("ar", [P, NS, 2, P], 2)
    kap, bet = one("kap", [P, S]), one("bet", [P, S])
    kas, bes = one("kas", [P, S], 2), one("bes", [P, S], 2)
    gf = one("gf", [P, NS], 2)
    bon = one("bon", [P, 2 * NS], 2)
    mk = one("mk", [P, 4, 512], 2)
    nm, T, TT, X = (one(n, [P, 4, P], 1) for n in ("nm", "T", "TT", "X"))
    ttf = one("ttf", [P, 4, P], 2)
    rz, uz = one("rz", [P, 3, P], 1), one("uz", [P, 3, P], 1)
    st = one("S", [P, P], 2)
    yb = one("y", [P, P], 2)
    stats, mv = c.sb("stats", [P, 2, 6]), c.sb("mv", [P, 2, 2])
    zero = [c.po.do(lambda e, v=v: e.memset(v, 0.0)) for v in
            [s.v[:, :, :, :] for s in vz.slots] + [rz.slots[0].v[:, :, :], uz.slots[0].v[:, :, :]]]
    mb, lbk, xb, tb, sq1, sq2 = c.psum([0, 1]), c.psum([2]), c.psum([3, 4]), c.psum([5]), c.psum([6]), c.psum([7])
    halves = [slice(0, 512), slice(512, 1024)]
    r3 = lambda t: t[:, :].rearrange("p (a e) -> p a e", a=NS)

    def prepare(p, res):
        r, k, VZ, wa, ln = (x.take() for x in (rb, kb, vz, wab, lnr))
        ps = slice(p * P, (p + 1) * P)
        tr = r.chan.dma(c.sp, r.v[:, :], zt[ps, :], ztok, *r.busy)
        tkk = k.chan.dma(c.sp, k.v[:, :], zt[1024 + p * P:1024 + (p + 1) * P, :], *k.busy)
        for n in range(2):
            tw = wa.chan.dma(c.sp, wa.v[:, n, :], i[("rwkv_w2", "rwkv_a2")[n]][0][:, ps], *wa.busy)
        for n in range(2):
            tln = ln.chan.dma(c.sp, ln.v[:, n, :], i[("rwkv_lnx_gain", "rwkv_lnx_bias")[n]][0][ps]
                              .rearrange("(a n) -> a n", a=1).to_broadcast([P, P]), *ln.busy)
        for hh in range(2):
            at = p * P + 64 * hh
            tv = VZ.chan.dma(c.sp, VZ.v[:, :, hh, 64 * hh:64 * hh + 64],
                             z[:, at:at + 64].rearrange("(a p) e -> p a e", p=P), zero, *VZ.busy)
        yield
        a, l, b, s1, s2 = (x.take() for x in (ab, lb, bb, t1b, t2b))
        ta, tl = [], []
        for dst, n, name, out in ((a, 1, "a0", ta), (l, 0, "w0", tl)):
            for hf in halves:
                bk = tb.take()
                t = mm_group(c, bk, [(bk.v[:, :], wa.v[:, n, :], lo[n][:, hf])], tw, *bk.busy)
                out.append(c.ac.do(act(dst.v[:, hf], bk.v[:, :], ACT.Sigmoid, bias=vec(name, p)), t, tvt, *dst.busy))
                bk.busy = [out[-1]]
            yield
        wa.busy = [t]
        t = V(c, ts(l.v[:, :], l.v[:, :], -SQRT_E_INV, None, ALU.mult), *tl)
        for n in range(NS):
            ns = slice(n * P, (n + 1) * P)
            tb_ = V(c, lambda e, ns=ns: e.tensor_tensor_scan(b.v[:, ns], l.v[:, ns], l.v[:, ns], 0.0, ALU.add,
                                                             ALU.bypass), t, *b.busy)
            if n == 3:
                yield
        yield
        kk = s1
        t = V(c, ts(kk.v[:, :], k.v[:, :], vec("k_k", p), None, ALU.mult), tkk, tvt, *s1.busy)
        tkn = t
        t = V(c, tt(s2.v[:, :], kk.v[:, :], kk.v[:, :], ALU.mult), t, *s2.busy)
        tn = []
        for hf in halves:
            bk = tb.take()
            t_ = mm_group(c, bk, [(bk.v[:, :], heads2[:, :], s2.v[:, hf])], t, *tk, *bk.busy)
            bk.busy = [c.ac.do(act(s2.v[:, hf], bk.v[:, :], ACT.Sqrt), t_)]
            tn += bk.busy
        yield
        t = V(c, ts(s2.v[:, :], s2.v[:, :], 1e-12, None, ALU.max), *tn)
        t = V(c, lambda e: e.reciprocal(s2.v[:, :], s2.v[:, :]), t)
        yield
        tkn = V(c, tt(kk.v[:, :], kk.v[:, :], s2.v[:, :], ALU.mult), t, tkn)
        t = V(c, ts(s2.v[:, :], a.v[:, :], 1.0, vec("k_a", p), ALU.subtract, ALU.mult), tkn, *ta)
        yield
        tkk = V(c, stt(k.v[:, :], s2.v[:, :], 1.0, k.v[:, :], ALU.add, ALU.mult), t, tkk)
        ta2 = c.po.do(tt(a.v[:, :], a.v[:, :], kk.v[:, :], ALU.mult), t, tkn)
        yield
        bo, bk = bon.take(), tb.take()
        t = V(c, stt(s2.v[:, :], r.v[:, :], vec("r_k", p), k.v[:, :], ALU.mult, ALU.mult), tr, tkk)
        t = part_matmuls(c, [(bk.v[:, 2 * n:2 * n + 2], s2.v[:, n * P:(n + 1) * P], cols2[:, :]) for n in range(NS)],
                         t, *tk, *bk.busy)
        tbo = V(c, cp(bo.v[:, :], bk.v[:, 0:2 * NS]), t, *bo.busy)
        bk.busy = [tbo]
        G = gf.take()
        mid = r3(b.v)[:, :, 63:64]
        t = V(c, tt(G.v[:, 0:7], r3(b.v)[:, 0:7, P - 1], r3(b.v)[:, 0:7, 63], ALU.subtract), tb_, *G.busy)
        t = V(c, tt(G.v[:, 0:7], G.v[:, 0:7], r3(b.v)[:, 1:8, 63], ALU.add), t)
        tG = c.ac.do(act(G.v[:, 0:7], G.v[:, 0:7], ACT.Exp), t)
        yield
        tD = V(c, tt(r3(s2.v), r3(b.v), mid.to_broadcast([P, NS, P]), ALU.subtract), tbo, tb_)
        t3_ = V(c, tt(l.v[:, :], s2.v[:, :], l.v[:, :], ALU.subtract), tD, tb_)
        tE3 = c.ac.do(act(l.v[:, :], l.v[:, :], ACT.Exp), t3_)
        tE1 = c.ac.do(act(b.v[:, :], s2.v[:, :], ACT.Exp), tD, t)
        tE2 = c.ac.do(act(s2.v[:, :], s2.v[:, :], ACT.Exp, scale=-1.0), t3_, tE1)
        res.update(r=r, k=k, a=a, l=l, b=b, s1=s1, s2=s2, VZ=VZ, G=G, bo=bo, ln=ln, p=p, tG=tG, tbo=tbo, tz=[tv],
                   tln=tln, tal=[tE3, tkn], trh=[tE1, tr], tka=[tE2, tkk], tbe=[tE2, ta2])
        yield

    def factors(d):
        r, k, a, l, b, kk, s2 = (d[n] for n in ("r", "k", "a", "l", "b", "s1", "s2"))
        AR, ka, be, KA, BE = (x.take() for x in (arb, kap, bet, kas, bes))
        tka = V(c, tt(ka.v[:, :], k.v[:, :], s2.v[:, :], ALU.mult), *d["tka"], *ka.busy)
        tbe = c.po.do(tt(be.v[:, :], a.v[:, :], s2.v[:, :], ALU.mult), *d["tbe"], *be.busy)
        tal = V(c, tt(AR.v[:, :, 0, :], r3(kk.v), r3(l.v), ALU.mult), *d["tal"], *AR.busy)
        yield
        trh = c.po.do(tt(AR.v[:, :, 1, :], r3(r.v), r3(b.v), ALU.mult), *d["trh"], *AR.busy)
        yield
        tks = []
        for src, dst, t, sc in ((ka, KA, tka, 1.0), (be, BE, tbe, -1.0)):
            for q in range(2):
                bk = tb.take()
                t_ = transposes(c, bk.v, [src.v[:, (4 * q + j) * P:(4 * q + j + 1) * P] for j in range(4)], t, *bk.busy)
                bk.busy = [c.ac.do(act(dst.v[:, 512 * q:512 * (q + 1)], bk.v[:, :], ACT.Copy, scale=sc), t_, *dst.busy)]
                tks += bk.busy
                yield
        for n, t in (("r", trh), ("k", tka), ("a", tbe), ("l", tal), ("b", trh), ("s1", tal)):
            d[n].busy = [t]
        d["s2"].busy = [tka, tbe]
        d.update(AR=AR, ka=ka, be=be, KA=KA, BE=BE, tar=[tal, trh], tkb=[tka, tbe], tks=tks)

    def inverse(d, grp, res):
        M, FT = mk.take(), ttf.take()
        AR, ka, be = d["AR"], d["ka"], d["be"]
        units = [(2 * grp + u // 2, u % 2) for u in range(4)]
        tM = []
        for u, (n, hh) in enumerate(units):
            hr, ns = slice(64 * hh, 64 * hh + 64), slice(n * P, (n + 1) * P)
            b = mb.take()
            rhs = AR.v[hr, n, :, :].rearrange("p a t -> p (a t)")
            t = part_matmuls(c, [(b.v[:, 0:256], be.v[hr, ns], rhs), (b.v[:, 256:512], ka.v[hr, ns], rhs)],
                             *d["tar"], *d["tkb"], *b.busy)
            b.busy = [V(c, tt(M.v[:, u, :], b.v[:, :], mask4[:, :, :].rearrange("p a t -> p (a t)"), ALU.mult), t,
                        *tm4, *M.busy)]
            tM += b.busy
            yield
        d["last_use"] = t
        b3 = lambda m: m.unsqueeze(1).to_broadcast([P, 4, P])
        lvl = lambda l: levels[:, l * P:(l + 1) * P]
        v4 = lambda b: b.v[:, :].rearrange("p (u t) -> p u t", u=4)
        NT = M.v[:, :, 0:P]
        t_, tt_, x_, m_ = T.take(), TT.take(), X.take(), nm.take()
        tm = c.po.do(tt(m_.v[:, :, :], NT, b3(lvl(6)), ALU.mult), *tM, *m_.busy)
        lk = lbk.take()
        tL = transposes(c, lk.v, [m_.v[:, u, :] for u in range(4)], tm, *lk.busy)
        tT = V(c, tt(t_.v[:, :, :], v4(lk), b3(eye[:, :]), ALU.add), tL, *t_.busy)
        lk.busy = [tT]
        t = tm
        tTT = c.po.do(tt(tt_.v[:, :, :], m_.v[:, :, :], b3(eye[:, :]), ALU.add), t, *tt_.busy)
        yield
        tx = None
        for l in range(5, -1, -1):
            tm = c.po.do(tt(m_.v[:, :, :], NT, b3(lvl(l)), ALU.mult), [tTT, tL] if l == 5 else tX)
            b = xb.take()
            tX = part_matmuls(c, [(b.v[:, u * P:(u + 1) * P], m_.v[:, u, :], t_.v[:, u, :]) for u in range(4)],
                              tm, tT, *b.busy)
            tx = c.ac.do(act(x_.v[:, :, :], v4(b), ACT.Copy), tX, tx, *x_.busy)
            b.busy = [tx]
            yield
            bt = xb.take()
            tTT2 = part_matmuls(c, [(bt.v[:, u * P:(u + 1) * P], x_.v[:, u, :], tt_.v[:, u, :]) for u in range(4)],
                                tx, tTT, *bt.busy)
            if l:
                b = xb.take()
                t1_ = part_matmuls(c, [(b.v[:, u * P:(u + 1) * P], tt_.v[:, u, :], x_.v[:, u, :]) for u in range(4)],
                                   *b.busy)
                tTT = V(c, tt(tt_.v[:, :, :], tt_.v[:, :, :], v4(bt), ALU.add), tTT2, t1_, tTT)
                bt.busy = [tTT]
                tT = V(c, tt(t_.v[:, :, :], t_.v[:, :, :], v4(b), ALU.add), t1_, tT)
                b.busy = [tT]
                x_.busy = [t1_]
            else:
                tTT = V(c, tt(FT.v[:, :, :], tt_.v[:, :, :], v4(bt), ALU.add), tTT2, tTT, *FT.busy)
                bt.busy = [tTT]
                t_.busy, tt_.busy, x_.busy, m_.busy = [tX], [tTT, tTT2], [tTT2], [tX]
            yield
        res.update(M=M, FT=FT, tM=tM, tT=tTT, d=d, grp=grp)

    def chain(g, carry):
        d = g["d"]
        M, FT, AR, VZ, p = g["M"], g["FT"], d["AR"], d["VZ"], d["p"]
        for n in (2 * g["grp"], 2 * g["grp"] + 1):
            ns = slice(n * P, (n + 1) * P)
            j = 2 * (n % 2)
            bank, out = sq1.take(), sq2.take()
            S_, tS = carry.get("S"), carry.get("tS")
            al, rh = AR.v[:, n, 0, :], AR.v[:, n, 1, :]
            items = [(bank.v[:, 0:P], M.v[:, j + hh, 256:384], VZ.v[:, n, hh, :]) for hh in range(2)]
            if n:
                items.append((bank.v[:, 0:P], al, S_.v[:, :]))
            t = mm_group(c, bank, items, *g["tM"], *d["tz"], d["tar"], tS, *bank.busy)
            R, U = rz.take(), uz.take()
            t = c.ac.do(act(own_columns(R), bank.v[:, 0:P].rearrange("p (a b) -> p a b", a=2), ACT.Copy), t, zero, *R.busy)
            yield
            t = mm_group(c, bank, [(bank.v[:, P:2 * P], FT.v[:, j + hh, :], R.v[:, hh, :]) for hh in range(2)],
                         t, g["tT"])
            R.busy = [t]
            tU = c.ac.do(act(own_columns(U), bank.v[:, P:2 * P].rearrange("p (a b) -> p a b", a=2), ACT.Copy), t, zero, *U.busy)
            bank.busy = [tU]
            yield
            if n < NS - 1:
                t = mm_group(c, bank, [
                    (bank.v[:, 2 * P:3 * P], d["KA"].v[:, ns], VZ.v[:, n, hh, :]) for hh in range(2)] + [
                    (bank.v[:, 2 * P:3 * P], d["BE"].v[:, ns], U.v[:, hh, :]) for hh in range(2)], tU, d["tks"])
                nx = st.take()
                if n:
                    t = V(c, tt(nx.v[:, :], bank.v[:, 2 * P:3 * P], S_.v[:, :], ALU.add), t, tS, *nx.busy)
                    tS2 = V(c, stt(nx.v[:, :], nx.v[:, :], d["G"].v[:, n:n + 1], heads2[:, :], ALU.mult, ALU.mult),
                            t, d["tG"])
                else:
                    tS2 = V(c, stt(nx.v[:, :], bank.v[:, 2 * P:3 * P], d["G"].v[:, n:n + 1], heads2[:, :],
                                   ALU.mult, ALU.mult), t, d["tG"], *nx.busy)
                bank.busy = [tS2]
                carry["S"], carry["tS"] = nx, tS2
            yo = out.v[:, 0:P]
            items = [(yo, M.v[:, j + hh, 384:512], VZ.v[:, n, hh, :]) for hh in range(2)]
            items += [(yo, M.v[:, j + hh, P:2 * P], U.v[:, hh, :]) for hh in range(2)]
            if n:
                items.append((yo, rh, S_.v[:, :]))
            t = mm_group(c, out, items, tU, *out.busy)
            U.busy = [t]
            if n:
                S_.busy = [t, tS2] if n < NS - 1 else [t]
            ty = t
            M.busy, FT.busy = [ty], [ty]
            AR.busy = [ty]
            yield
            y = yb.take()
            y2 = y.v[:, :].rearrange("p (h e) -> p h e", h=2)
            t = V(c, cp(y.v[:, :], yo), ty, *y.busy)
            out.busy = [t]
            t = normed_heads(c, y2, y2, (stats, mv), LNX_EPS, t, carry.get("ty"))
            carry["ty"] = t
            ln, gt = d["ln"], gb.take()
            tg = gt.chan.dma(c.sp, gt.v[:, :], z[ns, 1024 + p * P:1024 + (p + 1) * P], ztok, *gt.busy)
            t = V(c, tt(y.v[:, :], y.v[:, :], ln.v[:, 0, :], ALU.mult), t, d["tln"])
            t = V(c, tt(y.v[:, :], y.v[:, :], ln.v[:, 1, :], ALU.add), t)
            ln.busy = [t]
            yield
            for hh in range(2):
                es = slice(64 * hh, 64 * hh + 64)
                t2 = V(c, stt(y.v[:, es], VZ.v[:, n, hh, es], d["bo"].v[:, 2 * n + hh:2 * n + hh + 1], y.v[:, es],
                              ALU.mult, ALU.add), t, d["tbo"])
            t = V(c, tt(y.v[:, :], y.v[:, :], gt.v[:, :], ALU.mult), t2, tg)
            gt.busy, d["bo"].busy = [t], [t]
            VZ.busy = [t, ty]
            t = transposes(c, out.v, [y.v[:, :]], t, *out.busy)
            y.busy = [t]
            th = c.ac.do(act(c.XH[:, p, ns], out.v[:, 0:P], ACT.Copy), t)
            tl = V(c, tt(c.XL[:, p, ns], out.v[:, 0:P], f32(c.XH[:, p, ns]), ALU.subtract), th, t)
            out.busy = [tl, th]
            c.xt[n] = [th, tl]
            yield
        d["KA"].busy, d["BE"].busy, d["G"].busy = [ty], [ty], [ty]

    data, prev, carry = {}, None, {}
    alternate(prepare(0, data))
    alternate(factors(data))
    for p in range(8):
        nxt = {}
        ahead = prepare(p + 1, nxt) if p < 7 else iter(())
        for grp in range(4):
            res = {}
            alternate(inverse(data, grp, res), chain(prev, carry) if prev else None, some(ahead, 5))
            prev = res
        for _ in ahead:
            pass
        data["ka"].busy = data["be"].busy = [data["last_use"]]
        alternate(chain(prev, carry), factors(nxt) if p < 7 else None)
        data, prev, carry = nxt, None, {}


def some(gen, n):
    for _, _ in zip(range(n), gen):
        yield


def own_columns(s):
    return s.v[:, :, :].rearrange("p a b -> p (a b)").rearrange("p (a b) -> p a b", a=2)[:, :, 0:64]


def forget_sums(c, w, b_f):
    ready = w.get(8)
    cc = {n: c.keep.enter_context(c.nc.sbuf_tensor(f"c_{n}", [P, S], R32, side="right"))
          for n in ("ph", "pl", "mh", "ml")}
    fl, a, one = c.sb("fl", [P, S]), c.sb("fa", [P, S]), c.sb("fb", [P, 1])
    mm = c.psum([0, 1])
    r = slice(96, 128)
    tb0 = V(c, lambda e: e.memset(one[r, :], 0.0))
    tb0 = c.chan().dma(c.sp, one[112:128, :], b_f.rearrange("(a n) -> a n", n=1), tb0)
    ts_ = []
    for sh in range(2):
        b = mm.take()
        t = feat_tile(c, b, 0, sh, ready)
        cs = slice(512 * sh, 512 * (sh + 1))
        ts_.append(c.ac.do(act(fl[r, cs], b.v[r, :], ACT.Identity, bias=one[r, :]), t, tb0))
    t = c.ac.do(act(a[r, :], fl[r, :], ACT.Abs), *ts_)
    t = c.ac.do(act(a[r, :], a[r, :], ACT.Exp, scale=-1.0), t)
    t = c.ac.do(act(a[r, :], a[r, :], ACT.Ln, bias=1.0), t)
    t = V(c, stt(a[r, :], fl[r, :], 0.0, a[r, :], ALU.min, ALU.subtract), t)
    t = V(c, lambda e: e.tensor_tensor_scan(fl[r, :], a[r, :], a[r, :], 0.0, ALU.add, ALU.bypass), t)
    tp = V(c, cp(cc["ph"][r, :], fl[r, :]), t)
    t1 = V(c, tt(cc["pl"][r, :], fl[r, :], f32(cc["ph"][r, :]), ALU.subtract), tp)
    t2 = V(c, ts(cc["mh"][r, :], f32(cc["ph"][r, :]), -1.0, None, ALU.mult), tp)
    t3 = V(c, ts(cc["ml"][r, :], f32(cc["pl"][r, :]), -1.0, None, ALU.mult), t1)
    return cc, [t1, t2, t3]


def fox(c, z, zt, ztok, cc, ctok):
    c.phase()
    neg, t0 = c.const("neg")
    negr = c.sb("negr", [P, P], R32)
    idr = c.sb("idr", [P, P], R32)
    t0 = [V(c, cp(negr[:, :], neg[:, :]), t0), V(c, cp(idr[:, :], c.ident[:, :]), c.tid)]
    raw = c.buf("raw", [P, S], 2)
    qh, ql, kh, kl = (c.buf(n, [P, S], 1, R32) for n in ("qh", "ql", "kh", "kl"))
    vh, vl = (c.buf(n, [P, S], 1, R32) for n in ("vh", "vl"))
    gg = c.buf("gg", [P, S], 1)
    cq, ck = c.buf("cq", [4, S], 2, R32), c.buf("ck", [4, S], 2, R32)
    onef = c.sb("onef", [4, S])
    ws = c.buf("w", [P, S], 2)
    wh = c.buf("WH", [P, NS, 512], 1, R32)
    wl = c.buf("WL", [P, NS, 512], 1, R32)
    sts = c.buf("st", [P, 4], 4)
    mix = c.buf("mix", [P, 512], 2)
    sb_ = [Slot((c.banks[0], c.banks[1])), Slot((c.banks[2], c.banks[3]))]
    sring, tb, ob = Ring(sb_), c.psum([4, 5]), c.psum([6, 7])
    t1 = V(c, lambda e: e.memset(onef[:, :], 1.0))
    ones = [V(c, cp(s.v[:, :], onef[:, :]), t1) for s in cq.slots + ck.slots]

    def load(pair):
        r, got = slice(pair * P, (pair + 1) * P), []
        for (src, hi, lo, scale) in ((zt[r, :], qh, ql, 0.125), (zt[1024 + pair * P:1024 + (pair + 1) * P, :], kh, kl, 1.0),
                                     (None, vh, vl, 1.0)):
            b, h, l = raw.take(), hi.take(), lo.take()
            if src is None:
                t = b.chan.dma(c.sp, b.v[:, :].rearrange("p (a e) -> p a e", a=NS),
                               z[:, pair * P:(pair + 1) * P].rearrange("(a p) e -> p a e", p=P), ztok, *b.busy)
            else:
                t = b.chan.dma(c.sp, b.v[:, :], src, ztok, *b.busy)
            th = c.po.do(ts(h.v[:, :], b.v[:, :], scale, None, ALU.mult), t, *h.busy)
            tl = V(c, stt(l.v[:, :], b.v[:, :], scale, f32(h.v[:, :]), ALU.mult, ALU.subtract), th, *l.busy)
            b.busy = [tl]
            got.append((h, l, [th, tl]))
        b, g = raw.take(), gg.take()
        t = b.chan.dma(c.sp, b.v[:, :], zt[2048 + pair * P:2048 + (pair + 1) * P, :], *b.busy)
        t = c.ac.do(act(g.v[:, :], b.v[:, :], ACT.Sigmoid), t, *g.busy)
        t = c.po.do(tt(g.v[:, :], g.v[:, :], b.v[:, :], ALU.mult), t)
        b.busy = [t]
        return got + [(g, t)]

    for pair in range(8):
        (qH, qL, tq), (kH, kL, tk), (vH, vL, tv), (g, tg) = load(pair)
        for hh in range(2):
            head = 2 * pair + hh
            hr = slice(64 * hh, 64 * hh + 64)
            a, b = cq.take(), ck.take()
            row = slice(112 + head, 113 + head)
            toks = []
            for dst, rows in ((a, ((2, "ph"), (3, "pl"))), (b, ((0, "mh"), (1, "ml")))):
                for n, name in rows:
                    dst.busy = [dst.chan.dma(c.sp, f32(dst.v[n:n + 1, :]), f32(cc[name][row, :]), ctok, *ones, *dst.busy)]
                toks += dst.busy
            for half in range(2):
                WH, WL = wh.take(), wl.take()
                twt = []
                for qb in range(4 * half, 4 * half + 4):
                    sr, w, st = sring.take(), ws.take(), sts.take()
                    qs = slice(qb * P, (qb + 1) * P)
                    tot = (qb + 1) * P
                    for part in range(half + 1):
                        n = min(512, tot - 512 * part)
                        bank, kc = sr.v[part], slice(512 * part, 512 * part + n)
                        terms = [(qH, kH), (qL, kH), (qH, kL)]
                        first = [sr.busy, tq, tk, toks, t0] if part == 0 else []
                        for j, (x, y) in enumerate(terms):
                            c.pe.go(lambda e, bank=bank, x=x, y=y, n=n, kc=kc, j=j, qs=qs, hr=hr: e.matmul(
                                bank[:, 0:n], x.v[hr, qs], y.v[hr, kc], start=(j == 0), stop=False), *first)
                        if part == half:
                            c.pe.go(lambda e, bank=bank, n=n: e.matmul(
                                bank[:, n - P:n], idr[:, :], negr[:, :], start=False, stop=False,
                                skip_group_check=True))
                        ts_ = c.pe.do(lambda e, bank=bank, n=n, kc=kc, qs=qs, a=a, b=b: e.matmul(
                            bank[:, 0:n], a.v[:, qs], b.v[:, kc], start=False, stop=True))
                    parts = [(p_, min(512, tot - 512 * p_)) for p_ in range(half + 1)]
                    for p_, n in parts:
                        t = V(c, lambda e, p_=p_, n=n, sr=sr, st=st: e.tensor_reduce(
                            st.v[:, p_:p_ + 1], sr.v[p_][:, 0:n], AX, ALU.max), ts_, *st.busy)
                    if half:
                        t = V(c, tt(st.v[:, 0:1], st.v[:, 0:1], st.v[:, 1:2], ALU.max), t)
                    tm = V(c, ts(st.v[:, 2:3], st.v[:, 0:1], -1.0, None, ALU.mult), t)
                    te = []
                    for p_, n in parts:
                        te.append(c.ac.do(act(w.v[:, 512 * p_:512 * p_ + n], sr.v[p_][:, 0:n], ACT.Exp,
                                              bias=st.v[:, 2:3], accum_out=st.v[:, p_:p_ + 1]), tm, *w.busy))
                    sr.busy = [*te]
                    t = te[0]
                    if half:
                        t = V(c, tt(st.v[:, 0:1], st.v[:, 0:1], st.v[:, 1:2], ALU.add), *te)
                    t = V(c, lambda e, st=st: e.reciprocal(st.v[:, 3:4], st.v[:, 0:1]), t)
                    t = V(c, ts(w.v[:, 0:tot], w.v[:, 0:tot], st.v[:, 3:4], None, ALU.mult), t, *te)
                    st.busy = [t]
                    tn = t
                    for g4 in range(half + 1):
                        kbs = list(range(4 * g4, min(4 * g4 + 4, qb + 1)))
                        bt = tb.take()
                        tt_ = transposes(c, bt.v, [w.v[:, kb * P:(kb + 1) * P] for kb in kbs], tn, *bt.busy)
                        nb = len(kbs)
                        src = bt.v[:, 0:nb * P].rearrange("p (a b) -> p a b", a=nb)
                        qo = slice((qb - 4 * half) * P, (qb - 4 * half + 1) * P)
                        hi, lo = WH.v[:, 4 * g4:4 * g4 + nb, qo], WL.v[:, 4 * g4:4 * g4 + nb, qo]
                        th = c.ac.do(act(hi, src, ACT.Copy), tt_, *WH.busy)
                        tl = V(c, tt(lo, src, f32(hi), ALU.subtract), th, *WL.busy)
                        bt.busy = [th, tl]
                        twt = [th, tl]
                    w.busy = [tt_]
                o, mx = ob.take(), mix.take()
                kbs = list(range(4 * half + 3, -1, -1))
                for kb in kbs:
                    off = max(0, kb - 4 * half) * P
                    for j, (x, y) in enumerate(((vH, WH), (vL, WH), (vH, WL))):
                        fn = lambda e, o=o, x=x, y=y, kb=kb, off=off, j=j, kbs=kbs: e.matmul(
                            o.v[:, off:512], x.v[:, kb * P:(kb + 1) * P], y.v[:, kb, off:512],
                            start=(kb == kbs[0] and j == 0), stop=(kb == kbs[-1] and j == 2), skip_group_check=True)
                        if kb == kbs[-1] and j == 2:
                            to = c.pe.do(fn)
                        else:
                            c.pe.go(fn, twt, tv, *o.busy)
                WH.busy, WL.busy = [to], [to]
                qc = slice(512 * half, 512 * (half + 1))
                t = V(c, tt(mx.v[hr, :], o.v[hr, :], g.v[hr, qc], ALU.mult), to, tg, *mx.busy)
                o.busy = [t]
                th = c.ac.do(act(c.XH[hr, pair, qc], mx.v[hr, :], ACT.Copy), t)
                tl = V(c, tt(c.XL[hr, pair, qc], mx.v[hr, :], f32(c.XH[hr, pair, qc]), ALU.subtract), th, t)
                mx.busy = [tl, th]
                for s in range(4 * half, 4 * half + 4):
                    c.xt[s] = [th, tl]
            a.busy, b.busy = [ts_], [ts_]
        for x in (qH, qL, kH, kL):
            x.busy = [ts_]
        vH.busy, vL.busy, g.busy = [to], [to], [t]


def layer_fox(c, i):
    c.phase()
    c.keep = ExitStack()
    z, zt = c.scratch["z"], c.scratch["zt"]
    c.stage = c.buf("stage", [P, 512], 3)
    win = i["att_w_in_2"][0]
    w = Weights(c, [win[:, 512 * b:512 * (b + 1)] for b in range(8)] + [win[:, 3984:4112]], raw=3)
    modes = ["feat"] * 4 + ["seq"] * 2 + ["feat"] * 2
    dst = []
    for b in range(8):
        if 4 <= b < 6:
            dst.append(lambda j, at=512 * (b - 4): z[j * P:(j + 1) * P, at:at + 512])
        else:
            at = 512 * b if b < 4 else 2048 + 512 * (b - 6)
            dst.append(lambda j, at=at: zt[at + (j // 2) * P:at + (j // 2 + 1) * P, (j % 2) * 512:(j % 2 + 1) * 512])
    tok = project(c, None, modes, dst, w)
    cc, ct = forget_sums(c, w, i["att_b_f_2"][0])
    fox(c, z, zt, tok, cc, ct)
    c.drop = c.keep


def hgrn(c, z, zt, ztok, rec_lb, out_gain):
    c.phase()
    levels, t0 = c.const("levels")
    reset, t1 = c.const("reset")
    lv = levels[:, :].bitcast(I32).rearrange("p (l t) -> p l t", l=8)
    og = c.sb("og", [P, P])
    t2 = c.chan().dma(c.sp, og[:, :], out_gain.rearrange("(a n) -> a n", a=1).to_broadcast([P, P]))
    lb = c.sb("lb", [P, 4, 8])
    lr = c.sb("lr", [16, P])
    t = c.chan().dma(c.sp, lr[:, :], rec_lb.rearrange("l (h p) -> (l h) p", p=P))
    tb = c.psum([6, 7])
    b = tb.take()
    t = c.pe.do(lambda e: e.transpose(b.v[:, 0:16], lr[:, :], c.ident[0:16, 0:16]), t, c.tid)
    t = V(c, cp(lb[:, 0:2, :], b.v[:, 0:16].rearrange("p (l h) -> p l h", l=2)), t)
    b.busy = [t]
    t = V(c, tt(lb[:, 2, :], lb[:, 0, :], lb[:, 1, :], ALU.max), t)
    t = V(c, tt(lb[:, 0:2, :], lb[:, 0:2, :], lb[:, 2, :].unsqueeze(1).to_broadcast([P, 2, 8]), ALU.subtract), t)
    t = c.ac.do(act(lb[:, 0:2, :], lb[:, 0:2, :], ACT.Exp), t)
    t = V(c, tt(lb[:, 2, :], lb[:, 0, :], lb[:, 1, :], ALU.add), t)
    t = V(c, lambda e: e.reciprocal(lb[:, 2, :], lb[:, 2, :]), t)
    t = V(c, tt(lb[:, 0:2, :], lb[:, 0:2, :], lb[:, 2, :].unsqueeze(1).to_broadcast([P, 2, 8]), ALU.mult), t)
    tlb = t
    qs, fs, bs, ks = (c.buf(n, [P, S], 1) for n in ("q", "f", "b", "k"))
    vs, gs = c.buf("v", [P, S], 1), c.buf("g", [P, S], 1)
    ds, q2, k2 = c.buf("D", [P, S], 2), c.buf("q2", [P, S], 2), c.buf("k2", [P, S], 2)
    accs = c.buf("acc", [P, S], 1)
    kes = c.buf("ke", [P, S], 1)
    os_ = c.buf("o", [P, S], 1)
    sq = c.buf("sq", [P, S], 1)
    state = c.buf("state", [P, P], 2)
    ex, ss = c.sb("ex", [P, NS]), c.sb("ss", [P, NS])
    sring = Ring([Slot((c.banks[0], c.banks[1])), Slot((c.banks[2], c.banks[3]))])
    obs = c.psum([4, 5])
    tfin = None
    for h in range(8):
        q, f, bb, k, v, g, acc, ke, o, s_ = (r.take() for r in (qs, fs, bs, ks, vs, gs, accs, kes, os_, sq))
        rows = lambda n, h=h: zt[n + h * P:n + (h + 1) * P, :]
        cols = lambda n, h=h: z[:, n + h * P:n + (h + 1) * P].rearrange("(a p) e -> p a e", p=P)
        r3 = lambda t: t[:, :].rearrange("p (a e) -> p a e", a=NS)
        tq = q.chan.dma(c.sp, q.v[:, :], rows(0), ztok, *q.busy)
        tf = f.chan.dma(c.sp, f.v[:, :], rows(1024), *f.busy)
        tv = v.chan.dma(c.sp, r3(v.v), cols(0), *v.busy)
        tg = g.chan.dma(c.sp, r3(g.v), cols(1024), *g.busy)
        sg = s_
        tgs = c.ac.do(act(sg.v[:, :], g.v[:, :], ACT.Sigmoid), tg, *s_.busy)
        tgs = c.po.do(tt(g.v[:, :], sg.v[:, :], g.v[:, :], ALU.mult), tgs)
        t = c.ac.do(act(k.v[:, :], f.v[:, :], ACT.Sigmoid, scale=-1.0), tf, *k.busy)
        tk = c.po.do(ts(k.v[:, :], k.v[:, :], lb[:, 0, h:h + 1], None, ALU.mult), t, tlb)
        t = c.ac.do(act(f.v[:, :], f.v[:, :], ACT.Sigmoid), t)
        t = V(c, ts(f.v[:, :], f.v[:, :], lb[:, 0, h:h + 1], lb[:, 1, h:h + 1], ALU.mult, ALU.add), t, tlb)
        t = c.ac.do(act(f.v[:, :], f.v[:, :], ACT.Ln), t)
        tb_ = V(c, lambda e, bb=bb, f=f: e.tensor_tensor_scan(bb.v[:, :], reset[:, :], f.v[:, :], 0.0, ALU.mult, ALU.add),
                t, t1, *bb.busy)
        tacc = c.po.do(lambda e, acc=acc: e.memset(acc.v[:, :], 0.0), *acc.busy)
        for l in range(8):
            if l < 7:
                m = 64 >> l
                d, a, b2 = ds.take(), q2.take(), k2.take()
                bv = bb.v[:, :].rearrange("p (n a m) -> p n a m", a=2, m=m)
                dv = d.v[:, :].rearrange("p (n a m) -> p n a m", a=2, m=m)
                ref = bv[:, :, 0, m - 1:m].to_broadcast([P, S // (2 * m), m])
                V(c, tt(dv[:, :, 0, :], ref, bv[:, :, 0, :], ALU.subtract), tb_, *d.busy)
                t = V(c, tt(dv[:, :, 1, :], bv[:, :, 1, :], ref, ALU.subtract))
                t = c.ac.do(act(d.v[:, :], d.v[:, :], ACT.Exp), t)
                ta = V(c, tt(a.v[:, :], q.v[:, :], d.v[:, :], ALU.mult), t, tq, *a.busy)
                tk2 = c.po.do(tt(b2.v[:, :], k.v[:, :], d.v[:, :], ALU.mult), t, tk, *b2.busy)
                d.busy = [ta, tk2]
            else:
                a, b2, ta, tk2 = q, k, tq, tk
            sr = sring.take()
            tm = part_matmuls(c, [(sr.v[n // 4][:, (n % 4) * P:(n % 4 + 1) * P], b2.v[:, n * P:(n + 1) * P],
                                   a.v[:, n * P:(n + 1) * P]) for n in range(NS)], ta, tk2, *sr.busy)
            if l < 7:
                a.busy, b2.busy = [tm], [tm]
            for half in range(2):
                dst = acc.v[:, 512 * half:512 * (half + 1)].rearrange("p (a t) -> p a t", a=4)
                src = sr.v[half][:, :].rearrange("p (a t) -> p a t", a=4)
                mask = lv[:, l, :].unsqueeze(1).to_broadcast([P, 4, P])
                t = V(c, lambda e, dst=dst, mask=mask, src=src: e.copy_predicated(dst, mask, src), tm, tacc, t0)
            sr.busy = [t]
            tacc = t
        d, a, b2 = ds.take(), q2.take(), k2.take()
        t = c.ac.do(act(d.v[:, :], bb.v[:, :], ACT.Exp), tb_, *d.busy)
        ta = V(c, tt(a.v[:, :], q.v[:, :], d.v[:, :], ALU.mult), t, tq, *a.busy)
        te = V(c, cp(ex[:, :], r3(d.v)[:, :, P - 1]), t, tfin)
        d.busy = [ta, te]
        d = ds.take()
        t = V(c, tt(r3(d.v), r3(bb.v)[:, :, P - 1:P].to_broadcast([P, NS, P]), r3(bb.v), ALU.subtract), *d.busy)
        bb.busy, f.busy = [t], [tb_]
        t = c.ac.do(act(d.v[:, :], d.v[:, :], ACT.Exp), t)
        tk2 = c.po.do(tt(b2.v[:, :], k.v[:, :], d.v[:, :], ALU.mult), t, tk, *b2.busy)
        d.busy = [tk2]
        k.busy, q.busy = [tk2, tm], [ta, tm]
        tke = []
        for half in range(2):
            b = tb.take()
            t = transposes(c, b.v, [b2.v[:, (4 * half + j) * P:(4 * half + j + 1) * P] for j in range(4)], tk2, *b.busy)
            b.busy = [c.ac.do(act(ke.v[:, 512 * half:512 * (half + 1)], b.v[:, :], ACT.Copy), t, *ke.busy)]
            tke += b.busy
        b2.busy = [t]
        st, tst = None, None
        for n in range(NS):
            ns = slice(n * P, (n + 1) * P)
            ob = obs.take()
            oc, kc = slice(0, P), slice(P, 2 * P)
            items = [(ob.v[:, oc], acc.v[:, ns], v.v[:, ns])]
            if n:
                items.append((ob.v[:, oc], a.v[:, ns], st.v[:, :]))
            to = mm_group(c, ob, items, tacc, tv, ta, tst, *ob.busy)
            tkv = mm_group(c, ob, [(ob.v[:, kc], ke.v[:, ns], v.v[:, ns])], *tke)
            nx = state.take()
            if n:
                t = V(c, stt(nx.v[:, :], st.v[:, :], ex[:, n:n + 1], ob.v[:, kc], ALU.mult, ALU.add), tkv, te, tst, *nx.busy)
                st.busy = [t, to]
            else:
                t = V(c, cp(nx.v[:, :], ob.v[:, kc]), tkv, *nx.busy)
            st, tst = nx, t
            t2_ = c.ac.do(act(o.v[:, ns], ob.v[:, oc], ACT.Copy), to, tst, *o.busy)
            ob.busy = [t2_, tst]
        st.busy = [tst]
        a.busy, ke.busy, v.busy, acc.busy = [to], [tkv], [tkv], [to]
        tfin = tst
        t = V(c, tt(sg.v[:, :], o.v[:, :], o.v[:, :], ALU.mult), t2_, tgs)
        t = V(c, lambda e, sg=sg: e.tensor_reduce(ss[:, :], r3(sg.v), AX, ALU.add), t)
        t = V(c, ts(ss[:, :], ss[:, :], 1.0 / P, RMS_EPS, ALU.mult, ALU.add), t)
        t = rsqrt(c, ss[:, :], t)
        t = V(c, tt(r3(o.v), r3(o.v), last_axis(ss[:, :], [P, NS, P]), ALU.mult), t)
        t = V(c, tt(r3(o.v), r3(o.v), mid_axis(og[:, :], [P, NS, P]), ALU.mult), t, t2)
        t = V(c, tt(o.v[:, :], o.v[:, :], g.v[:, :], ALU.mult), t, tgs)
        s_.busy, g.busy = [t], [t]
        for half in range(2):
            b = tb.take()
            tt_ = transposes(c, b.v, [o.v[:, (4 * half + j) * P:(4 * half + j + 1) * P] for j in range(4)], t, *b.busy)
            hs = slice(512 * half, 512 * (half + 1))
            th = c.ac.do(act(c.XH[:, h, hs], b.v[:, :], ACT.Copy), tt_)
            tl = V(c, tt(c.XL[:, h, hs], b.v[:, :], f32(c.XH[:, h, hs]), ALU.subtract), th, tt_)
            b.busy = [th, tl]
            for s in range(4 * half, 4 * half + 4):
                c.xt[s] = [th, tl]
        o.busy = [tt_]


def layer_hgrn(c, i):
    c.phase()
    z, zt = c.scratch["z"], c.scratch["zt"]
    c.stage = c.buf("stage", [P, 512], 4)
    win = i["rec_w_in_2"][0]
    modes = ["feat"] * 4 + ["seq"] * 4
    dst = []
    for b in range(8):
        if b >= 4:
            dst.append(lambda j, at=512 * (b - 4): z[j * P:(j + 1) * P, at:at + 512])
        else:
            dst.append(lambda j, at=512 * b: zt[at + (j // 2) * P:at + (j // 2 + 1) * P, (j % 2) * 512:(j % 2 + 1) * 512])
    tok = project(c, [win[:, 512 * b:512 * (b + 1)] for b in range(8)], modes, dst)
    hgrn(c, z, zt, tok, i["rec_lb_2"], i["rec_out_norm_2"][0])


def program(nc, i, consts, out, where, layers=(0, 1, 2, 3)):
    scratch = {
        "h": nc.dram_tensor("sc_h", [S, D], F32, kind="Internal").ap(),
        "z": nc.dram_tensor("sc_z", [S, 4096], F32, kind="Internal").ap(),
        "zt": nc.dram_tensor("sc_zt", [4096, S], F32, kind="Internal").ap(),
    }
    with ExitStack() as ctx:
        c = Ctx(nc, ctx, consts, where, scratch)
        pre = {0: i["norm_gain"][0], 1: i["norm_gain"][1], 2: i["norm_pre_2"][0], 3: i["norm_pre_2"][1]}
        start(c, i["x"][0], pre[layers[0]])
        for n, l in enumerate(layers):
            nxt = layers[n + 1] if n + 1 < len(layers) else None
            kw = {"next_gain": None if nxt is None else pre[nxt], "out": out if nxt is None else None}
            if l == 0:
                layer_even(c, i)
                layer_end(c, i["even_w_out"][0], i["p"][0, 0], i["ple_proj"][0], i["ple_gate"][0], **kw)
            elif l == 1:
                layer_odd(c, i)
                layer_end(c, i["odd_w_out"][0], i["p"][1, 0], i["ple_proj"][1], i["ple_gate"][1],
                          mid_gain=i["final_gain"], **kw)
            elif l == 2:
                layer_fox(c, i)
                layer_end(c, i["att_w_out_2"][0], i["p_2"][0, 0], i["ple_w_proj_2"][0], i["ple_w_gate_2"][0],
                          post_gain=i["norm_post_2"][0], **kw)
            else:
                layer_hgrn(c, i)
                layer_end(c, i["rec_w_out_2"][0], i["p_2"][1, 0], i["ple_w_proj_2"][1], i["ple_w_gate_2"][1],
                          post_gain=i["norm_post_2"][1], **kw)
        c.phase()
        c.stack.close()
        block = ctx.enter_context(nc.Block())
        block.sync(lambda e: c.sp.run(e))
        block.tensor(lambda e: c.pe.run(e))
        block.vector(lambda e: c.ve.run(e))
        block.scalar(lambda e: c.ac.run(e))
        block.gpsimd(lambda e: c.po.run(e))


_INS = ["x", "p", "norm_gain", "final_gain", "ple_proj", "ple_gate", "even_w_in", "even_w_out", "ret_gn_gain",
        "odd_mu", "odd_w_in", "odd_w_out", "rwkv_w0", "rwkv_w1", "rwkv_w2", "rwkv_a0", "rwkv_a1", "rwkv_a2",
        "rwkv_k_k", "rwkv_k_a", "rwkv_r_k", "rwkv_lnx_gain", "rwkv_lnx_bias", "p_2", "norm_pre_2", "norm_post_2",
        "att_w_in_2", "att_b_f_2", "att_w_out_2", "rec_w_in_2", "rec_lb_2", "rec_out_norm_2", "rec_w_out_2",
        "ple_w_proj_2", "ple_w_gate_2"]


def kernel(**inputs):
    import concourse.bacc as _bacc
    from concourse.bass_utils import run_bass_kernel_spmd as _run

    nc = _bacc.Bacc("TRN2", target_bir_lowering=False, num_devices=1)
    arrays, args = {}, {}
    for name in _INS:
        a = np.ascontiguousarray(inputs[name])
        arrays[f"in_{name}"] = a
        args[name] = nc.dram_tensor(f"in_{name}", a.shape, mybir.dt.from_np(a.dtype), kind="ExternalInput").ap()
    table, where = shape_constants()
    arrays["consts"] = table
    consts = nc.dram_tensor("consts", table.shape, F32, kind="ExternalInput").ap()
    out = nc.dram_tensor("out_0", (1, S, D), F32, kind="ExternalOutput").ap()
    program(nc, args, consts, out[0], where)
    r = _run(nc, [arrays], core_ids=[0])
    return r.results[0]["out_0"]
```

```python
from contextlib import ExitStack

import numpy as np

import concourse.bass as bass
from concourse import mybir

P = 128
S = 1024
D = 1024
NS = S // P
NK = D // P
F32 = mybir.dt.float32
R32 = mybir.dt.float32r
I32 = mybir.dt.int32
ALU = mybir.AluOpType
ACT = mybir.ActivationFunctionType
AX = mybir.AxisListType.X
RMS_EPS = 1e-6
GN_EPS = 1e-5
LNX_EPS = 64e-5
RSQRT_CAP = 1e12
NEG = -1.0e30
SQRT_E_INV = float(np.exp(-0.5))


def shape_constants():
    half = 64
    inv = np.float32(10000.0) ** (-np.arange(half, dtype=np.float32) / np.float32(half))
    ang = (np.arange(S, dtype=np.float32)[:, None] * inv[None, :]).astype(np.float32).astype(np.float64)
    cos = np.cos(ang).reshape(NS, P, half).transpose(1, 0, 2)
    sin = np.sin(ang).reshape(NS, P, half).transpose(1, 0, 2)
    lg = np.log(1.0 - 2.0 ** (-5.0 - np.arange(4, dtype=np.float64)))
    c = np.arange(P, dtype=np.float64)
    scale = 128.0 ** -0.5
    diff = c[None, :] - c[:, None]
    intra = np.where(diff[:, None, :] >= 0, np.exp(np.maximum(diff, 0.0)[:, None, :] * lg[None, :, None]), 0.0) * scale
    kdec = np.exp((P - 1 - c)[:, None] * lg[None, :]) * scale
    qdec = np.exp((c + 1)[:, None] * lg[None, :])
    after = (c[None, :] > c[:, None]).astype(np.float64)
    upto = (c[None, :] >= c[:, None]).astype(np.float64)
    levels = []
    for m in (64, 32, 16, 8, 4, 2, 1):
        blk = np.floor(c / (2 * m))
        first = np.floor(c / m) % 2 == 0
        levels.append(((blk[:, None] == blk[None, :]) & first[:, None] & ~first[None, :]).astype(np.float64))
    levels.append(np.eye(P))
    heads2 = (np.floor(c / 64)[:, None] == np.floor(c / 64)[None, :]).astype(np.float64)
    reset = np.ones((P, S))
    reset[:, ::P] = 0.0
    f = lambda a: np.ascontiguousarray(np.asarray(a, np.float32).reshape(P, -1))
    parts = {
        "ident": f(np.eye(P)), "cos": f(cos), "sin": f(sin), "intra": f(intra), "kdec": f(kdec), "qdec": f(qdec),
        "after": f(after), "upto": f(upto), "before": f(after.T),
        "ntri": f(-upto.T), "nones": f(-np.ones((P, P))), "neg": f(np.where(after > 0, NEG, 0.0)),
        "levels": f(np.stack(levels, 1)), "heads2": f(heads2), "cols2": f(heads2[:, ::64]), "reset": f(reset),
    }
    where, at = {}, 0
    for name, a in parts.items():
        where[name] = (at, a.shape[1])
        at += a.shape[1]
    return np.concatenate(list(parts.values()), 1), where


class Line:

    def __init__(self, sem):
        self.todo, self.sem, self.n, self.seen = [], sem, 0, {}

    @property
    def last(self):
        return (self.sem, self.n)

    def wait(self, *tokens):
        for t in tokens:
            if t is None:
                continue
            if isinstance(t, list):
                self.wait(*t)
                continue
            sem, value = t
            if value > self.seen.get(id(sem), 0):
                self.seen[id(sem)] = value
                self.todo.append(lambda e, sem=sem, value=value: e.wait_ge(sem, value))

    def do(self, fn, *tokens):
        self.wait(*tokens)
        self.n += 1
        self.todo.append(lambda e: fn(e).then_inc(self.sem, 1))
        return (self.sem, self.n)

    def go(self, fn, *tokens):
        self.wait(*tokens)
        self.todo.append(fn)

    def run(self, e):
        for fn in self.todo:
            fn(e)


class Chan:

    def __init__(self, sem):
        self.sem, self.n = sem, 0

    @property
    def last(self):
        return (self.sem, 16 * self.n)

    def dma(self, line, out, in_, *tokens):
        line.wait(*tokens)
        self.n += 1
        line.todo.append(lambda e: e.dma_start(out, in_).then_inc(self.sem, 16))
        return (self.sem, 16 * self.n)


class Slot:

    def __init__(self, v, chan=None):
        self.v, self.chan, self.busy = v, chan, []


class Ring:
    def __init__(self, slots):
        self.slots, self.i = slots, 0

    def take(self):
        s = self.slots[self.i % len(self.slots)]
        self.i += 1
        return s


class Ctx:
    def __init__(self, nc, ctx, consts, where, scratch):
        self.nc, self.ctx, self.consts, self.where, self.scratch = nc, ctx, consts, where, scratch
        sem = lambda n: ctx.enter_context(nc.semaphore(n))
        self.pe, self.ve, self.ac, self.po, self.sp = (Line(sem(n)) for n in ("s_pe", "s_ve", "s_ac", "s_po", "s_sp"))
        self.lines = [self.pe, self.ve, self.ac, self.po, self.sp]
        self.chans = [Chan(sem(f"d{i}")) for i in range(80)]
        self.nch = 0
        self.banks = [ctx.enter_context(nc.psum_tensor(f"bank{i}", [P, 512], F32)) for i in range(8)]
        self.bank_slots = [Slot(b) for b in self.banks]
        self.XH = ctx.enter_context(nc.sbuf_tensor("XH", [P, NK, S], R32))
        self.XL = ctx.enter_context(nc.sbuf_tensor("XL", [P, NK, S], R32))
        self.ident = ctx.enter_context(nc.sbuf_tensor("ident", [P, P], F32))
        self.xt = [[] for _ in range(NS)]
        self.xk = [[] for _ in range(NK)]
        self.nph, self.drop = 0, None
        self.tid = self.chan().dma(self.sp, self.ident[:, :], self.const_in("ident"))

    def const_in(self, name):
        a, n = self.where[name]
        return self.consts[:, a:a + n]

    def chan(self):
        c = self.chans[self.nch]
        self.nch += 1
        return c

    def phase(self):
        if self.nph:
            self.stack.close()
            if self.drop is not None:
                self.drop.close()
                self.drop = None
            marks = [l.last for l in self.lines] + [c.last for c in self.chans if c.n]
            for l in self.lines:
                l.wait([m for m in marks if m[1] and m[0] is not l.sem or l in (self.ve, self.ac, self.po, self.pe) and m[1]])
        self.nph += 1
        self.nch = 1
        self.stack = ExitStack()

    def sb(self, name, shape, dt=F32):
        return self.stack.enter_context(self.nc.sbuf_tensor(f"{name}_{self.nph}", shape, dt))

    def psum(self, ids):
        return Ring([self.bank_slots[i] for i in ids])

    def const(self, name, shape=None):
        n = self.where[name][1]
        t = self.sb(name, [P, n])
        tok = self.chan().dma(self.sp, t[:, :], self.const_in(name))
        return t, tok

    def buf(self, name, shape, n, dt=F32):
        return Ring([Slot(self.sb(f"{name}{i}", shape, dt), self.chan()) for i in range(n)])


def f32(ap):
    return ap.bitcast(F32)


class Weights:

    def __init__(self, c, srcs, raw=4, ahead=1, pad=False):
        self.c, self.srcs, self.ahead = c, srcs, ahead
        self.raw = c.buf("wraw", [P, 2, 512], raw)
        self.slots = Ring([Slot((c.sb(f"wh{i}", [P, NK, 512], R32), c.sb(f"wl{i}", [P, NK, 512], R32)))
                           for i in range(2)])
        self.got = []

    def prepare(self, upto):
        c = self.c
        while len(self.got) < min(upto, len(self.srcs)):
            src = self.srcs[len(self.got)]
            n = src.shape[1]
            slot = self.slots.take()
            h, l = slot.v
            toks = []
            for j in range(NK // 2):
                r = self.raw.take()
                t = r.chan.dma(c.sp, r.v[:, :, 0:n], src[256 * j:256 * (j + 1), :].rearrange("(a p) n -> p a n", p=P),
                               *r.busy)
                hj, lj, rj = h[:, 2 * j:2 * j + 2, 0:n], l[:, 2 * j:2 * j + 2, 0:n], r.v[:, :, 0:n]
                th = c.po.do(lambda e, hj=hj, rj=rj: e.tensor_copy(hj, rj), t, *slot.busy)
                tl = c.ve.do(lambda e, hj=hj, lj=lj, rj=rj: e.tensor_tensor(lj, rj, f32(hj), ALU.subtract),
                             th, t, *slot.busy)
                r.busy = [tl]
                toks.append([th, tl])
            slot.busy = []
            self.got.append((slot, toks))

    def get(self, i, more=None):
        self.prepare(i + 1 + (self.ahead if more is None else more))
        return self.got[i]


def mm_group(c, bank, terms, *tokens):
    for i, (out, lhsT, rhs) in enumerate(terms):
        fn = lambda e, out=out, lhsT=lhsT, rhs=rhs, i=i: e.matmul(
            out, lhsT, rhs, start=(i == 0), stop=(i == len(terms) - 1))
        if i < len(terms) - 1:
            c.pe.go(fn, *(tokens if i == 0 else ()))
        else:
            return c.pe.do(fn, *(tokens if i == 0 else ()))


def big_product(c, bank, out, xs, w, wtoks, xtoks, x_is_lhs):
    last = None
    for k in range(NK):
        (xh, xl), (wh, wl) = xs(k), w(k)
        for j, (a, b) in enumerate(((xh, wh), (xl, wh), (xh, wl))):
            lhsT, rhs = (a, b) if x_is_lhs else (b, a)
            first, stop = k == 0 and j == 0, k == NK - 1 and j == 2
            fn = lambda e, lhsT=lhsT, rhs=rhs, first=first, stop=stop: e.matmul(
                out, lhsT, rhs, start=first, stop=stop)
            tokens = ([bank.busy, xtoks] if first else []) + ([wtoks[k // 2], c.xk[k]] if j == 0 else [])
            if stop:
                last = c.pe.do(fn, *tokens)
            else:
                c.pe.go(fn, *tokens)
    bank.busy = [last]
    return last


def seq_tile(c, bank, s, w, n=512, off=0):
    slot, toks = w
    h, l = slot.v
    t = big_product(c, bank, bank.v[:, off:off + n],
                    lambda k: (c.XH[:, k, s * P:(s + 1) * P], c.XL[:, k, s * P:(s + 1) * P]),
                    lambda k: (h[:, k, 0:n], l[:, k, 0:n]), toks, c.xt[s], True)
    slot.busy = [t]
    return t


def feat_tile(c, bank, f, sh, w):
    slot, toks = w
    h, l = slot.v
    t = big_product(c, bank, bank.v[:, :],
                    lambda k: (c.XH[:, k, sh * 512:(sh + 1) * 512], c.XL[:, k, sh * 512:(sh + 1) * 512]),
                    lambda k: (h[:, k, f * P:(f + 1) * P], l[:, k, f * P:(f + 1) * P]), toks,
                    [t for s in range(4 * sh, 4 * sh + 4) for t in c.xt[s]], False)
    slot.busy = [t]
    return t


def to_xt(c, rows, s, tbanks, *tokens):
    out = []
    for half in range(2):
        b = tbanks.take()
        for j in range(4):
            k = 4 * half + j
            fn = lambda e, b=b, j=j, k=k: e.transpose(b.v[:, j * P:(j + 1) * P], rows[:, k * P:(k + 1) * P],
                                                      c.ident[:, :])
            if j < 3:
                c.pe.go(fn, *tokens, c.tid, *b.busy)
            else:
                tt = c.pe.do(fn, *tokens)
        out += split_out(c, b, lambda t, half=half: t[:, 4 * half:4 * half + 4, s * P:(s + 1) * P], tt)
    c.xt[s] = out
    return tt


def split_out(c, bank, part, *tokens):
    src = bank.v[:, :].rearrange("p (a b) -> p a b", a=4)
    th = c.ac.do(lambda e: e.activation(part(c.XH), src, ACT.Copy), *tokens)
    tl = c.ve.do(lambda e: e.tensor_tensor(part(c.XL), src, f32(part(c.XH)), ALU.subtract), th, *tokens)
    bank.busy = [th, tl]
    return [th, tl]


def rsqrt(c, ap, *tokens):
    t = c.ac.do(lambda e: e.activation(ap, ap, ACT.Sqrt), *tokens)
    return c.ve.do(lambda e: e.reciprocal(ap, ap), t)


def rms_scale(c, sq, st, srcs, width, eps, *tokens):
    toks = []
    for i, a in enumerate(srcs):
        toks.append(c.ac.do(lambda e, a=a, i=i: e.activation(sq[:, 0:a.shape[1]], a, ACT.Square,
                                                             accum_out=st[:, i:i + 1]), *tokens, c.ac.last))
    if len(srcs) == 2:
        t = c.ve.do(lambda e: e.tensor_tensor(st[:, 0:1], st[:, 0:1], st[:, 1:2], ALU.add), *toks)
    else:
        t = toks[0]
    t = c.ve.do(lambda e: e.tensor_scalar(st[:, 2:3], st[:, 0:1], 1.0 / width, eps, ALU.mult, ALU.add), t)
    return rsqrt(c, st[:, 2:3], t), toks


def row_gain(c, name, src):
    t = c.sb(name, [P, D])
    return t, c.chan().dma(c.sp, t[:, :], src.rearrange("(a n) -> a n", a=1).to_broadcast([P, D]))


def start(c, x, gain):
    c.phase()
    g, tg = row_gain(c, "g", gain)
    rows, tmp = c.buf("h", [P, D], 2), c.buf("tmp", [P, D], 2)
    sq = c.sb("sq", [P, D])
    sts = c.buf("st", [P, 4], 2)
    tb = c.psum(range(4))
    for s in range(NS):
        r, m, st = rows.take(), tmp.take(), sts.take()
        t = r.chan.dma(c.sp, r.v[:, :], x[s * P:(s + 1) * P, :], *r.busy)
        tr, _ = rms_scale(c, sq, st.v, [r.v[:, :]], D, RMS_EPS, t, *st.busy)
        tm = c.ve.do(lambda e, r=r, m=m, st=st: e.scalar_tensor_tensor(
            out=m.v[:, :], in0=r.v[:, :], scalar=st.v[:, 2:3], in1=g[:, :], op0=ALU.mult, op1=ALU.mult),
            tr, tg, *m.busy)
        r.busy, st.busy = [tm], [tm]
        m.busy = [to_xt(c, m.v, s, tb, tm)]
    c.h = x
    c.h_tok = [None] * NS


def project(c, srcs, modes, dst, w=None, first=0, silu=()):
    w = w or Weights(c, srcs)
    mm = c.psum(range(8))
    stage = c.stage
    toks = []
    for i, mode in enumerate(modes):
        ready = w.get(first + i)
        for j in range(8):
            b, st = mm.take(), stage.take()
            if mode == "seq":
                t = seq_tile(c, b, j, ready)
            else:
                t = feat_tile(c, b, j // 2, j % 2, ready)
            f = ACT.Sigmoid if i in silu else ACT.Copy
            t = c.ac.do(lambda e, b=b, st=st, f=f: e.activation(st.v[:, :], b.v[:, :], f), t, *st.busy)
            if i in silu:
                t = c.ve.do(lambda e, b=b, st=st: e.tensor_tensor(st.v[:, :], b.v[:, :], st.v[:, :], ALU.mult), t)
            b.busy = [t]
            out = dst[i](j)
            st.busy = [st.chan.dma(c.sp, out, st.v[:, :], t)]
            toks += st.busy
    return toks


def layer_end(c, w_out, p, ple_w, gate_w, next_gain, post_gain=None, mid_gain=None, out=None):
    c.phase()
    w = Weights(c, [w_out[:, 0:512], w_out[:, 512:1024], gate_w[:, 0:512], gate_w[:, 512:1024]], raw=2)
    H = c.sb("H", [P, NS, D])
    pT = c.sb("pT", [P, 2, S])
    pw = c.sb("pw", [P, 2, D])
    tmp = c.buf("tmp", [P, D], 1)
    sg = c.buf("sg", [P, 512], 2)
    sts = c.buf("st", [P, 4], 2)
    tb = c.psum([6, 7])
    mm = c.psum(range(6))
    gains = []
    chans = [c.chan() for _ in range(NS)]
    th = [chans[s].dma(c.sp, H[:, s, :], c.h[s * P:(s + 1) * P, :], c.h_tok[s]) for s in range(NS)]
    if post_gain is not None:
        pg, tpg = row_gain(c, "pg", post_gain)
    w.get(0, more=1)
    tpw = c.chan().dma(c.sp, pw[:, :, :], ple_w.rearrange("(a p) n -> p a n", p=P))
    pt = tmp.take()
    tpt = []
    for q in range(2):
        t = pt.chan.dma(c.sp, pt.v[:, :].rearrange("p (a n) -> p a n", a=4),
                        p[512 * q:512 * (q + 1), :].rearrange("(a p) n -> p a n", p=P), *pt.busy)
        for k in range(2):
            b = tb.take()
            for a in range(4):
                fn = lambda e, b=b, a=a, k=k: e.transpose(b.v[:, a * P:(a + 1) * P],
                                                          pt.v[:, a * 256 + k * P:a * 256 + (k + 1) * P], c.ident[:, :])
                if a < 3:
                    c.pe.go(fn, t, c.tid, *b.busy)
                else:
                    tt = c.pe.do(fn)
            b.busy = [c.ac.do(lambda e, b=b, q=q, k=k: e.activation(pT[:, k, 512 * q:512 * (q + 1)], b.v[:, :], ACT.Copy), tt)]
            tpt += b.busy
            pt.busy = [tt]
    ready = [None] * NS
    w0, w1 = w.got[0], w.got[1]
    for s in range(NS + 1):
        if s < NS:
            bs = [mm.take(), mm.take()]
            ts = [seq_tile(c, bs[0], s, w0), seq_tile(c, bs[1], s, w1)]
            if post_gain is None:
                for half in range(2):
                    hs = H[:, s, 512 * half:512 * (half + 1)]
                    ts[half] = c.ve.do(lambda e, hs=hs, b=bs[half]: e.tensor_tensor(hs, b.v[:, :], hs, ALU.add),
                                       ts[half], th[s])
                    bs[half].busy = [ts[half]]
            else:
                st = sts.take()
                sq = sg.take()
                tr, tq = rms_scale(c, sq.v, st.v, [bs[0].v[:, :], bs[1].v[:, :]], D, RMS_EPS, *ts, *st.busy, *sq.busy)
                sq.busy = tq
                m = tmp.take()
                for half in range(2):
                    cs = slice(512 * half, 512 * (half + 1))
                    t = c.ve.do(lambda e, b=bs[half], st=st, cs=cs, m=m: e.scalar_tensor_tensor(
                        out=m.v[:, cs], in0=b.v[:, :], scalar=st.v[:, 2:3], in1=pg[:, cs], op0=ALU.mult, op1=ALU.mult),
                        tr, tpg, *m.busy)
                    bs[half].busy = [t, *tq]
                    ts[half] = c.ve.do(lambda e, s=s, cs=cs, m=m: e.tensor_tensor(H[:, s, cs], m.v[:, cs], H[:, s, cs], ALU.add),
                                       t, th[s])
                st.busy, m.busy = [t], [ts[1]]
            ready[s] = ts
        if s > 0:
            to_xt(c, H[:, s - 1, :], s - 1, tb, *ready[s - 1])
    w.get(2, more=1)
    w0, w1 = w.got[2], w.got[3]
    ng, tng = (pw, tpw) if next_gain is None else row_gain(c, "ng", next_gain)
    if mid_gain is not None:
        mg, tmg = row_gain(c, "mg", mid_gain)
    toks = [None] * NS
    pending = None
    for s in range(NS + 1):
        if s < NS:
            for half, wt in ((0, w0), (1, w1)):
                cs = slice(512 * half, 512 * (half + 1))
                gb, pb, g = mm.take(), mm.take(), sg.take()
                tg = seq_tile(c, gb, s, wt)
                tp = mm_group(c, pb, [(pb.v[:, :], pT[:, k, s * P:(s + 1) * P], pw[:, k, cs]) for k in range(2)],
                              *tpt, tpw, *pb.busy)
                tg = c.ac.do(lambda e, g=g, gb=gb: e.activation(g.v[:, :], gb.v[:, :], ACT.Sigmoid), tg, *g.busy)
                gb.busy = [tg]
                tp = c.ve.do(lambda e, g=g, pb=pb: e.tensor_tensor(g.v[:, :], pb.v[:, :], g.v[:, :], ALU.mult), tp, tg)
                pb.busy = [tp]
                t = c.ve.do(lambda e, g=g, s=s, cs=cs: e.tensor_tensor(H[:, s, cs], H[:, s, cs], g.v[:, :], ALU.add), tp)
                g.busy = [t]
            hs = H[:, s, :]
            if mid_gain is not None:
                st, m = sts.take(), tmp.take()
                tr, tq = rms_scale(c, m.v, st.v, [hs], D, RMS_EPS, t, *st.busy, *m.busy)
                m.busy = tq
                t = c.ve.do(lambda e, hs=hs, st=st: e.scalar_tensor_tensor(
                    out=hs, in0=hs, scalar=st.v[:, 2:3], in1=mg[:, :], op0=ALU.mult, op1=ALU.mult), tr, tmg, *tq)
                st.busy = [t]
            toks[s] = chans[s].dma(c.sp, (c.scratch["h"] if out is None else out)[s * P:(s + 1) * P, :], hs, t)
        if s > 0 and next_gain is not None:
            st, m = sts.take(), tmp.take()
            tr, tq = rms_scale(c, m.v, st.v, [H[:, s - 1, :]], D, RMS_EPS, pending, *st.busy, *m.busy)
            tm = c.ve.do(lambda e, s=s, m=m, st=st: e.scalar_tensor_tensor(
                out=m.v[:, :], in0=H[:, s - 1, :], scalar=st.v[:, 2:3], in1=ng[:, :], op0=ALU.mult, op1=ALU.mult),
                tr, tng, *tq)
            st.busy = [tm]
            m.busy = [to_xt(c, m.v, s - 1, tb, tm)]
        pending = t
    c.h, c.h_tok = c.scratch["h"], toks


def V(c, fn, *tokens):
    return c.ve.do(fn, *tokens)


def tt(out, a, b, op):
    return lambda e: e.tensor_tensor(out, a, b, op)


def stt(out, a, s, b, op0, op1):
    return lambda e: e.scalar_tensor_tensor(out=out, in0=a, scalar=s, in1=b, op0=op0, op1=op1)


def act(out, a, f, **kw):
    return lambda e: e.activation(out, a, f, **kw)


def ts(out, a, s1, s2, op0, op1=None):
    if op1 is None:
        return lambda e: e.tensor_scalar(out, a, s1, s2, op0)
    return lambda e: e.tensor_scalar(out, a, s1, s2, op0, op1)


def cp(out, a):
    return lambda e: e.tensor_copy(out, a)


def last_axis(ap, shape):
    return ap.unsqueeze(len(ap.shape)).to_broadcast(shape)


def mid_axis(ap, shape):
    return ap.unsqueeze(1).to_broadcast(shape)


def transposes(c, bank, srcs, *tokens):
    for i, a in enumerate(srcs):
        fn = lambda e, i=i, a=a: e.transpose(bank[:, i * P:(i + 1) * P], a, c.ident[:, :])
        if i < len(srcs) - 1:
            c.pe.go(fn, *tokens, c.tid)
        else:
            return c.pe.do(fn, *tokens, c.tid)


def part_matmuls(c, items, *tokens):
    for i, (out, lhsT, rhs) in enumerate(items):
        fn = lambda e, out=out, lhsT=lhsT, rhs=rhs: e.matmul(out, lhsT, rhs, start=True, stop=True)
        if i < len(items) - 1:
            c.pe.go(fn, *tokens)
        else:
            return c.pe.do(fn, *tokens)


def normed_heads(c, o, y, st, eps, *tokens):
    nh = o.shape[1]
    stats, mv = st
    for h in range(nh):
        t = V(c, lambda e, h=h: e.bn_stats(stats[:, h, :], o[:, h, :]), *tokens)
    for h in range(nh):
        t2 = V(c, lambda e, h=h: e.bn_aggr(mv[:, h, :], stats[:, h, :]), t)
    t = V(c, ts(mv[:, :, 1], mv[:, :, 1], eps, None, ALU.add), t2)
    t = rsqrt(c, mv[:, :, 1], t)
    for h in range(nh):
        t2 = V(c, ts(y[:, h, :], o[:, h, :], mv[:, h, 0:1], mv[:, h, 1:2], ALU.subtract, ALU.mult), t)
    return t2


def retention(c, z, ztok, gn_gain):
    c.phase()
    cos, t0 = c.const("cos")
    sin, t1 = c.const("sin")
    intra, t2 = c.const("intra")
    kdec, t3 = c.const("kdec")
    qdec, t4 = c.const("qdec")
    gn = c.sb("gn", [P, 512])
    t5 = c.chan().dma(c.sp, gn[:, :], gn_gain.rearrange("(a n) -> a n", a=1).to_broadcast([P, 512]))
    tk = [t0, t1, t2, t3, t4, t5]
    cos = cos[:, :].rearrange("p (n j) -> p n j", j=64)
    sin = sin[:, :].rearrange("p (n j) -> p n j", j=64)
    intra = intra[:, :]
    zs = c.buf("z", [P, 2048], 3)
    three = lambda n, shape: c.buf(n, shape, 3)
    As, Bs, kds, qkTs, scs, os_, ys, sgs = (three(n, s) for n, s in (
        ("A", [P, 1024]), ("B", [P, 1024]), ("kd", [P, 512]), ("qkT", [P, 1024]), ("sc", [P, 512]),
        ("o", [P, 512]), ("y", [P, 512]), ("sg", [P, 512])))
    stats, mv = c.sb("stats", [P, 4, 6]), c.sb("mv", [P, 4, 2])
    state = c.sb("state", [P, 4, P])
    lg = np.log(1.0 - 2.0 ** (-5.0 - np.arange(4, dtype=np.float64)))
    cd = [float(np.exp(P * x)) for x in lg]
    tb, sb_, ob, ib, kb, xb = (c.psum(x) for x in ([0, 1], [2], [3], [4], [5], [6, 7]))
    carry = {}

    def chunk(n):
        zr, A, B, kd, qkT, sc, o, y, sg = (r.take() for r in (zs, As, Bs, kds, qkTs, scs, os_, ys, sgs))
        tz = zr.chan.dma(c.sp, zr.v[:, :], z[n * P:(n + 1) * P, 0:2048], ztok, *zr.busy)
        qk = zr.v[:, 0:1024].rearrange("p (h a j) -> p h a j", h=8, a=2)
        Av = A.v[:, :].rearrange("p (h a j) -> p h a j", h=8, a=2)
        Bv = B.v[:, :].rearrange("p (h a j) -> p h a j", h=8, a=2)
        b8 = lambda t: t[:, n, :].unsqueeze(1).to_broadcast([P, 8, 64])
        ta = V(c, tt(Av[:, :, 0, :], qk[:, :, 0, :], b8(cos), ALU.mult), tz, *tk, *A.busy)
        ta = V(c, tt(Av[:, :, 1, :], qk[:, :, 1, :], b8(cos), ALU.mult))
        tb1 = c.po.do(tt(Bv[:, :, 0, :], qk[:, :, 1, :], b8(sin), ALU.mult), tz, *tk, *B.busy)
        tb2 = c.po.do(tt(Bv[:, :, 1, :], qk[:, :, 0, :], b8(sin), ALU.mult))
        ta = V(c, tt(Av[:, :, 0, :], Av[:, :, 0, :], Bv[:, :, 0, :], ALU.subtract), ta, tb2)
        ta = V(c, tt(Av[:, :, 1, :], Av[:, :, 1, :], Bv[:, :, 1, :], ALU.add), ta, tb2)
        B.busy = [ta]
        v = zr.v[:, 1024:1536].rearrange("p (h e) -> p h e", h=4)
        kdv = kd.v[:, :].rearrange("p (h e) -> p h e", h=4)
        tkd = V(c, tt(kdv, A.v[:, 512:1024].rearrange("p (h e) -> p h e", h=4),
                      last_axis(kdec[:, :], [P, 4, P]), ALU.mult), ta, *kd.busy)
        tq = []
        for j in range(2):
            b = tb.take()
            t = transposes(c, b.v, [A.v[:, 512 * j + P * h:512 * j + P * (h + 1)] for h in range(4)], ta, *b.busy)
            b.busy = [c.ac.do(act(qkT.v[:, 512 * j:512 * (j + 1)], b.v[:, :], ACT.Copy), t, *qkT.busy)]
            tq += b.busy
        A.busy = [t, tkd]
        yield
        tstate = carry.get("state")
        q = lambda h: qkT.v[:, h * P:(h + 1) * P]
        k = lambda h: qkT.v[:, 512 + h * P:512 + (h + 1) * P]
        b = sb_.take()
        t = part_matmuls(c, [(b.v[:, h * P:(h + 1) * P], k(h), q(h)) for h in range(4)], *tq, *b.busy)
        tsc = V(c, tt(sc.v[:, :], b.v[:, :], intra, ALU.mult), t, *sc.busy)
        b.busy = [tsc]
        bi = ib.take()
        ti = None
        if n:
            ti = part_matmuls(c, [(bi.v[:, h * P:(h + 1) * P], q(h), state[:, h, :]) for h in range(4)],
                              *tq, tstate, *bi.busy)
        bk = kb.take()
        tkv = part_matmuls(c, [(bk.v[:, h * P:(h + 1) * P], kdv[:, h, :], v[:, h, :]) for h in range(4)],
                           tkd, tz, *bk.busy)
        bo = ob.take()
        to = part_matmuls(c, [(bo.v[:, h * P:(h + 1) * P], sc.v[:, h * P:(h + 1) * P], v[:, h, :])
                              for h in range(4)], tsc, *bo.busy)
        qkT.busy, sc.busy, kd.busy = [to], [to], [to]
        for h in range(4):
            hs = slice(h * P, (h + 1) * P)
            if n:
                t = V(c, stt(state[:, h, :], state[:, h, :], cd[h], bk.v[:, hs], ALU.mult, ALU.add), tkv, ti, tstate)
            else:
                t = V(c, cp(state[:, h, :], bk.v[:, hs]), tkv)
        carry["state"] = t
        bk.busy = [t]
        if n:
            t = V(c, tt(o.v[:, :].rearrange("p (h e) -> p h e", h=4), bi.v[:, :].rearrange("p (h e) -> p h e", h=4),
                        last_axis(qdec[:, :], [P, 4, P]), ALU.mult), ti, *o.busy)
            bi.busy = [t]
            t = V(c, tt(o.v[:, :], o.v[:, :], bo.v[:, :], ALU.add), to, t)
        else:
            t = V(c, cp(o.v[:, :], bo.v[:, :]), to, *o.busy)
        bo.busy = [t]
        yield
        ty = normed_heads(c, o.v[:, :].rearrange("p (h e) -> p h e", h=4), y.v[:, :].rearrange("p (h e) -> p h e", h=4),
                          (stats, mv), GN_EPS, t, carry.get("ty"), *y.busy)
        carry["ty"] = ty
        o.busy = [ty]
        t = c.po.do(tt(sg.v[:, :], zr.v[:, 1536:2048], gn[:, :], ALU.mult), tz, *tk, *sg.busy)
        zr.busy = [t, to, tkv, ta, tb2]
        t = V(c, tt(y.v[:, :], y.v[:, :], sg.v[:, :], ALU.mult), t, ty)
        sg.busy = [t]
        yield
        b = xb.take()
        t = transposes(c, b.v, [y.v[:, h * P:(h + 1) * P] for h in range(4)], t, *b.busy)
        y.busy = [t]
        c.xt[n] = split_out(c, b, lambda X, n=n: X[:, 0:4, n * P:(n + 1) * P], t)

    staggered([chunk(n) for n in range(NS)], 1, 4)


def stick(c, z, zt, ztok):
    c.phase()
    ntri, t0 = c.const("ntri")
    nones, t1 = c.const("nones")
    after, t2 = c.const("after")
    tk = [t0, t1, t2]
    scale = 128.0 ** -0.5
    qs, ks, gs, vs = (c.buf(n, [P, S], 4) for n in ("q", "k", "g", "v"))
    a_, l_, sp_, w_ = (c.buf(n, [P, 512], 4) for n in ("a", "l", "sp", "w"))
    R = c.buf("R", [P, 512], 4)
    zb, ob = c.psum([0, 1, 2, 3]), c.psum([4, 5, 6, 7])
    heads = []
    for h in range(4):
        q, k, g, v = (r.take() for r in (qs, ks, gs, vs))
        tq = q.chan.dma(c.sp, q.v[:, :], zt[h * P:(h + 1) * P, :], ztok)
        tkk = k.chan.dma(c.sp, k.v[:, :], zt[512 + h * P:512 + (h + 1) * P, :])
        tv = v.chan.dma(c.sp, v.v[:, :].rearrange("p (a e) -> p a e", a=NS),
                        z[:, 2048 + h * P:2048 + (h + 1) * P].rearrange("(a p) e -> p a e", p=P))
        heads.append((q, k, g, v, tq, tkk, tv))
    for h, (q, k, g, v, tq, tkk, tv) in enumerate(heads):
        tg = g.chan.dma(c.sp, g.v[:, :], zt[1024 + h * P:1024 + (h + 1) * P, :])
        tq = V(c, ts(q.v[:, :], q.v[:, :], scale, None, ALU.mult), tq)
        heads[h] = (q, k, g, v, tq, tkk, tv, tg)

    def chain(h, half):
        q, k, g, v, tq, tkk, tv, tg = heads[h]
        o, r = ob.take(), R.take()
        tr = c.po.do(lambda e: e.memset(r.v[:, :], 0.0), *r.busy)
        top = 4 * half + 3
        late = None
        for kb in range(top, -1, -1):
            off = max(0, kb - 4 * half) * P
            cs, n = slice(off, 512), 512 - off
            qc = slice(512 * half + off, 512 * (half + 1))
            b, a, l, sp, w = (x.take() for x in (zb, a_, l_, sp_, w_))
            kv = k.v[:, kb * P:(kb + 1) * P]
            tz = c.pe.do(lambda e, b=b, n=n, qc=qc, kv=kv: e.matmul(b.v[:, 0:n], kv, q.v[:, qc], start=True, stop=True),
                         tq, tkk, *b.busy)
            if late:
                to = weighted(o, *late)
            t = c.ac.do(act(a.v[:, 0:n], b.v[:, 0:n], ACT.Abs), tz, *a.busy)
            t = c.ac.do(act(a.v[:, 0:n], a.v[:, 0:n], ACT.Exp, scale=-1.0), t)
            yield
            t = c.ac.do(act(l.v[:, 0:n], a.v[:, 0:n], ACT.Ln, bias=1.0), t, *l.busy)
            a.busy = [t]
            t = V(c, stt(sp.v[:, 0:n], b.v[:, 0:n], 0.0, l.v[:, 0:n], ALU.max, ALU.add), t, *sp.busy)
            l.busy = [t]
            if kb >= 4 * half:
                t = V(c, tt(sp.v[:, 0:P], sp.v[:, 0:P], after[:, :], ALU.mult), t, *tk)
            yield
            c.pe.go(lambda e, b=b, sp=sp, n=n: e.matmul(b.v[:, 0:n], ntri[:, :], sp.v[:, 0:n], start=False,
                                                        stop=False, skip_group_check=True), t, *tk)
            tz = c.pe.do(lambda e, b=b, n=n, cs=cs: e.matmul(
                b.v[:, 0:n], nones[:, :], r.v[:, cs], start=False, stop=True, skip_group_check=True), tr)
            if kb:
                tr = c.po.do(tt(r.v[:, cs], r.v[:, cs], sp.v[:, 0:n], ALU.add), t, tz, tr)
            sp.busy = [tz, tr]
            t = c.ac.do(act(w.v[:, 0:n], b.v[:, 0:n], ACT.Exp), tz, *w.busy)
            b.busy = [t]
            if kb >= 4 * half:
                t = V(c, tt(w.v[:, 0:P], w.v[:, 0:P], after[:, :], ALU.mult), t, *tk)
            late = (cs, v.v[:, kb * P:(kb + 1) * P], w, n, kb == top, kb == 0, [t, tv])
            yield
        to = weighted(o, *late)
        r.busy = [to]
        qc = slice(512 * half, 512 * (half + 1))
        t = V(c, tt(g.v[:, qc], o.v[:, :], g.v[:, qc], ALU.mult), to, tg)
        o.busy = [t]
        th = c.ac.do(act(c.XH[:, 4 + h, qc], g.v[:, qc], ACT.Copy), t)
        tl = V(c, tt(c.XL[:, 4 + h, qc], g.v[:, qc], f32(c.XH[:, 4 + h, qc]), ALU.subtract), th, t)
        for s in range(4 * half, 4 * half + 4):
            c.xt[s] = c.xt[s] + [th, tl]

    def weighted(o, cs, vv, w, n, first, last, toks):
        to = c.pe.do(lambda e: e.matmul(o.v[:, cs], vv, w.v[:, 0:n], start=first, stop=last, skip_group_check=True),
                     toks, *o.busy)
        w.busy = [to]
        return to

    alternate(*[chain(h, 1) for h in range(4)])
    alternate(*[chain(h, 0) for h in range(4)])


def layer_even(c, i, xt_stage=True):
    c.phase()
    z, zt = c.scratch["z"], c.scratch["zt"]
    c.stage = c.buf("stage", [P, 512], 4)
    win = i["even_w_in"][0]
    order = [(0, "seq", 0), (1, "seq", 512), (2, "seq", 1024), (3, "seq", 1536), (4, "feat", 0), (5, "feat", 512),
             (6, "seq", 2048), (7, "feat", 1024)]
    dst = []
    for blk, mode, at in order:
        if mode == "seq":
            dst.append(lambda j, at=at: z[j * P:(j + 1) * P, at:at + 512])
        else:
            dst.append(lambda j, at=at: zt[at + (j // 2) * P:at + (j // 2 + 1) * P, (j % 2) * 512:(j % 2 + 1) * 512])
    tok = project(c, [win[:, 512 * b:512 * (b + 1)] for b, _, _ in order], [m for _, m, _ in order], dst, silu=(3, 7))
    retention(c, z, tok, i["ret_gn_gain"][0])
    stick(c, z, zt, tok)


VECS = {"mu": 0, "w0": 48, "a0": 56, "k_k": 64, "k_a": 72, "r_k": 80}


def per_feature(c, i, bank):
    rows, vt = c.sb("vrows", [88, P]), c.sb("vt", [P, 88])
    blk = lambda a: a.rearrange("(k q) -> k q", q=P)
    srcs = [i["odd_mu"][0].rearrange("p (k q) -> (p k) q", q=P), blk(i["rwkv_w0"][0]), blk(i["rwkv_a0"][0]),
            blk(i["rwkv_k_k"][0]), blk(i["rwkv_k_a"][0]), i["rwkv_r_k"][0].rearrange("(k a) q -> k (a q)", a=2)]
    at, toks = 0, []
    for a in srcs:
        n = a.shape[0]
        toks.append(c.chan().dma(c.sp, rows[at:at + n, :], a))
        at += n
    t = c.pe.do(lambda e: e.transpose(bank.v[:, 0:88], rows[:, :], c.ident[0:88, 0:88]), c.tid, *toks, *bank.busy)
    t = V(c, cp(vt[:, :], bank.v[:, 0:88]), t)
    bank.busy = [t]
    return vt, t


def shifted(c, n, HN, vt, omu, us, xs, tokens, last):
    for k in range(NK):
        u, x = us.take(), xs.take()
        t = c.ac.do(act(u.v[:, :], HN[:, k, 1:S + 1], ACT.Copy, scale=omu[:, 8 * n + k:8 * n + k + 1]), *tokens, *u.busy)
        t = V(c, stt(x.v[:, :], HN[:, k, 0:S], vt[:, 8 * n + k:8 * n + k + 1], u.v[:, :], ALU.mult, ALU.add), t, *x.busy)
        u.busy = [t]
        th = c.ac.do(act(c.XH[:, k, :], x.v[:, :], ACT.Copy), t, last)
        tl = V(c, tt(c.XL[:, k, :], x.v[:, :], f32(c.XH[:, k, :]), ALU.subtract), th, last)
        x.busy = [tl]
        c.xk[k] = [th, tl]


def layer_odd(c, i):
    c.phase()
    c.keep = ExitStack()
    z, zt = c.scratch["z"], c.scratch["zt"]
    c.stage = c.buf("stage", [P, 512], 4)
    win = i["odd_w_in"][0]
    tabs = [win[n][:, 512 * j:512 * (j + 1)] for n in range(4) for j in range(2)]
    w = Weights(c, tabs + [i["rwkv_w1"][0], i["rwkv_a1"][0]], raw=3)
    HN = c.sb("HN", [P, NK, S + 1])
    us, xs = c.buf("u", [P, S], 1), c.buf("x", [P, S], 2)
    lo = [c.keep.enter_context(c.nc.sbuf_tensor(f"lora{n}", [64, S], F32, side="right")) for n in range(2)]
    vt, tvt = per_feature(c, i, c.bank_slots[0])
    omu = c.sb("omu", [P, 48])
    to = V(c, ts(omu[:, :], vt[:, 0:48], -1.0, 1.0, ALU.mult, ALU.add), tvt)
    t0 = c.po.do(lambda e: e.memset(HN[:, :, 0:1], 0.0))
    hn = [V(c, tt(HN[:, k, 1:S + 1], f32(c.XH[:, k, :]), f32(c.XL[:, k, :]), ALU.add), *[c.xt[s] for s in range(NS)])
          for k in range(NK)]
    c.xt = [[] for _ in range(NS)]
    tokens = [t0, to, tvt, *hn]
    last, toks = None, []
    for n in range(4):
        shifted(c, n, HN, vt, omu, us, xs, tokens, last)
        dst = []
        for j in range(2):
            at = 1024 * n + 512 * j
            if n < 2:
                dst.append(lambda q, at=at: zt[at + (q // 2) * P:at + (q // 2 + 1) * P,
                                               (q % 2) * 512:(q % 2 + 1) * 512])
            else:
                dst.append(lambda q, at=at - 2048: z[q * P:(q + 1) * P, at:at + 512])
        toks += project(c, None, ["feat" if n < 2 else "seq"] * 2, dst, w, first=2 * n, silu=(0, 1) if n == 3 else ())
        last = c.pe.last
    mm = c.psum(range(8))
    for n in range(2):
        shifted(c, 4 + n, HN, vt, omu, us, xs, tokens, last)
        ready = w.get(8 + n)
        for sh in range(2):
            b = mm.take()
            t = feat_tile(c, b, 0, sh, ready)
            b.busy = [c.ac.do(act(lo[n][:, 512 * sh:512 * (sh + 1)], b.v[0:64, :], ACT.Copy if n else ACT.Tanh), t)]
        last = c.pe.last
    c.xk = [[] for _ in range(NK)]
    rwkv(c, i, z, zt, toks, lo)
    c.drop = c.keep


def alternate(*gens):
    gens = [g for g in gens if g is not None]
    while gens:
        for g in list(gens):
            try:
                next(g)
            except StopIteration:
                gens.remove(g)


def staggered(gens, apart, most=2):
    live, age = [], 0
    gens = list(gens)
    while gens or live:
        if gens and (not live or len(live) < most and age >= apart):
            live.append(gens.pop(0))
            age = 0
        for g in list(live):
            try:
                next(g)
            except StopIteration:
                live.remove(g)
        age += 1


def rwkv(c, i, z, zt, ztok, lo):
    c.phase()
    after, t0 = c.const("after")
    upto, t1 = c.const("upto")
    levels, t3 = c.const("levels")
    heads2, t4 = c.const("heads2")
    cols2, t5 = c.const("cols2")
    tk = [t0, t1, t3, t4, t5]
    vt, tvt = per_feature(c, i, c.bank_slots[0])
    vec = lambda n, p: vt[:, VECS[n] + p:VECS[n] + p + 1]
    mask4 = c.sb("mask4", [P, 4, P])
    tm4 = [V(c, ts(mask4[:, 0, :], after[:, :], -1.0, None, ALU.mult), *tk),
           V(c, ts(mask4[:, 1, :], upto[:, :], -1.0, None, ALU.mult)),
           V(c, cp(mask4[:, 2, :], after[:, :])), V(c, cp(mask4[:, 3, :], upto[:, :]))]
    eye = c.ident
    wab = c.buf("wab", [64, 2, P], 2)
    lnr = c.buf("ln", [P, 2, P], 2)
    one = lambda n, shape, k=1: c.buf(n, shape, k)
    rb, kb = one("r", [P, S]), one("k", [P, S])
    gb = one("g", [P, P], 3)
    vz = one("vz", [P, NS, 2, P], 2)
    ab, lb, bb, t1b, t2b = (one(n, [P, S]) for n in ("a", "lw", "b", "t1", "t2"))
    arb = one("ar", [P, NS, 2, P], 2)
    kap, bet = one("kap", [P, S]), one("bet", [P, S])
    kas, bes = one("kas", [P, S], 2), one("bes", [P, S], 2)
    gf = one("gf", [P, NS], 2)
    bon = one("bon", [P, 2 * NS], 2)
    mk, ttf = ([one(f"{n}{x}", [P, 2, w], 2) for x in range(2)] for n, w in (("mk", 512), ("ttf", P)))
    nm, T, TT, X = ([one(f"{n}{x}", [P, 2, P]) for x in range(2)] for n in ("nm", "T", "TT", "X"))
    rz, uz = one("rz", [P, 3, P], 1), one("uz", [P, 3, P], 1)
    st = one("S", [P, P], 2)
    yb = one("y", [P, P], 2)
    stats, mv = c.sb("stats", [P, 2, 6]), c.sb("mv", [P, 2, 2])
    zero = [c.po.do(lambda e, v=v: e.memset(v, 0.0)) for v in
            [s.v[:, :, :, :] for s in vz.slots] + [rz.slots[0].v[:, :, :], uz.slots[0].v[:, :, :]]]
    xb, yb2 = [c.psum([2]), c.psum([4])], [c.psum([3]), c.psum([5])]
    tb, sq1, sq2 = c.psum([0, 1]), c.psum([6]), c.psum([7])
    halves = [slice(0, 512), slice(512, 1024)]
    r3 = lambda t: t[:, :].rearrange("p (a e) -> p a e", a=NS)

    def prepare(p, res):
        r, k, VZ, wa, ln = (x.take() for x in (rb, kb, vz, wab, lnr))
        ps = slice(p * P, (p + 1) * P)
        tr = r.chan.dma(c.sp, r.v[:, :], zt[ps, :], ztok, *r.busy)
        tkk = k.chan.dma(c.sp, k.v[:, :], zt[1024 + p * P:1024 + (p + 1) * P, :], *k.busy)
        for n in range(2):
            tw = wa.chan.dma(c.sp, wa.v[:, n, :], i[("rwkv_w2", "rwkv_a2")[n]][0][:, ps], *wa.busy)
        for n in range(2):
            tln = ln.chan.dma(c.sp, ln.v[:, n, :], i[("rwkv_lnx_gain", "rwkv_lnx_bias")[n]][0][ps]
                              .rearrange("(a n) -> a n", a=1).to_broadcast([P, P]), *ln.busy)
        for hh in range(2):
            at = p * P + 64 * hh
            tv = VZ.chan.dma(c.sp, VZ.v[:, :, hh, 64 * hh:64 * hh + 64],
                             z[:, at:at + 64].rearrange("(a p) e -> p a e", p=P), zero, *VZ.busy)
        yield
        a, l, b, s1, s2 = (x.take() for x in (ab, lb, bb, t1b, t2b))
        ta, tl = [], []
        for dst, n, name, out in ((a, 1, "a0", ta), (l, 0, "w0", tl)):
            for hf in halves:
                bk = tb.take()
                t = mm_group(c, bk, [(bk.v[:, :], wa.v[:, n, :], lo[n][:, hf])], tw, *bk.busy)
                out.append(c.ac.do(act(dst.v[:, hf], bk.v[:, :], ACT.Sigmoid, bias=vec(name, p)), t, tvt, *dst.busy))
                bk.busy = [out[-1]]
            yield
        wa.busy = [t]
        t = V(c, ts(l.v[:, :], l.v[:, :], -SQRT_E_INV, None, ALU.mult), *tl)
        for n in range(NS):
            ns = slice(n * P, (n + 1) * P)
            tb_ = V(c, lambda e, ns=ns: e.tensor_tensor_scan(b.v[:, ns], l.v[:, ns], l.v[:, ns], 0.0, ALU.add,
                                                             ALU.bypass), t, *b.busy)
            if n == 3:
                yield
        yield
        kk = s1
        t = V(c, ts(kk.v[:, :], k.v[:, :], vec("k_k", p), None, ALU.mult), tkk, tvt, *s1.busy)
        tkn = t
        t = V(c, tt(s2.v[:, :], kk.v[:, :], kk.v[:, :], ALU.mult), t, *s2.busy)
        tn = []
        for hf in halves:
            bk = tb.take()
            t_ = mm_group(c, bk, [(bk.v[:, :], heads2[:, :], s2.v[:, hf])], t, *tk, *bk.busy)
            bk.busy = [c.ac.do(act(s2.v[:, hf], bk.v[:, :], ACT.Sqrt), t_)]
            tn += bk.busy
        yield
        t = V(c, ts(s2.v[:, :], s2.v[:, :], 1e-12, None, ALU.max), *tn)
        t = V(c, lambda e: e.reciprocal(s2.v[:, :], s2.v[:, :]), t)
        yield
        tkn = V(c, tt(kk.v[:, :], kk.v[:, :], s2.v[:, :], ALU.mult), t, tkn)
        t = V(c, ts(s2.v[:, :], a.v[:, :], 1.0, vec("k_a", p), ALU.subtract, ALU.mult), tkn, *ta)
        yield
        tkk = V(c, stt(k.v[:, :], s2.v[:, :], 1.0, k.v[:, :], ALU.add, ALU.mult), t, tkk)
        ta2 = c.po.do(tt(a.v[:, :], a.v[:, :], kk.v[:, :], ALU.mult), t, tkn)
        yield
        bo, bk = bon.take(), tb.take()
        t = V(c, stt(s2.v[:, :], r.v[:, :], vec("r_k", p), k.v[:, :], ALU.mult, ALU.mult), tr, tkk)
        t = part_matmuls(c, [(bk.v[:, 2 * n:2 * n + 2], s2.v[:, n * P:(n + 1) * P], cols2[:, :]) for n in range(NS)],
                         t, *tk, *bk.busy)
        tbo = V(c, cp(bo.v[:, :], bk.v[:, 0:2 * NS]), t, *bo.busy)
        bk.busy = [tbo]
        G = gf.take()
        mid = r3(b.v)[:, :, 63:64]
        t = V(c, tt(G.v[:, 0:7], r3(b.v)[:, 0:7, P - 1], r3(b.v)[:, 0:7, 63], ALU.subtract), tb_, *G.busy)
        t = V(c, tt(G.v[:, 0:7], G.v[:, 0:7], r3(b.v)[:, 1:8, 63], ALU.add), t)
        tG = c.ac.do(act(G.v[:, 0:7], G.v[:, 0:7], ACT.Exp), t)
        yield
        tD = V(c, tt(r3(s2.v), r3(b.v), mid.to_broadcast([P, NS, P]), ALU.subtract), tbo, tb_)
        t3_ = V(c, tt(l.v[:, :], s2.v[:, :], l.v[:, :], ALU.subtract), tD, tb_)
        tE3 = c.ac.do(act(l.v[:, :], l.v[:, :], ACT.Exp), t3_)
        tE1 = c.ac.do(act(b.v[:, :], s2.v[:, :], ACT.Exp), tD, t)
        tE2 = c.ac.do(act(s2.v[:, :], s2.v[:, :], ACT.Exp, scale=-1.0), t3_, tE1)
        res.update(r=r, k=k, a=a, l=l, b=b, s1=s1, s2=s2, VZ=VZ, G=G, bo=bo, ln=ln, p=p, tG=tG, tbo=tbo, tz=[tv],
                   tln=tln, tal=[tE3, tkn], trh=[tE1, tr], tka=[tE2, tkk], tbe=[tE2, ta2])
        yield

    def factors(d):
        r, k, a, l, b, kk, s2 = (d[n] for n in ("r", "k", "a", "l", "b", "s1", "s2"))
        AR, ka, be, KA, BE = (x.take() for x in (arb, kap, bet, kas, bes))
        tka = V(c, tt(ka.v[:, :], k.v[:, :], s2.v[:, :], ALU.mult), *d["tka"], *ka.busy)
        tbe = c.po.do(tt(be.v[:, :], a.v[:, :], s2.v[:, :], ALU.mult), *d["tbe"], *be.busy)
        tal = V(c, tt(AR.v[:, :, 0, :], r3(kk.v), r3(l.v), ALU.mult), *d["tal"], *AR.busy)
        yield
        trh = c.po.do(tt(AR.v[:, :, 1, :], r3(r.v), r3(b.v), ALU.mult), *d["trh"], *AR.busy)
        yield
        tks = []
        for src, dst, t, sc in ((ka, KA, tka, 1.0), (be, BE, tbe, -1.0)):
            for q in range(2):
                bk = tb.take()
                t_ = transposes(c, bk.v, [src.v[:, (4 * q + j) * P:(4 * q + j + 1) * P] for j in range(4)], t, *bk.busy)
                bk.busy = [c.ac.do(act(dst.v[:, 512 * q:512 * (q + 1)], bk.v[:, :], ACT.Copy, scale=sc), t_, *dst.busy)]
                tks += bk.busy
                yield
        for n, t in (("r", trh), ("k", tka), ("a", tbe), ("l", tal), ("b", trh), ("s1", tal)):
            d[n].busy = [t]
        d["s2"].busy = [tka, tbe]
        d.update(AR=AR, ka=ka, be=be, KA=KA, BE=BE, tar=[tal, trh], tkb=[tka, tbe], tks=tks)

    def inverse(d, n, res):
        x = n % 2
        M, FT = mk[x].take(), ttf[x].take()
        AR, ka, be = d["AR"], d["ka"], d["be"]
        ns = slice(n * P, (n + 1) * P)
        tM = []
        for hh in range(2):
            hr = slice(64 * hh, 64 * hh + 64)
            b = (xb, yb2)[hh][x].take()
            rhs = AR.v[hr, n, :, :].rearrange("p a t -> p (a t)")
            t = part_matmuls(c, [(b.v[:, 0:256], be.v[hr, ns], rhs), (b.v[:, 256:512], ka.v[hr, ns], rhs)],
                             *d["tar"], *d["tkb"], *b.busy)
            b.busy = [V(c, tt(M.v[:, hh, :], b.v[:, :], mask4[:, :, :].rearrange("p a t -> p (a t)"), ALU.mult), t,
                        *tm4, *M.busy)]
            tM += b.busy
            yield
        d["last_use"].append(t)
        b3 = lambda m: m.unsqueeze(1).to_broadcast([P, 2, P])
        lvl = lambda l: levels[:, l * P:(l + 1) * P]
        v2 = lambda b, at=0: b.v[:, at:at + 256].rearrange("p (u t) -> p u t", u=2)
        NT = M.v[:, :, 0:P]
        t_, tt_, x_, m_ = T[x].take(), TT[x].take(), X[x].take(), nm[x].take()
        tm = c.po.do(tt(m_.v[:, :, :], NT, b3(lvl(6)), ALU.mult), *tM, *m_.busy)
        tTT = c.po.do(tt(tt_.v[:, :, :], m_.v[:, :, :], b3(eye[:, :]), ALU.add), tm, *tt_.busy)
        yield
        lk = xb[x].take()
        tL = transposes(c, lk.v, [m_.v[:, u, :] for u in range(2)], tm, *lk.busy)
        tT = V(c, tt(t_.v[:, :, :], v2(lk), b3(eye[:, :]), ALU.add), tL, *t_.busy)
        lk.busy = [tT]
        tm = c.po.do(tt(m_.v[:, :, :], NT, b3(lvl(5)), ALU.mult), tTT, tL)
        yield
        for l in range(5, -1, -1):
            b, b2 = xb[x].take(), yb2[x].take()
            tX = part_matmuls(c, [(b.v[:, u * P:(u + 1) * P], m_.v[:, u, :], t_.v[:, u, :]) for u in range(2)],
                              tm, tT, *b.busy)
            tx = c.ac.do(act(x_.v[:, :, :], v2(b), ACT.Copy), tX, *x_.busy)
            b.busy = [tx]
            if l:
                tm = c.po.do(tt(m_.v[:, :, :], NT, b3(lvl(l - 1)), ALU.mult), tX)
            yield
            items = [(b2.v[:, u * P:(u + 1) * P], x_.v[:, u, :], tt_.v[:, u, :]) for u in range(2)]
            if l:
                items += [(b2.v[:, (2 + u) * P:(3 + u) * P], tt_.v[:, u, :], x_.v[:, u, :]) for u in range(2)]
            tb2 = part_matmuls(c, items, tx, tTT, *b2.busy)
            x_.busy = [tb2]
            if l:
                tT = V(c, tt(t_.v[:, :, :], t_.v[:, :, :], v2(b2, 256), ALU.add), tb2, tT)
                tTT = V(c, tt(tt_.v[:, :, :], tt_.v[:, :, :], v2(b2), ALU.add), tTT)
                b2.busy = [tTT]
            else:
                tTT = V(c, tt(FT.v[:, :, :], tt_.v[:, :, :], v2(b2), ALU.add), tb2, tTT, *FT.busy)
                b2.busy = [tTT]
                t_.busy, tt_.busy, m_.busy = [tX], [tTT, tb2], [tX]
            yield
        res.update(M=M, FT=FT, tM=tM, tT=tTT, d=d, n=n)

    def chain(g, carry):
        d, n = g["d"], g["n"]
        M, FT, AR, VZ, p = g["M"], g["FT"], d["AR"], d["VZ"], d["p"]
        ns = slice(n * P, (n + 1) * P)
        bank, out = sq1.take(), sq2.take()
        S_, tS = carry.get("S"), carry.get("tS")
        al, rh = AR.v[:, n, 0, :], AR.v[:, n, 1, :]
        items = [(bank.v[:, 0:P], M.v[:, hh, 256:384], VZ.v[:, n, hh, :]) for hh in range(2)]
        if n:
            items.append((bank.v[:, 0:P], al, S_.v[:, :]))
        t = mm_group(c, bank, items, *g["tM"], *d["tz"], d["tar"], tS, *bank.busy)
        R, U = rz.take(), uz.take()
        t = c.ac.do(act(own_columns(R), bank.v[:, 0:P].rearrange("p (a b) -> p a b", a=2), ACT.Copy), t, zero, *R.busy)
        yield
        t = mm_group(c, bank, [(bank.v[:, P:2 * P], FT.v[:, hh, :], R.v[:, hh, :]) for hh in range(2)],
                     t, g["tT"])
        R.busy = [t]
        tU = c.ac.do(act(own_columns(U), bank.v[:, P:2 * P].rearrange("p (a b) -> p a b", a=2), ACT.Copy), t, zero, *U.busy)
        bank.busy = [tU]
        yield
        if n < NS - 1:
            t = mm_group(c, bank, [
                (bank.v[:, 2 * P:3 * P], d["KA"].v[:, ns], VZ.v[:, n, hh, :]) for hh in range(2)] + [
                (bank.v[:, 2 * P:3 * P], d["BE"].v[:, ns], U.v[:, hh, :]) for hh in range(2)], tU, d["tks"])
            nx = st.take()
            if n:
                t = V(c, tt(nx.v[:, :], bank.v[:, 2 * P:3 * P], S_.v[:, :], ALU.add), t, tS, *nx.busy)
                tS2 = V(c, stt(nx.v[:, :], nx.v[:, :], d["G"].v[:, n:n + 1], heads2[:, :], ALU.mult, ALU.mult),
                        t, d["tG"])
            else:
                tS2 = V(c, stt(nx.v[:, :], bank.v[:, 2 * P:3 * P], d["G"].v[:, n:n + 1], heads2[:, :],
                               ALU.mult, ALU.mult), t, d["tG"], *nx.busy)
            bank.busy = [tS2]
            carry["S"], carry["tS"] = nx, tS2
        yo = out.v[:, 0:P]
        items = [(yo, M.v[:, hh, 384:512], VZ.v[:, n, hh, :]) for hh in range(2)]
        items += [(yo, M.v[:, hh, P:2 * P], U.v[:, hh, :]) for hh in range(2)]
        if n:
            items.append((yo, rh, S_.v[:, :]))
        t = mm_group(c, out, items, tU, *out.busy)
        U.busy = [t]
        if n:
            S_.busy = [t, tS2] if n < NS - 1 else [t]
        ty = t
        M.busy, FT.busy = [ty], [ty]
        AR.busy = [ty]
        yield
        y = yb.take()
        y2 = y.v[:, :].rearrange("p (h e) -> p h e", h=2)
        t = V(c, cp(y.v[:, :], yo), ty, *y.busy)
        out.busy = [t]
        t = normed_heads(c, y2, y2, (stats, mv), LNX_EPS, t, carry.get("ty"))
        carry["ty"] = t
        ln, gt = d["ln"], gb.take()
        tg = gt.chan.dma(c.sp, gt.v[:, :], z[ns, 1024 + p * P:1024 + (p + 1) * P], ztok, *gt.busy)
        t = V(c, tt(y.v[:, :], y.v[:, :], ln.v[:, 0, :], ALU.mult), t, d["tln"])
        t = V(c, tt(y.v[:, :], y.v[:, :], ln.v[:, 1, :], ALU.add), t)
        ln.busy = [t]
        yield
        for hh in range(2):
            es = slice(64 * hh, 64 * hh + 64)
            t2 = V(c, stt(y.v[:, es], VZ.v[:, n, hh, es], d["bo"].v[:, 2 * n + hh:2 * n + hh + 1], y.v[:, es],
                          ALU.mult, ALU.add), t, d["tbo"])
        t = V(c, tt(y.v[:, :], y.v[:, :], gt.v[:, :], ALU.mult), t2, tg)
        gt.busy, d["bo"].busy = [t], [t]
        VZ.busy = [t, ty]
        t = transposes(c, out.v, [y.v[:, :]], t, *out.busy)
        y.busy = [t]
        th = c.ac.do(act(c.XH[:, p, ns], out.v[:, 0:P], ACT.Copy), t)
        tl = V(c, tt(c.XL[:, p, ns], out.v[:, 0:P], f32(c.XH[:, p, ns]), ALU.subtract), th, t)
        out.busy = [tl, th]
        c.xt[n] = [th, tl]
        yield
        d["KA"].busy, d["BE"].busy, d["G"].busy = [ty], [ty], [ty]

    data = [{"last_use": []} for _ in range(8)]
    inverses = [[{} for _ in range(NS)] for _ in range(8)]
    done, carry = [0], {}

    def inverse_line(x):
        for p in range(8):
            while "AR" not in data[p]:
                yield
            if p == 0:
                for _ in range(4 * x):
                    yield
            for n in range(x, NS, 2):
                yield from inverse(data[p], n, inverses[p][n])

    def chain_line():
        for p in range(8):
            for n in range(NS):
                while not inverses[p][n]:
                    yield
                yield from chain(inverses[p][n], carry)
            done[0] += 1

    def factor_line():
        for p in range(8):
            while done[0] < p - 1:
                yield
            for _ in prepare(p, data[p]):
                yield
                yield
            if p:
                while len(data[p - 1]["last_use"]) < NS:
                    yield
                data[p - 1]["ka"].busy = data[p - 1]["be"].busy = data[p - 1]["last_use"]
            yield from factors(data[p])

    alternate(inverse_line(0), inverse_line(1), chain_line(), factor_line())


def own_columns(s):
    return s.v[:, :, :].rearrange("p a b -> p (a b)").rearrange("p (a b) -> p a b", a=2)[:, :, 0:64]


def forget_sums(c, w, b_f):
    ready = w.get(8)
    cc = {n: c.keep.enter_context(c.nc.sbuf_tensor(f"c_{n}", [P, S], R32, side="right"))
          for n in ("ph", "pl", "mh", "ml")}
    fl, a, one = c.sb("fl", [P, S]), c.sb("fa", [P, S]), c.sb("fb", [P, 1])
    mm = c.psum([0, 1])
    r = slice(96, 128)
    tb0 = V(c, lambda e: e.memset(one[r, :], 0.0))
    tb0 = c.chan().dma(c.sp, one[112:128, :], b_f.rearrange("(a n) -> a n", n=1), tb0)
    ts_ = []
    for sh in range(2):
        b = mm.take()
        t = feat_tile(c, b, 0, sh, ready)
        cs = slice(512 * sh, 512 * (sh + 1))
        ts_.append(c.ac.do(act(fl[r, cs], b.v[r, :], ACT.Identity, bias=one[r, :]), t, tb0))
    t = c.ac.do(act(a[r, :], fl[r, :], ACT.Abs), *ts_)
    t = c.ac.do(act(a[r, :], a[r, :], ACT.Exp, scale=-1.0), t)
    t = c.ac.do(act(a[r, :], a[r, :], ACT.Ln, bias=1.0), t)
    t = V(c, stt(a[r, :], fl[r, :], 0.0, a[r, :], ALU.min, ALU.subtract), t)
    t = V(c, lambda e: e.tensor_tensor_scan(fl[r, :], a[r, :], a[r, :], 0.0, ALU.add, ALU.bypass), t)
    tp = V(c, cp(cc["ph"][r, :], fl[r, :]), t)
    t1 = V(c, tt(cc["pl"][r, :], fl[r, :], f32(cc["ph"][r, :]), ALU.subtract), tp)
    t2 = V(c, ts(cc["mh"][r, :], f32(cc["ph"][r, :]), -1.0, None, ALU.mult), tp)
    t3 = V(c, ts(cc["ml"][r, :], f32(cc["pl"][r, :]), -1.0, None, ALU.mult), t1)
    return cc, [t1, t2, t3]


def fox(c, z, zt, ztok, cc, ctok):
    c.phase()
    neg, t0 = c.const("neg")
    negr = c.sb("negr", [P, P], R32)
    idr = c.sb("idr", [P, P], R32)
    t0 = [V(c, cp(negr[:, :], neg[:, :]), t0), V(c, cp(idr[:, :], c.ident[:, :]), c.tid)]
    raw = c.buf("raw", [P, S], 2)
    qk = [{n: c.buf(f"{n}{hh}", [P, S], 1, R32).take() for n in ("qh", "ql", "kh", "kl")} for hh in range(2)]
    for x in qk:
        x["chans"] = [c.chan(), c.chan(), c.chan(), c.chan()]
    vh, vl = (c.buf(n, [P, S], 2, R32) for n in ("vh", "vl"))
    gg = c.buf("gg", [P, S], 2)
    ws = c.buf("w", [P, S], 2)
    wts = [(c.buf(f"WH{n}", [P, 4 * (n + 1), 512], 1, R32).take(), c.buf(f"WL{n}", [P, 4 * (n + 1), 512], 1, R32).take())
           for n in range(2)]
    sts = c.buf("st", [P, 6], 4)
    mix = c.buf("mix", [P, 512], 1)
    sring = Ring([Slot((c.banks[0], c.banks[1])), Slot((c.banks[2], c.banks[3]))])
    tb, ob = c.psum([4, 5, 6]), c.psum([7])
    w0, w1 = ws.slots
    t1 = [V(c, lambda e: e.memset(w0.v[:, :], 0.0)), c.po.do(lambda e: e.memset(w1.v[:, :], 1.0))]
    zeroed = []
    for hh in range(2):
        other = slice(64 * (1 - hh), 64 * (1 - hh) + 64)
        for n in ("qh", "ql", "kh", "kl"):
            zeroed.append(V(c, cp(qk[hh][n].v[other, :], w0.v[other, :]), *t1))
        at = 64 * (1 - hh)
        zeroed.append(V(c, cp(qk[hh]["qh"].v[at:at + 2, :], w1.v[at:at + 2, :]), *t1, c.ve.last))
        ch = c.chan()
        zeroed.append(ch.dma(c.sp, f32(qk[hh]["kh"].v[at + 2:at + 4, :]), w1.v[at:at + 2, :], *zeroed))
    w0.busy = w1.busy = zeroed

    def load(pair, hh):
        x = qk[hh]
        hr, at, head = slice(64 * hh, 64 * hh + 64), 64 * (1 - hh), 2 * pair + hh
        row = slice(112 + head, 113 + head)
        toks = []
        for hi, lo, base, scale in (("qh", "ql", 0, 0.125), ("kh", "kl", 1024, 1.0)):
            b = raw.take()
            r0 = base + pair * P + 64 * hh
            t = b.chan.dma(c.sp, b.v[hr, :], zt[r0:r0 + 64, :], ztok, *b.busy)
            h, l = x[hi], x[lo]
            th = c.ac.do(act(h.v[hr, :], b.v[hr, :], ACT.Copy, scale=scale), t, *h.busy)
            tl = V(c, stt(l.v[hr, :], b.v[hr, :], scale, f32(h.v[hr, :]), ALU.mult, ALU.subtract), th, *l.busy)
            b.busy = [tl]
            toks += [th, tl]
        for n, (dst, r, name) in enumerate((("qh", 2, "ph"), ("qh", 3, "pl"), ("kh", 0, "mh"), ("kh", 1, "ml"))):
            toks.append(x["chans"][n].dma(c.sp, f32(x[dst].v[at + r:at + r + 1, :]), f32(cc[name][row, :]), ctok,
                                          *zeroed, *x[dst].busy))
        d = {"x": x, "tq": toks}
        if hh == 0:
            b, h, l, g = raw.take(), vh.take(), vl.take(), gg.take()
            t = b.chan.dma(c.sp, b.v[:, :].rearrange("p (a e) -> p a e", a=NS),
                           z[:, pair * P:(pair + 1) * P].rearrange("(a p) e -> p a e", p=P), *b.busy)
            th = c.ac.do(act(h.v[:, :], b.v[:, :], ACT.Copy), t, *h.busy)
            tl = V(c, tt(l.v[:, :], b.v[:, :], f32(h.v[:, :]), ALU.subtract), th, *l.busy)
            b.busy = [tl]
            d["v"] = (h, l, [th, tl])
            d["g"] = (g, g.chan.dma(c.sp, g.v[:, :], zt[2048 + pair * P:2048 + (pair + 1) * P, :], *g.busy))
        return d

    def scores(x):
        half, qb, d = x["half"], x["qb"], x["d"]
        q = d["x"]
        qs = slice(qb * P, (qb + 1) * P)
        sr = x["sr"] = sring.take()
        tot = x["tot"] = (qb + 1) * P
        for part in range(half + 1):
            n = min(512, tot - 512 * part)
            bank, kc = sr.v[part], slice(512 * part, 512 * part + n)
            for j, (u, v) in enumerate((("qh", "kh"), ("ql", "kh"), ("qh", "kl"))):
                fn = lambda e, bank=bank, u=q[u], v=q[v], n=n, kc=kc, j=j: e.matmul(
                    bank[:, 0:n], u.v[:, qs], v.v[:, kc], start=(j == 0), stop=(j == 2))
                if j == 1 and part == half:
                    c.pe.go(lambda e, bank=bank, n=n: e.matmul(
                        bank[:, n - P:n], idr[:, :], negr[:, :], start=False, stop=False, skip_group_check=True), t0)
                if j < 2:
                    c.pe.go(fn, sr.busy, d["tq"])
                else:
                    t = c.pe.do(fn)
        x["ts"] = t
        for n in ("qh", "ql", "kh", "kl"):
            q[n].busy = [t]

    def exps(x):
        half, sr, tot = x["half"], x["sr"], x["tot"]
        w, st = ws.take(), sts.take()
        x["w"], x["st"] = w, st
        parts = [(p_, min(512, tot - 512 * p_)) for p_ in range(half + 1)]
        for p_, n in parts:
            t = V(c, lambda e, p_=p_, n=n: e.tensor_reduce(st.v[:, p_:p_ + 1], sr.v[p_][:, 0:n], AX, ALU.max,
                                                           negate=True), x["ts"], *st.busy)
        m = st.v[:, 0:1]
        if half:
            m = st.v[:, 2:3]
            t = V(c, tt(m, st.v[:, 0:1], st.v[:, 1:2], ALU.min), t)
        te = [c.ac.do(act(w.v[:, 512 * p_:512 * p_ + n], sr.v[p_][:, 0:n], ACT.Exp, bias=m,
                          accum_out=st.v[:, 3 + p_:4 + p_]), t, *w.busy) for p_, n in parts]
        sr.busy = te
        x["te"] = te

    def normed(x):
        w, st, te, tot = x["w"], x["st"], x["te"], x["tot"]
        t = te[0]
        if x["half"]:
            t = V(c, tt(st.v[:, 3:4], st.v[:, 3:4], st.v[:, 4:5], ALU.add), *te)
        t = V(c, lambda e: e.reciprocal(st.v[:, 5:6], st.v[:, 3:4]), t)
        x["tn"] = V(c, ts(w.v[:, 0:tot], w.v[:, 0:tot], st.v[:, 5:6], None, ALU.mult), t, *te)
        st.busy = [x["tn"]]

    def turned(x):
        half, qb, w = x["half"], x["qb"], x["w"]
        WH, WL = wts[half]
        for g4 in range(half + 1):
            kbs = list(range(4 * g4, min(4 * g4 + 4, qb + 1)))
            bt, nb = tb.take(), len(kbs)
            t = transposes(c, bt.v, [w.v[:, kb * P:(kb + 1) * P] for kb in kbs], x["tn"], *bt.busy)
            src = bt.v[:, 0:nb * P].rearrange("p (a b) -> p a b", a=nb)
            qo = slice((qb - 4 * half) * P, (qb - 4 * half + 1) * P)
            hi, lo = WH.v[:, 4 * g4:4 * g4 + nb, qo], WL.v[:, 4 * g4:4 * g4 + nb, qo]
            th = c.ac.do(act(hi, src, ACT.Copy), t, *WH.busy)
            tl = V(c, tt(lo, src, f32(hi), ALU.subtract), th, *WL.busy)
            bt.busy = [th, tl]
        w.busy = [t]
        x["tw"] = [th, tl]

    def weighted(x):
        pair, hh, half, d = x["pair"], x["hh"], x["half"], x["d"]
        (vH, vL, tv), (g, tg) = d["v"], d["g"]
        WH, WL = wts[half]
        hr = slice(64 * hh, 64 * hh + 64)
        o, mx = ob.take(), mix.take()
        kbs = list(range(4 * half + 3, -1, -1))
        for kb in kbs:
            off = max(0, kb - 4 * half) * P
            for j, (u, y) in enumerate(((vH, WH), (vL, WH), (vH, WL))):
                last = kb == 0 and j == 2
                fn = lambda e, u=u, y=y, kb=kb, off=off, j=j, last=last: e.matmul(
                    o.v[:, off:512], u.v[:, kb * P:(kb + 1) * P], y.v[:, kb, off:512],
                    start=(kb == kbs[0] and j == 0), stop=last, skip_group_check=True)
                if last:
                    to = c.pe.do(fn)
                else:
                    c.pe.go(fn, x["tw"], tv, *o.busy)
        WH.busy, WL.busy, vH.busy, vL.busy = [to], [to], [to], [to]
        qc = slice(512 * half, 512 * (half + 1))
        t = V(c, tt(mx.v[hr, :], o.v[hr, :], g.v[hr, qc], ALU.mult), to, tg, *mx.busy)
        o.busy, g.busy = [t], [t]
        th = c.ac.do(act(c.XH[hr, pair, qc], mx.v[hr, :], ACT.Copy), t)
        tl = V(c, tt(c.XL[hr, pair, qc], mx.v[hr, :], f32(c.XH[hr, pair, qc]), ALU.subtract), th, t)
        mx.busy = [tl, th]
        for s in range(4 * half, 4 * half + 4):
            c.xt[s] = [th, tl]

    steps = [dict(pair=p, hh=hh, half=qb // 4, qb=qb) for p in range(8) for hh in range(2) for qb in range(8)]
    heads = {(0, 0): load(0, 0)}
    for n in range(len(steps) + 3):
        if n < len(steps):
            x = steps[n]
            x["d"] = heads[x["pair"], x["hh"]]
            scores(x)
        if 0 <= n - 2 < len(steps):
            turned(steps[n - 2])
        if n < len(steps):
            exps(x)
        if 0 <= n - 1 < len(steps):
            normed(steps[n - 1])
        if 0 <= n - 3 < len(steps) and steps[n - 3]["qb"] % 4 == 3:
            weighted(steps[n - 3])
        if n < len(steps) and x["qb"] == 3:
            head = 2 * x["pair"] + x["hh"] + 1
            if head < 16:
                nxt = heads[head // 2, head % 2] = load(head // 2, head % 2)
                if head % 2:
                    nxt["v"], nxt["g"] = x["d"]["v"], x["d"]["g"]


def layer_fox(c, i):
    c.phase()
    c.keep = ExitStack()
    z, zt = c.scratch["z"], c.scratch["zt"]
    c.stage = c.buf("stage", [P, 512], 3)
    win = i["att_w_in_2"][0]
    w = Weights(c, [win[:, 512 * b:512 * (b + 1)] for b in range(8)] + [win[:, 3984:4112]], raw=3)
    modes = ["feat"] * 4 + ["seq"] * 2 + ["feat"] * 2
    dst = []
    for b in range(8):
        if 4 <= b < 6:
            dst.append(lambda j, at=512 * (b - 4): z[j * P:(j + 1) * P, at:at + 512])
        else:
            at = 512 * b if b < 4 else 2048 + 512 * (b - 6)
            dst.append(lambda j, at=at: zt[at + (j // 2) * P:at + (j // 2 + 1) * P, (j % 2) * 512:(j % 2 + 1) * 512])
    tok = project(c, None, modes, dst, w, silu=(6, 7))
    cc, ct = forget_sums(c, w, i["att_b_f_2"][0])
    fox(c, z, zt, tok, cc, ct)
    c.drop = c.keep


def hgrn(c, z, zt, ztok, rec_lb, out_gain):
    c.phase()
    levels, t0 = c.const("levels")
    reset, t1 = c.const("reset")
    lv = levels[:, :].bitcast(I32).rearrange("p (l t) -> p l t", l=8)
    ogt = c.sb("og", [P, 1])
    t2 = c.chan().dma(c.sp, ogt[:, :], out_gain.rearrange("(n a) -> n a", a=1))
    lb = c.sb("lb", [P, 4, 8])
    lr = c.sb("lr", [16, P])
    t = c.chan().dma(c.sp, lr[:, :], rec_lb.rearrange("l (h p) -> (l h) p", p=P))
    tb = c.psum([6, 7])
    b = tb.take()
    t = c.pe.do(lambda e: e.transpose(b.v[:, 0:16], lr[:, :], c.ident[0:16, 0:16]), t, c.tid)
    t = V(c, cp(lb[:, 0:2, :], b.v[:, 0:16].rearrange("p (l h) -> p l h", l=2)), t)
    b.busy = [t]
    t = V(c, tt(lb[:, 2, :], lb[:, 0, :], lb[:, 1, :], ALU.max), t)
    t = V(c, tt(lb[:, 0:2, :], lb[:, 0:2, :], lb[:, 2, :].unsqueeze(1).to_broadcast([P, 2, 8]), ALU.subtract), t)
    t = c.ac.do(act(lb[:, 0:2, :], lb[:, 0:2, :], ACT.Exp), t)
    t = V(c, tt(lb[:, 2, :], lb[:, 0, :], lb[:, 1, :], ALU.add), t)
    t = V(c, lambda e: e.reciprocal(lb[:, 2, :], lb[:, 2, :]), t)
    t = V(c, tt(lb[:, 0:2, :], lb[:, 0:2, :], lb[:, 2, :].unsqueeze(1).to_broadcast([P, 2, 8]), ALU.mult), t)
    tlb = t
    names = ("q", "f", "b", "k", "v", "g", "acc", "ke", "o")
    rings = {n: c.buf(n, [P, S], 2) for n in names}
    ds, q2, k2 = c.buf("D", [P, S], 3), c.buf("q2", [P, S], 3), c.buf("k2", [P, S], 3)
    state = c.buf("state", [P, P], 4)
    sts = c.buf("st", [P, 2, NS], 2)
    sring = Ring([Slot((c.banks[0], c.banks[1])), Slot((c.banks[2], c.banks[3]))])
    obs = c.psum([4, 5])
    junk = c.sb("junk", [P, P])
    r3 = lambda t: t[:, :].rearrange("p (a e) -> p a e", a=NS)

    def head(h):
        q, f, bb, k, v, g, acc, ke, o = (rings[n].take() for n in names)
        st_ = sts.take()
        rows = lambda n: zt[n + h * P:n + (h + 1) * P, :]
        cols = lambda n: z[:, n + h * P:n + (h + 1) * P].rearrange("(a p) e -> p a e", p=P)
        tf = f.chan.dma(c.sp, f.v[:, :], rows(1024), ztok, *f.busy)
        tq = q.chan.dma(c.sp, q.v[:, :], rows(0), *q.busy)
        tv = v.chan.dma(c.sp, r3(v.v), cols(0), *v.busy)
        tg = g.chan.dma(c.sp, r3(g.v), cols(1024), *g.busy)
        tacc = c.po.do(lambda e: e.memset(acc.v[:, :], 0.0), *acc.busy)
        yield
        t = c.ac.do(act(k.v[:, :], f.v[:, :], ACT.Sigmoid, scale=-1.0), tf, *k.busy)
        tk = c.po.do(ts(k.v[:, :], k.v[:, :], lb[:, 0, h:h + 1], None, ALU.mult), t, tlb)
        t = c.ac.do(act(f.v[:, :], f.v[:, :], ACT.Sigmoid), t)
        t = V(c, ts(f.v[:, :], f.v[:, :], lb[:, 0, h:h + 1], lb[:, 1, h:h + 1], ALU.mult, ALU.add), t, tlb)
        yield
        t = c.ac.do(act(f.v[:, :], f.v[:, :], ACT.Ln), t)
        tb_ = V(c, lambda e: e.tensor_tensor_scan(bb.v[:, :], reset[:, :], f.v[:, :], 0.0, ALU.mult, ALU.add),
                t, t1, *bb.busy)
        f.busy = [tb_]
        yield

        def decays(l):
            m = 64 >> l
            d = ds.take()
            bv = bb.v[:, :].rearrange("p (n a m) -> p n a m", a=2, m=m)
            dv = d.v[:, :].rearrange("p (n a m) -> p n a m", a=2, m=m)
            ref = bv[:, :, 0, m - 1:m].to_broadcast([P, S // (2 * m), m])
            V(c, tt(dv[:, :, 0, :], ref, bv[:, :, 0, :], ALU.subtract), tb_, *d.busy)
            t = V(c, tt(dv[:, :, 1, :], bv[:, :, 1, :], ref, ALU.subtract))
            return d, c.ac.do(act(d.v[:, :], d.v[:, :], ACT.Exp), t)

        def scored(l, sr, tm, tacc):
            for half in range(2):
                dst = acc.v[:, 512 * half:512 * (half + 1)].rearrange("p (a t) -> p a t", a=4)
                src = sr.v[half][:, :].rearrange("p (a t) -> p a t", a=4)
                if l < 2:
                    m = 64 >> l
                    for x in range(1 + l):
                        r, cs = slice(2 * m * x, 2 * m * x + m), slice(2 * m * x + m, 2 * m * (x + 1))
                        t = c.ac.do(act(dst[r, :, cs], src[r, :, cs], ACT.Copy), tm, tacc)
                else:
                    mask = lv[:, l, :].unsqueeze(1).to_broadcast([P, 4, P])
                    t = V(c, lambda e, dst=dst, mask=mask, src=src: e.copy_predicated(dst, mask, src), tm, tacc, t0)
            sr.busy = [t]
            return t

        nxt = decays(0)
        held = None

        def products(a, b2, ta, tk2):
            sr = sring.take()
            tm = part_matmuls(c, [(sr.v[n // 4][:, (n % 4) * P:(n % 4 + 1) * P], b2.v[:, n * P:(n + 1) * P],
                                   a.v[:, n * P:(n + 1) * P]) for n in range(NS)], ta, tk2, *sr.busy)
            if a is not q:
                a.busy, b2.busy = [tm], [tm]
            return sr, tm

        for l in range(8):
            yield
            if held is not None:
                sr, tm = products(*held)
            if l < 7:
                d, t = nxt
                a, b2 = q2.take(), k2.take()
                ta = V(c, tt(a.v[:, :], q.v[:, :], d.v[:, :], ALU.mult), t, tq, *a.busy)
                tk2 = c.po.do(tt(b2.v[:, :], k.v[:, :], d.v[:, :], ALU.mult), t, tk, *b2.busy)
                d.busy = [ta, tk2]
                if l < 6:
                    nxt = decays(l + 1)
            else:
                a, b2, ta, tk2 = q, k, tq, tk
            if held is not None:
                tacc = scored(l - 1, sr, tm, tacc)
            held = (a, b2, ta, tk2)
        sr, tm = products(*held)
        d, e2 = ds.take(), ds.take()
        t = c.ac.do(act(d.v[:, :], bb.v[:, :], ACT.Exp), tb_, *d.busy)
        te2 = V(c, tt(r3(e2.v), r3(bb.v)[:, :, P - 1:P].to_broadcast([P, NS, P]), r3(bb.v), ALU.subtract), *e2.busy)
        bb.busy = [te2, t]
        te2 = c.ac.do(act(e2.v[:, :], e2.v[:, :], ACT.Exp), te2)
        tacc = scored(7, sr, tm, tacc)
        ta = V(c, tt(q.v[:, :], q.v[:, :], d.v[:, :], ALU.mult), t, tm)
        a = q
        ex = st_.v[:, 0, :]
        te = V(c, cp(ex, r3(d.v)[:, :, P - 1]), t, *st_.busy)
        d.busy = [ta, te]
        tk2 = c.po.do(tt(k.v[:, :], k.v[:, :], e2.v[:, :], ALU.mult), te2, tm)
        e2.busy = [tk2]
        yield
        tke = []
        for half in range(2):
            b = tb.take()
            t = transposes(c, b.v, [k.v[:, (4 * half + j) * P:(4 * half + j + 1) * P] for j in range(4)], tk2, *b.busy)
            b.busy = [c.ac.do(act(ke.v[:, 512 * half:512 * (half + 1)], b.v[:, :], ACT.Copy), t, *ke.busy)]
            tke += b.busy
        k.busy = [t]
        st, tst = None, None
        for n in range(NS):
            if n:
                yield
            ns = slice(n * P, (n + 1) * P)
            ob = obs.take()
            oc, kc = slice(0, P), slice(P, 2 * P)
            tkv = mm_group(c, ob, [(ob.v[:, kc], ke.v[:, ns], v.v[:, ns])], *tke, tv, *ob.busy)
            items = [(ob.v[:, oc], acc.v[:, ns], v.v[:, ns])]
            if n:
                items.append((ob.v[:, oc], a.v[:, ns], st.v[:, :]))
            to = mm_group(c, ob, items, tacc, tv, ta, tst)
            nx = state.take()
            if n:
                t = V(c, stt(nx.v[:, :], st.v[:, :], ex[:, n:n + 1], ob.v[:, kc], ALU.mult, ALU.add), to, tkv, te, tst,
                      *nx.busy)
                st.busy = [t, to]
            else:
                t = V(c, cp(nx.v[:, :], ob.v[:, kc]), to, tkv, *nx.busy)
            st, tst = nx, t
            t2_ = c.ac.do(act(o.v[:, ns], ob.v[:, oc], ACT.Copy), to, tst, *o.busy)
            tss = c.ac.do(act(junk[:, :], ob.v[:, oc], ACT.Square, accum_out=st_.v[:, 1, n:n + 1]), to, tst,
                          *st_.busy, c.ac.last)
            ob.busy = [tss, tst]
        st.busy = [tst]
        q.busy, ke.busy, v.busy, acc.busy = [to, ta], [tkv], [to], [to]
        ss = st_.v[:, 1, :]
        t = V(c, ts(ss, ss, 1.0 / P, RMS_EPS, ALU.mult, ALU.add), tss)
        t = rsqrt(c, ss, t)
        for n in range(NS):
            ns = slice(n * P, (n + 1) * P)
            t_ = V(c, stt(o.v[:, ns], o.v[:, ns], ss[:, n:n + 1], g.v[:, ns], ALU.mult, ALU.mult), t, t2_, tg)
        t = t_
        st_.busy, g.busy = [t, tst], [t]
        yield
        for half in range(2):
            b = tb.take()
            tt_ = transposes(c, b.v, [o.v[:, (4 * half + j) * P:(4 * half + j + 1) * P] for j in range(4)], t, *b.busy)
            hs = slice(512 * half, 512 * (half + 1))
            th = c.ac.do(act(c.XH[:, h, hs], b.v[:, :], ACT.Copy, scale=ogt[:, 0:1]), tt_, t2)
            tl = V(c, stt(c.XL[:, h, hs], b.v[:, :], ogt[:, 0:1], f32(c.XH[:, h, hs]), ALU.mult, ALU.subtract), th, tt_, t2)
            b.busy = [th, tl]
            for s in range(4 * half, 4 * half + 4):
                c.xt[s] = [th, tl]
        o.busy = [tt_]

    staggered([head(h) for h in range(8)], 9)


def layer_hgrn(c, i):
    c.phase()
    z, zt = c.scratch["z"], c.scratch["zt"]
    c.stage = c.buf("stage", [P, 512], 4)
    win = i["rec_w_in_2"][0]
    modes = ["feat"] * 4 + ["seq"] * 4
    dst = []
    for b in range(8):
        if b >= 4:
            dst.append(lambda j, at=512 * (b - 4): z[j * P:(j + 1) * P, at:at + 512])
        else:
            dst.append(lambda j, at=512 * b: zt[at + (j // 2) * P:at + (j // 2 + 1) * P, (j % 2) * 512:(j % 2 + 1) * 512])
    tok = project(c, [win[:, 512 * b:512 * (b + 1)] for b in range(8)], modes, dst, silu=(6, 7))
    hgrn(c, z, zt, tok, i["rec_lb_2"], i["rec_out_norm_2"][0])


def program(nc, i, consts, out, where, layers=(0, 1, 2, 3)):
    scratch = {
        "h": nc.dram_tensor("sc_h", [S, D], F32, kind="Internal").ap(),
        "z": nc.dram_tensor("sc_z", [S, 4096], F32, kind="Internal").ap(),
        "zt": nc.dram_tensor("sc_zt", [4096, S], F32, kind="Internal").ap(),
    }
    with ExitStack() as ctx:
        c = Ctx(nc, ctx, consts, where, scratch)
        pre = {0: i["norm_gain"][0], 1: i["norm_gain"][1], 2: i["norm_pre_2"][0], 3: i["norm_pre_2"][1]}
        start(c, i["x"][0], pre[layers[0]])
        for n, l in enumerate(layers):
            nxt = layers[n + 1] if n + 1 < len(layers) else None
            kw = {"next_gain": None if nxt is None else pre[nxt], "out": out if nxt is None else None}
            if l == 0:
                layer_even(c, i)
                layer_end(c, i["even_w_out"][0], i["p"][0, 0], i["ple_proj"][0], i["ple_gate"][0], **kw)
            elif l == 1:
                layer_odd(c, i)
                layer_end(c, i["odd_w_out"][0], i["p"][1, 0], i["ple_proj"][1], i["ple_gate"][1],
                          mid_gain=i["final_gain"], **kw)
            elif l == 2:
                layer_fox(c, i)
                layer_end(c, i["att_w_out_2"][0], i["p_2"][0, 0], i["ple_w_proj_2"][0], i["ple_w_gate_2"][0],
                          post_gain=i["norm_post_2"][0], **kw)
            else:
                layer_hgrn(c, i)
                layer_end(c, i["rec_w_out_2"][0], i["p_2"][1, 0], i["ple_w_proj_2"][1], i["ple_w_gate_2"][1],
                          post_gain=i["norm_post_2"][1], **kw)
        c.phase()
        c.stack.close()
        block = ctx.enter_context(nc.Block())
        block.sync(lambda e: c.sp.run(e))
        block.tensor(lambda e: c.pe.run(e))
        block.vector(lambda e: c.ve.run(e))
        block.scalar(lambda e: c.ac.run(e))
        block.gpsimd(lambda e: c.po.run(e))


_INS = ["x", "p", "norm_gain", "final_gain", "ple_proj", "ple_gate", "even_w_in", "even_w_out", "ret_gn_gain",
        "odd_mu", "odd_w_in", "odd_w_out", "rwkv_w0", "rwkv_w1", "rwkv_w2", "rwkv_a0", "rwkv_a1", "rwkv_a2",
        "rwkv_k_k", "rwkv_k_a", "rwkv_r_k", "rwkv_lnx_gain", "rwkv_lnx_bias", "p_2", "norm_pre_2", "norm_post_2",
        "att_w_in_2", "att_b_f_2", "att_w_out_2", "rec_w_in_2", "rec_lb_2", "rec_out_norm_2", "rec_w_out_2",
        "ple_w_proj_2", "ple_w_gate_2"]


def kernel(**inputs):
    import concourse.bacc as _bacc
    from concourse.bass_utils import run_bass_kernel_spmd as _run

    nc = _bacc.Bacc("TRN2", target_bir_lowering=False, num_devices=1)
    arrays, args = {}, {}
    for name in _INS:
        a = np.ascontiguousarray(inputs[name])
        arrays[f"in_{name}"] = a
        args[name] = nc.dram_tensor(f"in_{name}", a.shape, mybir.dt.from_np(a.dtype), kind="ExternalInput").ap()
    table, where = shape_constants()
    arrays["consts"] = table
    consts = nc.dram_tensor("consts", table.shape, F32, kind="ExternalInput").ap()
    out = nc.dram_tensor("out_0", (1, S, D), F32, kind="ExternalOutput").ap()
    program(nc, args, consts, out[0], where)
    r = _run(nc, [arrays], core_ids=[0])
    return r.results[0]["out_0"]
```

```python
from contextlib import ExitStack

import numpy as np

import concourse.bass as bass
from concourse import mybir

P = 128
S = 1024
D = 1024
NS = S // P
NK = D // P
F32 = mybir.dt.float32
R32 = mybir.dt.float32r
I32 = mybir.dt.int32
ALU = mybir.AluOpType
ACT = mybir.ActivationFunctionType
AX = mybir.AxisListType.X
RMS_EPS = 1e-6
GN_EPS = 1e-5
LNX_EPS = 64e-5
RSQRT_CAP = 1e12
NEG = -1.0e30
SQRT_E_INV = float(np.exp(-0.5))


def shape_constants():
    half = 64
    inv = np.float32(10000.0) ** (-np.arange(half, dtype=np.float32) / np.float32(half))
    ang = (np.arange(S, dtype=np.float32)[:, None] * inv[None, :]).astype(np.float32).astype(np.float64)
    cos = np.cos(ang).reshape(NS, P, half).transpose(1, 0, 2)
    sin = np.sin(ang).reshape(NS, P, half).transpose(1, 0, 2)
    lg = np.log(1.0 - 2.0 ** (-5.0 - np.arange(4, dtype=np.float64)))
    c = np.arange(P, dtype=np.float64)
    scale = 128.0 ** -0.5
    diff = c[None, :] - c[:, None]
    intra = np.where(diff[:, None, :] >= 0, np.exp(np.maximum(diff, 0.0)[:, None, :] * lg[None, :, None]), 0.0) * scale
    kdec = np.exp((P - 1 - c)[:, None] * lg[None, :]) * scale
    qdec = np.exp((c + 1)[:, None] * lg[None, :])
    after = (c[None, :] > c[:, None]).astype(np.float64)
    upto = (c[None, :] >= c[:, None]).astype(np.float64)
    levels = []
    for m in (64, 32, 16, 8, 4, 2, 1):
        blk = np.floor(c / (2 * m))
        first = np.floor(c / m) % 2 == 0
        levels.append(((blk[:, None] == blk[None, :]) & first[:, None] & ~first[None, :]).astype(np.float64))
    levels.append(np.eye(P))
    heads2 = (np.floor(c / 64)[:, None] == np.floor(c / 64)[None, :]).astype(np.float64)
    reset = np.ones((P, S))
    reset[:, ::P] = 0.0
    f = lambda a: np.ascontiguousarray(np.asarray(a, np.float32).reshape(P, -1))
    parts = {
        "ident": f(np.eye(P)), "cos": f(cos), "sin": f(sin), "intra": f(intra), "kdec": f(kdec), "qdec": f(qdec),
        "after": f(after), "upto": f(upto),
        "ntri": f(-upto.T), "nones": f(-np.ones((P, P))), "neg": f(np.where(after > 0, NEG, 0.0)),
        "levels": f(np.stack(levels, 1)), "heads2": f(heads2), "cols2": f(heads2[:, ::64]), "reset": f(reset),
    }
    where, at = {}, 0
    for name, a in parts.items():
        where[name] = (at, a.shape[1])
        at += a.shape[1]
    return np.concatenate(list(parts.values()), 1), where


class Line:

    def __init__(self, sem):
        self.todo, self.sem, self.n, self.seen = [], sem, 0, {}

    @property
    def last(self):
        return (self.sem, self.n)

    def wait(self, *tokens):
        for t in tokens:
            if t is None:
                continue
            if isinstance(t, list):
                self.wait(*t)
                continue
            sem, value = t
            if value > self.seen.get(id(sem), 0):
                self.seen[id(sem)] = value
                self.todo.append(lambda e, sem=sem, value=value: e.wait_ge(sem, value))

    def do(self, fn, *tokens):
        self.wait(*tokens)
        self.n += 1
        self.todo.append(lambda e: fn(e).then_inc(self.sem, 1))
        return (self.sem, self.n)

    def go(self, fn, *tokens):
        self.wait(*tokens)
        self.todo.append(fn)

    def run(self, e):
        for fn in self.todo:
            fn(e)


class Chan:

    def __init__(self, sem):
        self.sem, self.n = sem, 0

    @property
    def last(self):
        return (self.sem, 16 * self.n)

    def dma(self, line, out, in_, *tokens):
        line.wait(*tokens)
        self.n += 1
        line.todo.append(lambda e: e.dma_start(out, in_).then_inc(self.sem, 16))
        return (self.sem, 16 * self.n)


class Slot:

    def __init__(self, v, chan=None):
        self.v, self.chan, self.busy = v, chan, []


class Ring:
    def __init__(self, slots):
        self.slots, self.i = slots, 0

    def take(self):
        s = self.slots[self.i % len(self.slots)]
        self.i += 1
        return s


class Ctx:
    def __init__(self, nc, ctx, consts, where, scratch):
        self.nc, self.ctx, self.consts, self.where, self.scratch = nc, ctx, consts, where, scratch
        sem = lambda n: ctx.enter_context(nc.semaphore(n))
        self.pe, self.ve, self.ac, self.po, self.sp = (Line(sem(n)) for n in ("s_pe", "s_ve", "s_ac", "s_po", "s_sp"))
        self.lines = [self.pe, self.ve, self.ac, self.po, self.sp]
        self.chans = [Chan(sem(f"d{i}")) for i in range(80)]
        self.nch = 0
        self.banks = [ctx.enter_context(nc.psum_tensor(f"bank{i}", [P, 512], F32)) for i in range(8)]
        self.bank_slots = [Slot(b) for b in self.banks]
        self.XH = ctx.enter_context(nc.sbuf_tensor("XH", [P, NK, S], R32))
        self.XL = ctx.enter_context(nc.sbuf_tensor("XL", [P, NK, S], R32))
        self.ident = ctx.enter_context(nc.sbuf_tensor("ident", [P, P], F32))
        self.xt = [[] for _ in range(NS)]
        self.forget_features()
        self.nph, self.drop = 0, None
        self.tid = self.chan().dma(self.sp, self.ident[:, :], self.const_in("ident"))

    def forget_features(self):
        self.xk = [[[] for _ in range(NK)] for _ in range(2)]

    def const_in(self, name):
        a, n = self.where[name]
        return self.consts[:, a:a + n]

    def chan(self):
        c = self.chans[self.nch]
        self.nch += 1
        return c

    def phase(self):
        if self.nph:
            self.stack.close()
            if self.drop is not None:
                self.drop.close()
                self.drop = None
            marks = [l.last for l in self.lines] + [c.last for c in self.chans if c.n]
            for l in self.lines:
                l.wait([m for m in marks if m[1] and m[0] is not l.sem or l in (self.ve, self.ac, self.po, self.pe) and m[1]])
        self.nph += 1
        self.nch = 1
        self.stack = ExitStack()

    def sb(self, name, shape, dt=F32):
        return self.stack.enter_context(self.nc.sbuf_tensor(f"{name}_{self.nph}", shape, dt))

    def psum(self, ids):
        return Ring([self.bank_slots[i] for i in ids])

    def const(self, name, shape=None):
        n = self.where[name][1]
        t = self.sb(name, [P, n])
        tok = self.chan().dma(self.sp, t[:, :], self.const_in(name))
        return t, tok

    def buf(self, name, shape, n, dt=F32):
        return Ring([Slot(self.sb(f"{name}{i}", shape, dt), self.chan()) for i in range(n)])


def f32(ap):
    return ap.bitcast(F32)


class Weights:

    def __init__(self, c, srcs, raw=4, ahead=1):
        self.c, self.srcs, self.ahead = c, srcs, ahead
        self.raw = c.buf("wraw", [P, 2, 512], raw)
        self.slots = Ring([Slot((c.sb(f"wh{i}", [P, NK, 512], R32), c.sb(f"wl{i}", [P, NK, 512], R32)))
                           for i in range(2)])
        self.got = []

    def prepare(self, upto):
        c = self.c
        while len(self.got) < min(upto, len(self.srcs)):
            src = self.srcs[len(self.got)]
            n = src.shape[1]
            slot = self.slots.take()
            h, l = slot.v
            toks = []
            for j in range(NK // 2):
                r = self.raw.take()
                t = r.chan.dma(c.sp, r.v[:, :, 0:n], src[256 * j:256 * (j + 1), :].rearrange("(a p) n -> p a n", p=P),
                               *r.busy)
                hj, lj, rj = h[:, 2 * j:2 * j + 2, 0:n], l[:, 2 * j:2 * j + 2, 0:n], r.v[:, :, 0:n]
                th = c.ac.do(lambda e, hj=hj, rj=rj: e.activation(hj, rj, ACT.Copy), t, *slot.busy)
                tl = c.ve.do(lambda e, hj=hj, lj=lj, rj=rj: e.tensor_tensor(lj, rj, f32(hj), ALU.subtract),
                             th, t, *slot.busy)
                r.busy = [tl]
                toks.append([th, tl])
            slot.busy = []
            self.got.append((slot, toks))

    def get(self, i, more=None):
        self.prepare(i + 1 + (self.ahead if more is None else more))
        return self.got[i]


def mm_group(c, bank, terms, *tokens):
    for i, (out, lhsT, rhs) in enumerate(terms):
        fn = lambda e, out=out, lhsT=lhsT, rhs=rhs, i=i: e.matmul(
            out, lhsT, rhs, start=(i == 0), stop=(i == len(terms) - 1))
        if i < len(terms) - 1:
            c.pe.go(fn, *(tokens if i == 0 else ()))
        else:
            return c.pe.do(fn, *(tokens if i == 0 else ()))


def big_product(c, bank, out, xs, w, wtoks, xtoks, half, x_is_lhs):
    last = None
    for k in range(NK):
        (xh, xl), (wh, wl) = xs(k), w(k)
        for j, (a, b) in enumerate(((xh, wh), (xl, wh), (xh, wl))):
            lhsT, rhs = (a, b) if x_is_lhs else (b, a)
            first, stop = k == 0 and j == 0, k == NK - 1 and j == 2
            fn = lambda e, lhsT=lhsT, rhs=rhs, first=first, stop=stop: e.matmul(
                out, lhsT, rhs, start=first, stop=stop)
            tokens = ([bank.busy, xtoks] if first else []) + ([wtoks[k // 2], c.xk[half][k]] if j == 0 else [])
            if stop:
                last = c.pe.do(fn, *tokens)
            else:
                c.pe.go(fn, *tokens)
    bank.busy = [last]
    return last


def seq_tile(c, bank, s, w, n=512, off=0):
    slot, toks = w
    h, l = slot.v
    t = big_product(c, bank, bank.v[:, off:off + n],
                    lambda k: (c.XH[:, k, s * P:(s + 1) * P], c.XL[:, k, s * P:(s + 1) * P]),
                    lambda k: (h[:, k, 0:n], l[:, k, 0:n]), toks, c.xt[s], s // 4, True)
    slot.busy = [t]
    return t


def feat_tile(c, bank, f, sh, w):
    slot, toks = w
    h, l = slot.v
    t = big_product(c, bank, bank.v[:, :],
                    lambda k: (c.XH[:, k, sh * 512:(sh + 1) * 512], c.XL[:, k, sh * 512:(sh + 1) * 512]),
                    lambda k: (h[:, k, f * P:(f + 1) * P], l[:, k, f * P:(f + 1) * P]), toks,
                    [t for s in range(4 * sh, 4 * sh + 4) for t in c.xt[s]], sh, False)
    slot.busy = [t]
    return t


def to_xt(c, rows, s, tbanks, *tokens):
    out = []
    for half in range(2):
        b = tbanks.take()
        for j in range(4):
            k = 4 * half + j
            fn = lambda e, b=b, j=j, k=k: e.transpose(b.v[:, j * P:(j + 1) * P], rows[:, k * P:(k + 1) * P],
                                                      c.ident[:, :])
            if j < 3:
                c.pe.go(fn, *tokens, c.tid, *b.busy)
            else:
                tt = c.pe.do(fn, *tokens)
        out += split_out(c, b, lambda t, half=half: t[:, 4 * half:4 * half + 4, s * P:(s + 1) * P], tt)
    c.xt[s] = out
    return tt


def split_out(c, bank, part, *tokens):
    src = bank.v[:, :].rearrange("p (a b) -> p a b", a=4)
    th = c.ac.do(lambda e: e.activation(part(c.XH), src, ACT.Copy), *tokens)
    tl = c.ve.do(lambda e: e.tensor_tensor(part(c.XL), src, f32(part(c.XH)), ALU.subtract), th, *tokens)
    bank.busy = [th, tl]
    return [th, tl]


def rsqrt(c, ap, *tokens):
    t = c.ac.do(lambda e: e.activation(ap, ap, ACT.Sqrt), *tokens)
    return c.ve.do(lambda e: e.reciprocal(ap, ap), t)


def rms_scale(c, sq, st, srcs, width, eps, *tokens):
    toks = []
    for i, a in enumerate(srcs):
        toks.append(c.ac.do(lambda e, a=a, i=i: e.activation(sq[:, 0:a.shape[1]], a, ACT.Square,
                                                             accum_out=st[:, i:i + 1]), *tokens, c.ac.last))
    if len(srcs) == 2:
        t = c.ve.do(lambda e: e.tensor_tensor(st[:, 0:1], st[:, 0:1], st[:, 1:2], ALU.add), *toks)
    else:
        t = toks[0]
    t = c.ve.do(lambda e: e.tensor_scalar(st[:, 2:3], st[:, 0:1], 1.0 / width, eps, ALU.mult, ALU.add), t)
    return rsqrt(c, st[:, 2:3], t), toks


def row_gain(c, name, src):
    t = c.sb(name, [P, D])
    return t, c.chan().dma(c.sp, t[:, :], src.rearrange("(a n) -> a n", a=1).to_broadcast([P, D]))


def start(c, x, gain, srcs):
    c.phase()
    c.stage = c.buf("stage", [P, 512], 4)
    g, tg = row_gain(c, "g", gain)
    rows, tmp = c.buf("h", [P, D], NS).slots, c.buf("tmp", [P, D], 2)
    sq, st = c.sb("sq", [P, D]), c.sb("st", [P, NS])
    tb = c.psum(range(4))
    w = Weights(c, srcs)
    tr = [r.chan.dma(c.sp, r.v[:, :], x[s * P:(s + 1) * P, :]) for s, r in enumerate(rows)]
    for a, b in ((0, 1), (1, 3), (3, 5), (5, 8)):
        for s in range(a, b):
            t = c.ac.do(lambda e, s=s: e.activation(sq[:, :], rows[s].v[:, :], ACT.Square,
                                                    accum_out=st[:, s:s + 1]), tr[s], c.ac.last)
        t = c.ve.do(lambda e, a=a, b=b: e.tensor_scalar(st[:, a:b], st[:, a:b], 1.0 / D, RMS_EPS, ALU.mult, ALU.add), t)
        t = rsqrt(c, st[:, a:b], t)
        for s in range(a, b):
            m = tmp.take()
            tm = c.ve.do(lambda e, s=s, m=m: e.scalar_tensor_tensor(
                out=m.v[:, :], in0=rows[s].v[:, :], scalar=st[:, s:s + 1], in1=g[:, :], op0=ALU.mult, op1=ALU.mult),
                t, tg, *m.busy)
            m.busy = [to_xt(c, m.v, s, tb, tm)]
        if a == 3:
            w.prepare(1)
    c.h = x
    c.h_tok = [None] * NS
    return w


def project(c, srcs, modes, dst, w=None, first=0, silu=(), behind=None):
    w = w or Weights(c, srcs)
    mm = c.psum(range(8))
    stage = c.stage
    toks = []
    for i, mode in enumerate(modes):
        ready = w.get(first + i)
        for j in range(8):
            b, st = mm.take(), stage.take()
            if mode == "seq":
                t = seq_tile(c, b, j, ready)
            else:
                t = feat_tile(c, b, j % 4, j // 4, ready)
            t_pe = t
            f = ACT.Sigmoid if i in silu else ACT.Copy
            t = c.ac.do(lambda e, b=b, st=st, f=f: e.activation(st.v[:, :], b.v[:, :], f), t, *st.busy)
            if i in silu:
                t = c.ve.do(lambda e, b=b, st=st: e.tensor_tensor(st.v[:, :], b.v[:, :], st.v[:, :], ALU.mult), t)
            b.busy = [t]
            out = dst[i](j)
            st.busy = [st.chan.dma(c.sp, out, st.v[:, :], t)]
            toks += st.busy
            if behind is not None and i == len(modes) - 1 and j % 4 == 3:
                behind(j // 4, t_pe)
    return toks


def layer_end(c, w_out, p, ple_w, gate_w, next_gain, post_gain=None, mid_gain=None, out=None):
    c.phase()
    w = Weights(c, [w_out[:, 0:512], w_out[:, 512:1024], gate_w[:, 0:512], gate_w[:, 512:1024]], raw=3)
    H = c.sb("H", [P, NS, D])
    pT = c.sb("pT", [P, 2, S])
    pw = c.sb("pw", [P, 2, D])
    tmp = c.buf("tmp", [P, D], 1)
    sg = c.buf("sg", [P, 512], 2)
    sts = c.buf("st", [P, 4], 2)
    tb = c.psum([6, 7])
    mm = c.psum(range(6))
    gains = []
    chans = [c.chan() for _ in range(NS)]
    w.prepare(2)
    th = [chans[s].dma(c.sp, H[:, s, :], c.h[s * P:(s + 1) * P, :], c.h_tok[s]) for s in range(NS)]
    if post_gain is not None:
        pg, tpg = row_gain(c, "pg", post_gain)
    tpw = c.chan().dma(c.sp, pw[:, :, :], ple_w.rearrange("(a p) n -> p a n", p=P))
    ready = [None] * NS
    w0, w1 = w.got[0], w.got[1]
    made = [[mm.take(), mm.take()] for _ in range(3)]
    for half, wt in ((0, w0), (1, w1)):
        for s in range(3):
            made[s].append(seq_tile(c, made[s][half], s, wt))
    for s in range(NS + 1):
        if s < NS:
            bs, ts = made[s][:2], made[s][2:]
            if post_gain is None:
                for half in range(2):
                    hs = H[:, s, 512 * half:512 * (half + 1)]
                    ts[half] = c.ve.do(lambda e, hs=hs, b=bs[half]: e.tensor_tensor(hs, b.v[:, :], hs, ALU.add),
                                       ts[half], th[s])
                    bs[half].busy = [ts[half]]
            else:
                st = sts.take()
                sq = sg.take()
                tr, tq = rms_scale(c, sq.v, st.v, [bs[0].v[:, :], bs[1].v[:, :]], D, RMS_EPS, *ts, *st.busy, *sq.busy)
                sq.busy = tq
                m = tmp.take()
                for half in range(2):
                    cs = slice(512 * half, 512 * (half + 1))
                    t = c.ve.do(lambda e, b=bs[half], st=st, cs=cs, m=m: e.scalar_tensor_tensor(
                        out=m.v[:, cs], in0=b.v[:, :], scalar=st.v[:, 2:3], in1=pg[:, cs], op0=ALU.mult, op1=ALU.mult),
                        tr, tpg, *m.busy)
                    bs[half].busy = [t, *tq]
                    ts[half] = c.ve.do(lambda e, s=s, cs=cs, m=m: e.tensor_tensor(H[:, s, cs], m.v[:, cs], H[:, s, cs], ALU.add),
                                       t, th[s])
                st.busy, m.busy = [t], [ts[1]]
            ready[s] = ts
        if s > 0:
            to_xt(c, H[:, s - 1, :], s - 1, tb, *ready[s - 1])
        if s + 3 < NS:
            bs = [mm.take(), mm.take()]
            made.append(bs + [seq_tile(c, bs[0], s + 3, w0), seq_tile(c, bs[1], s + 3, w1)])
    pt = tmp.take()
    tpt = []
    for q in range(2):
        t = pt.chan.dma(c.sp, pt.v[:, :].rearrange("p (a n) -> p a n", a=4),
                        p[512 * q:512 * (q + 1), :].rearrange("(a p) n -> p a n", p=P), *pt.busy)
        for k in range(2):
            b = tb.take()
            for a in range(4):
                fn = lambda e, b=b, a=a, k=k: e.transpose(b.v[:, a * P:(a + 1) * P],
                                                          pt.v[:, a * 256 + k * P:a * 256 + (k + 1) * P], c.ident[:, :])
                if a < 3:
                    c.pe.go(fn, t, c.tid, *b.busy)
                else:
                    tt = c.pe.do(fn)
            b.busy = [c.ac.do(lambda e, b=b, q=q, k=k: e.activation(pT[:, k, 512 * q:512 * (q + 1)], b.v[:, :], ACT.Copy), tt)]
            tpt += b.busy
            pt.busy = [tt]
    w.get(2, more=1)
    w0, w1 = w.got[2], w.got[3]
    ng, tng = (pw, tpw) if next_gain is None else row_gain(c, "ng", next_gain)
    if mid_gain is not None:
        mg, tmg = row_gain(c, "mg", mid_gain)
    toks = [None] * NS
    pending = None
    for s in range(NS + 1):
        if s < NS:
            for half, wt in ((0, w0), (1, w1)):
                cs = slice(512 * half, 512 * (half + 1))
                gb, pb, g = mm.take(), mm.take(), sg.take()
                tg = seq_tile(c, gb, s, wt)
                tp = mm_group(c, pb, [(pb.v[:, :], pT[:, k, s * P:(s + 1) * P], pw[:, k, cs]) for k in range(2)],
                              *tpt, tpw, *pb.busy)
                tg = c.ac.do(lambda e, g=g, gb=gb: e.activation(g.v[:, :], gb.v[:, :], ACT.Sigmoid), tg, *g.busy)
                gb.busy = [tg]
                tp = c.ve.do(lambda e, g=g, pb=pb: e.tensor_tensor(g.v[:, :], pb.v[:, :], g.v[:, :], ALU.mult), tp, tg)
                pb.busy = [tp]
                t = c.ve.do(lambda e, g=g, s=s, cs=cs: e.tensor_tensor(H[:, s, cs], H[:, s, cs], g.v[:, :], ALU.add), tp)
                g.busy = [t]
            hs = H[:, s, :]
            if mid_gain is not None:
                st, m = sts.take(), tmp.take()
                tr, tq = rms_scale(c, m.v, st.v, [hs], D, RMS_EPS, t, *st.busy, *m.busy)
                m.busy = tq
                t = c.ve.do(lambda e, hs=hs, st=st: e.scalar_tensor_tensor(
                    out=hs, in0=hs, scalar=st.v[:, 2:3], in1=mg[:, :], op0=ALU.mult, op1=ALU.mult), tr, tmg, *tq)
                st.busy = [t]
            toks[s] = chans[s].dma(c.sp, (c.scratch["h"] if out is None else out)[s * P:(s + 1) * P, :], hs, t)
        if s > 0 and next_gain is not None:
            st, m = sts.take(), tmp.take()
            tr, tq = rms_scale(c, m.v, st.v, [H[:, s - 1, :]], D, RMS_EPS, pending, *st.busy, *m.busy)
            tm = c.ve.do(lambda e, s=s, m=m, st=st: e.scalar_tensor_tensor(
                out=m.v[:, :], in0=H[:, s - 1, :], scalar=st.v[:, 2:3], in1=ng[:, :], op0=ALU.mult, op1=ALU.mult),
                tr, tng, *tq)
            st.busy = [tm]
            m.busy = [to_xt(c, m.v, s - 1, tb, tm)]
        pending = t
    c.h, c.h_tok = c.scratch["h"], toks


def V(c, fn, *tokens):
    return c.ve.do(fn, *tokens)


def tt(out, a, b, op):
    return lambda e: e.tensor_tensor(out, a, b, op)


def stt(out, a, s, b, op0, op1):
    return lambda e: e.scalar_tensor_tensor(out=out, in0=a, scalar=s, in1=b, op0=op0, op1=op1)


def act(out, a, f, **kw):
    return lambda e: e.activation(out, a, f, **kw)


def ts(out, a, s1, s2, op0, op1=None):
    if op1 is None:
        return lambda e: e.tensor_scalar(out, a, s1, s2, op0)
    return lambda e: e.tensor_scalar(out, a, s1, s2, op0, op1)


def cp(out, a):
    return lambda e: e.tensor_copy(out, a)


def last_axis(ap, shape):
    return ap.unsqueeze(len(ap.shape)).to_broadcast(shape)


def mid_axis(ap, shape):
    return ap.unsqueeze(1).to_broadcast(shape)


def transposes(c, bank, srcs, *tokens):
    for i, a in enumerate(srcs):
        fn = lambda e, i=i, a=a: e.transpose(bank[:, i * P:(i + 1) * P], a, c.ident[:, :])
        if i < len(srcs) - 1:
            c.pe.go(fn, *tokens, c.tid)
        else:
            return c.pe.do(fn, *tokens, c.tid)


def part_matmuls(c, items, *tokens):
    for i, (out, lhsT, rhs) in enumerate(items):
        fn = lambda e, out=out, lhsT=lhsT, rhs=rhs: e.matmul(out, lhsT, rhs, start=True, stop=True)
        if i < len(items) - 1:
            c.pe.go(fn, *tokens)
        else:
            return c.pe.do(fn, *tokens)


def normed_heads(c, o, y, st, eps, *tokens):
    nh = o.shape[1]
    stats, mv = st
    for h in range(nh):
        t = V(c, lambda e, h=h: e.bn_stats(stats[:, h, :], o[:, h, :]), *tokens)
    for h in range(nh):
        t2 = V(c, lambda e, h=h: e.bn_aggr(mv[:, h, :], stats[:, h, :]), t)
    t = V(c, ts(mv[:, :, 1], mv[:, :, 1], eps, None, ALU.add), t2)
    t = rsqrt(c, mv[:, :, 1], t)
    for h in range(nh):
        t2 = V(c, ts(y[:, h, :], o[:, h, :], mv[:, h, 0:1], mv[:, h, 1:2], ALU.subtract, ALU.mult), t)
    return t2


def retention(c, z, ztok, gn_gain):
    c.phase()
    cos, t0 = c.const("cos")
    sin, t1 = c.const("sin")
    intra, t2 = c.const("intra")
    kdec, t3 = c.const("kdec")
    qdec, t4 = c.const("qdec")
    gn = c.sb("gn", [P, 512])
    t5 = c.chan().dma(c.sp, gn[:, :], gn_gain.rearrange("(a n) -> a n", a=1).to_broadcast([P, 512]))
    tk = [t0, t1, t2, t3, t4, t5]
    cos = cos[:, :].rearrange("p (n j) -> p n j", j=64)
    sin = sin[:, :].rearrange("p (n j) -> p n j", j=64)
    intra = intra[:, :]
    zs = c.buf("z", [P, 2048], 3)
    three = lambda n, shape: c.buf(n, shape, 3)
    As, Bs, kds, qkTs, scs, os_, ys, sgs = (three(n, s) for n, s in (
        ("A", [P, 1024]), ("B", [P, 1024]), ("kd", [P, 512]), ("qkT", [P, 1024]), ("sc", [P, 512]),
        ("o", [P, 512]), ("y", [P, 512]), ("sg", [P, 512])))
    stats, mv = c.sb("stats", [P, 4, 6]), c.sb("mv", [P, 4, 2])
    state = c.sb("state", [P, 4, P])
    lg = np.log(1.0 - 2.0 ** (-5.0 - np.arange(4, dtype=np.float64)))
    cd = [float(np.exp(P * x)) for x in lg]
    tb, sb_, ob, ib, kb, xb = (c.psum(x) for x in ([0, 1], [2], [3], [4], [5], [6, 7]))
    carry = {}

    def chunk(n):
        zr, A, B, kd, qkT, sc, o, y, sg = (r.take() for r in (zs, As, Bs, kds, qkTs, scs, os_, ys, sgs))
        tz = zr.chan.dma(c.sp, zr.v[:, :], z[n * P:(n + 1) * P, 0:2048], ztok, *zr.busy)
        qk = zr.v[:, 0:1024].rearrange("p (h a j) -> p h a j", h=8, a=2)
        Av = A.v[:, :].rearrange("p (h a j) -> p h a j", h=8, a=2)
        Bv = B.v[:, :].rearrange("p (h a j) -> p h a j", h=8, a=2)
        b8 = lambda t: t[:, n, :].unsqueeze(1).to_broadcast([P, 8, 64])
        ta = V(c, tt(Av[:, :, 0, :], qk[:, :, 0, :], b8(cos), ALU.mult), tz, *tk, *A.busy)
        ta = V(c, tt(Av[:, :, 1, :], qk[:, :, 1, :], b8(cos), ALU.mult))
        tb1 = c.po.do(tt(Bv[:, :, 0, :], qk[:, :, 1, :], b8(sin), ALU.mult), tz, *tk, *B.busy)
        tb2 = c.po.do(tt(Bv[:, :, 1, :], qk[:, :, 0, :], b8(sin), ALU.mult))
        ta = V(c, tt(Av[:, :, 0, :], Av[:, :, 0, :], Bv[:, :, 0, :], ALU.subtract), ta, tb2)
        ta = V(c, tt(Av[:, :, 1, :], Av[:, :, 1, :], Bv[:, :, 1, :], ALU.add), ta, tb2)
        B.busy = [ta]
        v = zr.v[:, 1024:1536].rearrange("p (h e) -> p h e", h=4)
        kdv = kd.v[:, :].rearrange("p (h e) -> p h e", h=4)
        tkd = V(c, tt(kdv, A.v[:, 512:1024].rearrange("p (h e) -> p h e", h=4),
                      last_axis(kdec[:, :], [P, 4, P]), ALU.mult), ta, *kd.busy)
        tq = []
        for j in range(2):
            b = tb.take()
            t = transposes(c, b.v, [A.v[:, 512 * j + P * h:512 * j + P * (h + 1)] for h in range(4)], ta, *b.busy)
            b.busy = [c.ac.do(act(qkT.v[:, 512 * j:512 * (j + 1)], b.v[:, :], ACT.Copy), t, *qkT.busy)]
            tq += b.busy
        A.busy = [t, tkd]
        yield
        tstate = carry.get("state")
        q = lambda h: qkT.v[:, h * P:(h + 1) * P]
        k = lambda h: qkT.v[:, 512 + h * P:512 + (h + 1) * P]
        b = sb_.take()
        t = part_matmuls(c, [(b.v[:, h * P:(h + 1) * P], k(h), q(h)) for h in range(4)], *tq, *b.busy)
        tsc = V(c, tt(sc.v[:, :], b.v[:, :], intra, ALU.mult), t, *sc.busy)
        b.busy = [tsc]
        bi = ib.take()
        ti = None
        if n:
            ti = part_matmuls(c, [(bi.v[:, h * P:(h + 1) * P], q(h), state[:, h, :]) for h in range(4)],
                              *tq, tstate, *bi.busy)
        bk = kb.take()
        tkv = part_matmuls(c, [(bk.v[:, h * P:(h + 1) * P], kdv[:, h, :], v[:, h, :]) for h in range(4)],
                           tkd, tz, *bk.busy)
        bo = ob.take()
        to = part_matmuls(c, [(bo.v[:, h * P:(h + 1) * P], sc.v[:, h * P:(h + 1) * P], v[:, h, :])
                              for h in range(4)], tsc, *bo.busy)
        qkT.busy, sc.busy, kd.busy = [to], [to], [to]
        for h in range(4):
            hs = slice(h * P, (h + 1) * P)
            if n:
                t = V(c, stt(state[:, h, :], state[:, h, :], cd[h], bk.v[:, hs], ALU.mult, ALU.add), tkv, ti, tstate)
            else:
                t = V(c, cp(state[:, h, :], bk.v[:, hs]), tkv)
        carry["state"] = t
        bk.busy = [t]
        if n:
            t = V(c, tt(o.v[:, :].rearrange("p (h e) -> p h e", h=4), bi.v[:, :].rearrange("p (h e) -> p h e", h=4),
                        last_axis(qdec[:, :], [P, 4, P]), ALU.mult), ti, *o.busy)
            bi.busy = [t]
            t = V(c, tt(o.v[:, :], o.v[:, :], bo.v[:, :], ALU.add), to, t)
        else:
            t = V(c, cp(o.v[:, :], bo.v[:, :]), to, *o.busy)
        bo.busy = [t]
        yield
        ty = normed_heads(c, o.v[:, :].rearrange("p (h e) -> p h e", h=4), y.v[:, :].rearrange("p (h e) -> p h e", h=4),
                          (stats, mv), GN_EPS, t, carry.get("ty"), *y.busy)
        carry["ty"] = ty
        o.busy = [ty]
        t = c.po.do(tt(sg.v[:, :], zr.v[:, 1536:2048], gn[:, :], ALU.mult), tz, *tk, *sg.busy)
        zr.busy = [t, to, tkv, ta, tb2]
        t = V(c, tt(y.v[:, :], y.v[:, :], sg.v[:, :], ALU.mult), t, ty)
        sg.busy = [t]
        yield
        b = xb.take()
        t = transposes(c, b.v, [y.v[:, h * P:(h + 1) * P] for h in range(4)], t, *b.busy)
        y.busy = [t]
        c.xt[n] = split_out(c, b, lambda X, n=n: X[:, 0:4, n * P:(n + 1) * P], t)

    staggered([chunk(n) for n in range(NS)], 1, 4)


def stick(c, z, zt, ztok):
    c.phase()
    ntri, t0 = c.const("ntri")
    nones, t1 = c.const("nones")
    after, t2 = c.const("after")
    tk = [t0, t1, t2]
    scale = 128.0 ** -0.5
    qs, ks, gs, vs = (c.buf(n, [P, S], 4) for n in ("q", "k", "g", "v"))
    a_, l_, sp_, w_ = (c.buf(n, [P, 512], 4) for n in ("a", "l", "sp", "w"))
    R = c.buf("R", [P, 512], 4)
    zb, ob = c.psum([0, 1, 2, 3]), c.psum([4, 5, 6, 7])
    heads = []
    for h in range(4):
        q, k, g, v = (r.take() for r in (qs, ks, gs, vs))
        tq = q.chan.dma(c.sp, q.v[:, :], zt[h * P:(h + 1) * P, :], ztok)
        tkk = k.chan.dma(c.sp, k.v[:, :], zt[512 + h * P:512 + (h + 1) * P, :])
        tv = v.chan.dma(c.sp, v.v[:, :].rearrange("p (a e) -> p a e", a=NS),
                        z[:, 2048 + h * P:2048 + (h + 1) * P].rearrange("(a p) e -> p a e", p=P))
        heads.append((q, k, g, v, tq, tkk, tv))
    for h, (q, k, g, v, tq, tkk, tv) in enumerate(heads):
        tg = g.chan.dma(c.sp, g.v[:, :], zt[1024 + h * P:1024 + (h + 1) * P, :])
        tq = V(c, ts(q.v[:, :], q.v[:, :], scale, None, ALU.mult), tq)
        heads[h] = (q, k, g, v, tq, tkk, tv, tg)

    def chain(h, half):
        q, k, g, v, tq, tkk, tv, tg = heads[h]
        o, r = ob.take(), R.take()
        tr = c.po.do(lambda e: e.memset(r.v[:, :], 0.0), *r.busy)
        top = 4 * half + 3
        late = None
        for kb in range(top, -1, -1):
            off = max(0, kb - 4 * half) * P
            cs, n = slice(off, 512), 512 - off
            qc = slice(512 * half + off, 512 * (half + 1))
            b, a, l, sp, w = (x.take() for x in (zb, a_, l_, sp_, w_))
            kv = k.v[:, kb * P:(kb + 1) * P]
            tz = c.pe.do(lambda e, b=b, n=n, qc=qc, kv=kv: e.matmul(b.v[:, 0:n], kv, q.v[:, qc], start=True, stop=True),
                         tq, tkk, *b.busy)
            if late:
                to = weighted(o, *late)
            t = c.ac.do(act(a.v[:, 0:n], b.v[:, 0:n], ACT.Abs), tz, *a.busy)
            t = c.ac.do(act(a.v[:, 0:n], a.v[:, 0:n], ACT.Exp, scale=-1.0), t)
            yield
            t = c.ac.do(act(l.v[:, 0:n], a.v[:, 0:n], ACT.Ln, bias=1.0), t, *l.busy)
            a.busy = [t]
            t = V(c, stt(sp.v[:, 0:n], b.v[:, 0:n], 0.0, l.v[:, 0:n], ALU.max, ALU.add), t, *sp.busy)
            l.busy = [t]
            if kb >= 4 * half:
                t = V(c, tt(sp.v[:, 0:P], sp.v[:, 0:P], after[:, :], ALU.mult), t, *tk)
            yield
            c.pe.go(lambda e, b=b, sp=sp, n=n: e.matmul(b.v[:, 0:n], ntri[:, :], sp.v[:, 0:n], start=False,
                                                        stop=False, skip_group_check=True), t, *tk)
            tz = c.pe.do(lambda e, b=b, n=n, cs=cs: e.matmul(
                b.v[:, 0:n], nones[:, :], r.v[:, cs], start=False, stop=True, skip_group_check=True), tr)
            if kb:
                tr = c.po.do(tt(r.v[:, cs], r.v[:, cs], sp.v[:, 0:n], ALU.add), t, tz, tr)
            sp.busy = [tz, tr]
            t = c.ac.do(act(w.v[:, 0:n], b.v[:, 0:n], ACT.Exp), tz, *w.busy)
            b.busy = [t]
            if kb >= 4 * half:
                t = V(c, tt(w.v[:, 0:P], w.v[:, 0:P], after[:, :], ALU.mult), t, *tk)
            late = (cs, v.v[:, kb * P:(kb + 1) * P], w, n, kb == top, kb == 0, [t, tv])
            yield
        to = weighted(o, *late)
        r.busy = [to]
        qc = slice(512 * half, 512 * (half + 1))
        t = V(c, tt(g.v[:, qc], o.v[:, :], g.v[:, qc], ALU.mult), to, tg)
        o.busy = [t]
        th = c.ac.do(act(c.XH[:, 4 + h, qc], g.v[:, qc], ACT.Copy), t)
        tl = V(c, tt(c.XL[:, 4 + h, qc], g.v[:, qc], f32(c.XH[:, 4 + h, qc]), ALU.subtract), th, t)
        for s in range(4 * half, 4 * half + 4):
            c.xt[s] = c.xt[s] + [th, tl]

    def weighted(o, cs, vv, w, n, first, last, toks):
        to = c.pe.do(lambda e: e.matmul(o.v[:, cs], vv, w.v[:, 0:n], start=first, stop=last, skip_group_check=True),
                     toks, *o.busy)
        w.busy = [to]
        return to

    alternate(*[chain(h, 1) for h in range(4)])
    alternate(*[chain(h, 0) for h in range(4)])


def layer_even(c, i, w):
    z, zt = c.scratch["z"], c.scratch["zt"]
    order = [(0, "seq", 0), (1, "seq", 512), (2, "seq", 1024), (3, "seq", 1536), (4, "feat", 0), (5, "feat", 512),
             (6, "seq", 2048), (7, "feat", 1024)]
    dst = []
    for blk, mode, at in order:
        if mode == "seq":
            dst.append(lambda j, at=at: z[j * P:(j + 1) * P, at:at + 512])
        else:
            dst.append(lambda j, at=at: zt[at + (j % 4) * P:at + (j % 4 + 1) * P, (j // 4) * 512:(j // 4 + 1) * 512])
    tok = project(c, None, [m for _, m, _ in order], dst, w, silu=(3, 7))
    retention(c, z, tok, i["ret_gn_gain"][0])
    stick(c, z, zt, tok)


def column_blocks(w):
    return [w[:, 512 * b:512 * (b + 1)] for b in range(8)]


VECS = {"mu": 0, "w0": 48, "a0": 56, "k_k": 64, "k_a": 72, "r_k": 80}


def per_feature(c, i, bank):
    rows, vt = c.sb("vrows", [88, P]), c.sb("vt", [P, 88])
    blk = lambda a: a.rearrange("(k q) -> k q", q=P)
    srcs = [i["odd_mu"][0].rearrange("p (k q) -> (p k) q", q=P), blk(i["rwkv_w0"][0]), blk(i["rwkv_a0"][0]),
            blk(i["rwkv_k_k"][0]), blk(i["rwkv_k_a"][0]), i["rwkv_r_k"][0].rearrange("(k a) q -> k (a q)", a=2)]
    at, toks = 0, []
    for a in srcs:
        n = a.shape[0]
        toks.append(c.chan().dma(c.sp, rows[at:at + n, :], a))
        at += n
    t = c.pe.do(lambda e: e.transpose(bank.v[:, 0:88], rows[:, :], c.ident[0:88, 0:88]), c.tid, *toks, *bank.busy)
    t = V(c, cp(vt[:, :], bank.v[:, 0:88]), t)
    bank.busy = [t]
    return vt, t


def shifted(c, n, half, HN, vt, omu, us, xs, tokens, last):
    ps = slice(512 * half, 512 * (half + 1))
    for k in range(NK):
        u, x = us.take(), xs.take()
        t = c.ac.do(act(u.v[:, :], HN[:, k, ps.start + 1:ps.stop + 1], ACT.Copy,
                        scale=omu[:, 8 * n + k:8 * n + k + 1]), *tokens, *u.busy)
        t = V(c, stt(x.v[:, :], HN[:, k, ps], vt[:, 8 * n + k:8 * n + k + 1], u.v[:, :], ALU.mult, ALU.add), t, *x.busy)
        u.busy = [t]
        th = c.ac.do(act(c.XH[:, k, ps], x.v[:, :], ACT.Copy), t, last)
        tl = V(c, tt(c.XL[:, k, ps], x.v[:, :], f32(c.XH[:, k, ps]), ALU.subtract), th, last)
        x.busy = [tl]
        c.xk[half][k] = [th, tl]


def layer_odd(c, i):
    c.phase()
    c.keep = ExitStack()
    z, zt = c.scratch["z"], c.scratch["zt"]
    c.stage = c.buf("stage", [P, 512], 4)
    win = i["odd_w_in"][0]
    tabs = [win[n][:, 512 * j:512 * (j + 1)] for n in range(4) for j in range(2)]
    w = Weights(c, tabs + [i["rwkv_w1"][0], i["rwkv_a1"][0]], raw=3)
    HN = c.sb("HN", [P, NK, S + 1])
    us, xs = c.buf("u", [P, 512], 2), c.buf("x", [P, 512], 3)
    lo = [c.keep.enter_context(c.nc.sbuf_tensor(f"lora{n}", [64, S], F32, side="right")) for n in range(2)]
    vt, tvt = per_feature(c, i, c.bank_slots[0])
    omu = c.sb("omu", [P, 48])
    to = V(c, ts(omu[:, :], vt[:, 0:48], -1.0, 1.0, ALU.mult, ALU.add), tvt)
    t0 = c.po.do(lambda e: e.memset(HN[:, :, 0:1], 0.0))
    hn = [V(c, tt(HN[:, k, 1:S + 1], f32(c.XH[:, k, :]), f32(c.XL[:, k, :]), ALU.add), *[c.xt[s] for s in range(NS)])
          for k in range(NK)]
    c.xt = [[] for _ in range(NS)]
    tokens = [t0, to, tvt, *hn]
    w.prepare(1)
    for half in range(2):
        shifted(c, 0, half, HN, vt, omu, us, xs, tokens, None)
    toks = []
    for n in range(4):
        dst = []
        for j in range(2):
            at = 1024 * n + 512 * j
            if n < 2:
                dst.append(lambda q, at=at: zt[at + (q % 4) * P:at + (q % 4 + 1) * P,
                                               (q // 4) * 512:(q // 4 + 1) * 512])
            else:
                dst.append(lambda q, at=at - 2048: z[q * P:(q + 1) * P, at:at + 512])
        toks += project(c, None, ["feat" if n < 2 else "seq"] * 2, dst, w, first=2 * n, silu=(0, 1) if n == 3 else (),
                        behind=lambda half, t, n=n: shifted(c, n + 1, half, HN, vt, omu, us, xs, tokens, t))
    mm = c.psum(range(8))
    for n in range(2):
        ready = w.get(8 + n)
        for sh in range(2):
            b = mm.take()
            t = feat_tile(c, b, 0, sh, ready)
            b.busy = [c.ac.do(act(lo[n][:, 512 * sh:512 * (sh + 1)], b.v[0:64, :], ACT.Copy if n else ACT.Tanh), t)]
            if n == 0:
                shifted(c, 5, sh, HN, vt, omu, us, xs, tokens, t)
    c.forget_features()
    rwkv(c, i, z, zt, toks, lo)
    c.drop = c.keep


def alternate(*gens):
    gens = [g for g in gens if g is not None]
    while gens:
        for g in list(gens):
            try:
                next(g)
            except StopIteration:
                gens.remove(g)


def staggered(gens, apart, most=2):
    live, age = [], 0
    gens = list(gens)
    while gens or live:
        if gens and (not live or len(live) < most and age >= apart):
            live.append(gens.pop(0))
            age = 0
        for g in list(live):
            try:
                next(g)
            except StopIteration:
                live.remove(g)
        age += 1


def rwkv(c, i, z, zt, ztok, lo):
    c.phase()
    after, t0 = c.const("after")
    upto, t1 = c.const("upto")
    levels, t3 = c.const("levels")
    heads2, t4 = c.const("heads2")
    cols2, t5 = c.const("cols2")
    tk = [t0, t1, t3, t4, t5]
    vt, tvt = per_feature(c, i, c.bank_slots[0])
    vec = lambda n, p: vt[:, VECS[n] + p:VECS[n] + p + 1]
    mask4 = c.sb("mask4", [P, 4, P])
    tm4 = [V(c, ts(mask4[:, 0, :], after[:, :], -1.0, None, ALU.mult), *tk),
           V(c, ts(mask4[:, 1, :], upto[:, :], -1.0, None, ALU.mult)),
           V(c, cp(mask4[:, 2, :], after[:, :])), V(c, cp(mask4[:, 3, :], upto[:, :]))]
    eye = c.ident
    wab = c.buf("wab", [64, 2, P], 2)
    lnr = c.buf("ln", [P, 2, P], 2)
    one = lambda n, shape, k=1: c.buf(n, shape, k)
    rb, kb = one("r", [P, S]), one("k", [P, S])
    gb = one("g", [P, P], 3)
    vz = one("vz", [P, NS, 2, P], 2)
    ab, lb, bb, t1b, t2b = (one(n, [P, S]) for n in ("a", "lw", "b", "t1", "t2"))
    arb = one("ar", [P, NS, 2, P], 2)
    kap, bet = one("kap", [P, S]), one("bet", [P, S])
    kas, bes = one("kas", [P, S], 2), one("bes", [P, S], 2)
    gf = one("gf", [P, NS], 2)
    bon = one("bon", [P, 2 * NS], 2)
    mk, ttf = ([one(f"{n}{x}", [P, 2, w], 2) for x in range(2)] for n, w in (("mk", 512), ("ttf", P)))
    nm, T, TT, X = ([one(f"{n}{x}", [P, 2, P]) for x in range(2)] for n in ("nm", "T", "TT", "X"))
    rz, uz = one("rz", [P, 3, P], 1), one("uz", [P, 3, P], 1)
    st = one("S", [P, P], 2)
    yb = one("y", [P, P], 2)
    stats, mv, nr = c.sb("stats", [P, 2, 6]), c.sb("mv", [P, 2, 2]), c.sb("nr", [P, 2 * NS])
    zero = [c.po.do(lambda e, v=v: e.memset(v, 0.0)) for v in
            [s.v[:, :, :, :] for s in vz.slots] + [rz.slots[0].v[:, :, :], uz.slots[0].v[:, :, :]]]
    xb, yb2 = [c.psum([2]), c.psum([4])], [c.psum([3]), c.psum([5])]
    tb, sq1, sq2 = c.psum([0, 1]), c.psum([6]), c.psum([7])
    halves = [slice(0, 512), slice(512, 1024)]
    r3 = lambda t: t[:, :].rearrange("p (a e) -> p a e", a=NS)

    carry = {}

    def prepare(p, res):
        r, k, VZ, wa, ln = (x.take() for x in (rb, kb, vz, wab, lnr))
        ps = slice(p * P, (p + 1) * P)
        tr = r.chan.dma(c.sp, r.v[:, :], zt[ps, :], ztok, *r.busy)
        tkk = k.chan.dma(c.sp, k.v[:, :], zt[1024 + p * P:1024 + (p + 1) * P, :], *k.busy)
        for n in range(2):
            tw = wa.chan.dma(c.sp, wa.v[:, n, :], i[("rwkv_w2", "rwkv_a2")[n]][0][:, ps], *wa.busy)
        for n in range(2):
            tln = ln.chan.dma(c.sp, ln.v[:, n, :], i[("rwkv_lnx_gain", "rwkv_lnx_bias")[n]][0][ps]
                              .rearrange("(a n) -> a n", a=1).to_broadcast([P, P]), *ln.busy)
        for hh in range(2):
            at = p * P + 64 * hh
            tv = VZ.chan.dma(c.sp, VZ.v[:, :, hh, 64 * hh:64 * hh + 64],
                             z[:, at:at + 64].rearrange("(a p) e -> p a e", p=P), zero, *VZ.busy)
        yield
        a, l, b, s1, s2 = (x.take() for x in (ab, lb, bb, t1b, t2b))
        ta, tl = [], []
        for dst, n, name, out in ((a, 1, "a0", ta), (l, 0, "w0", tl)):
            for hf in halves:
                bk = tb.take()
                t = mm_group(c, bk, [(bk.v[:, :], wa.v[:, n, :], lo[n][:, hf])], tw, *bk.busy)
                out.append(c.ac.do(act(dst.v[:, hf], bk.v[:, :], ACT.Sigmoid, bias=vec(name, p)), t, tvt, *dst.busy))
                bk.busy = [out[-1]]
            yield
        wa.busy = [t]
        t = V(c, ts(l.v[:, :], l.v[:, :], -SQRT_E_INV, None, ALU.mult), *tl)
        for n in range(NS):
            ns = slice(n * P, (n + 1) * P)
            tb_ = V(c, lambda e, ns=ns: e.tensor_tensor_scan(b.v[:, ns], l.v[:, ns], l.v[:, ns], 0.0, ALU.add,
                                                             ALU.bypass), t, *b.busy)
            if n == 3:
                yield
        yield
        kk = s1
        t = V(c, ts(kk.v[:, :], k.v[:, :], vec("k_k", p), None, ALU.mult), tkk, tvt, *s1.busy)
        tkn = t
        t = V(c, tt(s2.v[:, :], kk.v[:, :], kk.v[:, :], ALU.mult), t, *s2.busy)
        bk = tb.take()
        t = part_matmuls(c, [(bk.v[:, 2 * n:2 * n + 2], s2.v[:, n * P:(n + 1) * P], cols2[:, :]) for n in range(NS)],
                         t, *tk, *bk.busy)
        yield
        tc2 = t
        bk.busy = [c.ac.do(act(nr[:, :], bk.v[:, 0:2 * NS], ACT.Sqrt), t, carry.get("nr"))]
        t = V(c, ts(nr[:, :], nr[:, :], 1e-12, None, ALU.max), bk.busy)
        t = V(c, lambda e: e.reciprocal(nr[:, :], nr[:, :]), t)
        yield
        t = c.ac.do(act(s2.v[:, :].rearrange("p (a e) -> p a e", e=64), last_axis(nr[:, :], [P, 2 * NS, 64]), ACT.Copy),
                    t, tc2)
        carry["nr"] = t
        for q, hf in enumerate(halves):
            bk = tb.take()
            t_ = part_matmuls(c, [(bk.v[:, j * P:(j + 1) * P],
                                   s2.v[:, 512 * q + j * P:512 * q + (j + 1) * P],
                                   eye[:, :]) for j in range(4)], t, c.tid, *bk.busy)
            tkn = V(c, tt(kk.v[:, hf], kk.v[:, hf], bk.v[:, :], ALU.mult), t_, tkn)
            bk.busy = [tkn]
            yield
        t = V(c, ts(s2.v[:, :], a.v[:, :], 1.0, vec("k_a", p), ALU.subtract, ALU.mult), t, tkn, *ta)
        yield
        tkk = V(c, stt(k.v[:, :], s2.v[:, :], 1.0, k.v[:, :], ALU.add, ALU.mult), t, tkk)
        for hf in halves:
            yield
            ta2 = c.po.do(tt(a.v[:, hf], a.v[:, hf], kk.v[:, hf], ALU.mult), t, tkn)
        yield
        bo, bk = bon.take(), tb.take()
        t = V(c, stt(s2.v[:, :], r.v[:, :], vec("r_k", p), k.v[:, :], ALU.mult, ALU.mult), tr, tkk)
        t = part_matmuls(c, [(bk.v[:, 2 * n:2 * n + 2], s2.v[:, n * P:(n + 1) * P], cols2[:, :]) for n in range(NS)],
                         t, *tk, *bk.busy)
        tbo = V(c, cp(bo.v[:, :], bk.v[:, 0:2 * NS]), t, *bo.busy)
        bk.busy = [tbo]
        G = gf.take()
        mid = r3(b.v)[:, :, 63:64]
        t = V(c, tt(G.v[:, 0:7], r3(b.v)[:, 0:7, P - 1], r3(b.v)[:, 0:7, 63], ALU.subtract), tb_, *G.busy)
        t = V(c, tt(G.v[:, 0:7], G.v[:, 0:7], r3(b.v)[:, 1:8, 63], ALU.add), t)
        tG = c.ac.do(act(G.v[:, 0:7], G.v[:, 0:7], ACT.Exp), t)
        yield
        tD = V(c, tt(r3(s2.v), r3(b.v), mid.to_broadcast([P, NS, P]), ALU.subtract), tbo, tb_)
        yield
        t3_ = V(c, tt(l.v[:, :], s2.v[:, :], l.v[:, :], ALU.subtract), tD, tb_)
        tE3 = c.ac.do(act(l.v[:, :], l.v[:, :], ACT.Exp), t3_)
        yield
        tE1 = c.ac.do(act(b.v[:, :], s2.v[:, :], ACT.Exp), tD, t)
        tE2 = c.ac.do(act(s2.v[:, :], s2.v[:, :], ACT.Exp, scale=-1.0), t3_, tE1)
        res.update(r=r, k=k, a=a, l=l, b=b, s1=s1, s2=s2, VZ=VZ, G=G, bo=bo, ln=ln, p=p, tG=tG, tbo=tbo, tz=[tv],
                   tln=tln, tal=[tE3, tkn], trh=[tE1, tr], tka=[tE2, tkk], tbe=[tE2, ta2])
        yield

    def factors(d):
        r, k, a, l, b, kk, s2 = (d[n] for n in ("r", "k", "a", "l", "b", "s1", "s2"))
        AR, ka, be, KA, BE = (x.take() for x in (arb, kap, bet, kas, bes))
        tka = V(c, tt(ka.v[:, :], k.v[:, :], s2.v[:, :], ALU.mult), *d["tka"], *ka.busy)
        tbe = c.po.do(tt(be.v[:, :], a.v[:, :], s2.v[:, :], ALU.mult), *d["tbe"], *be.busy)
        tal = V(c, tt(AR.v[:, :, 0, :], r3(kk.v), r3(l.v), ALU.mult), *d["tal"], *AR.busy)
        yield
        trh = c.po.do(tt(AR.v[:, :, 1, :], r3(r.v), r3(b.v), ALU.mult), *d["trh"], *AR.busy)
        yield
        tks = []
        for src, dst, t, sc in ((ka, KA, tka, 1.0), (be, BE, tbe, -1.0)):
            for q in range(2):
                bk = tb.take()
                t_ = transposes(c, bk.v, [src.v[:, (4 * q + j) * P:(4 * q + j + 1) * P] for j in range(4)], t, *bk.busy)
                bk.busy = [c.ac.do(act(dst.v[:, 512 * q:512 * (q + 1)], bk.v[:, :], ACT.Copy, scale=sc), t_, *dst.busy)]
                tks += bk.busy
                yield
        for n, t in (("r", trh), ("k", tka), ("a", tbe), ("l", tal), ("b", trh), ("s1", tal)):
            d[n].busy = [t]
        d["s2"].busy = [tka, tbe]
        d.update(AR=AR, ka=ka, be=be, KA=KA, BE=BE, tar=[tal, trh], tkb=[tka, tbe], tks=tks)

    def inverse(d, n, res):
        x = n % 2
        M, FT = mk[x].take(), ttf[x].take()
        AR, ka, be = d["AR"], d["ka"], d["be"]
        ns = slice(n * P, (n + 1) * P)
        tM = []
        for hh in range(2):
            hr = slice(64 * hh, 64 * hh + 64)
            b = (xb, yb2)[hh][x].take()
            rhs = AR.v[hr, n, :, :].rearrange("p a t -> p (a t)")
            t = part_matmuls(c, [(b.v[:, 0:256], be.v[hr, ns], rhs), (b.v[:, 256:512], ka.v[hr, ns], rhs)],
                             *d["tar"], *d["tkb"], *b.busy)
            b.busy = [V(c, tt(M.v[:, hh, :], b.v[:, :], mask4[:, :, :].rearrange("p a t -> p (a t)"), ALU.mult), t,
                        *tm4, *M.busy)]
            tM += b.busy
            yield
        d["last_use"].append(t)
        b3 = lambda m: m.unsqueeze(1).to_broadcast([P, 2, P])
        lvl = lambda l: levels[:, l * P:(l + 1) * P]
        v2 = lambda b, at=0: b.v[:, at:at + 256].rearrange("p (u t) -> p u t", u=2)
        NT = M.v[:, :, 0:P]
        t_, tt_, x_, m_ = T[x].take(), TT[x].take(), X[x].take(), nm[x].take()
        tm = c.po.do(tt(m_.v[:, :, :], NT, b3(lvl(6)), ALU.mult), *tM, *m_.busy)
        tTT = c.po.do(tt(tt_.v[:, :, :], m_.v[:, :, :], b3(eye[:, :]), ALU.add), tm, *tt_.busy)
        yield
        lk = xb[x].take()
        tL = transposes(c, lk.v, [m_.v[:, u, :] for u in range(2)], tm, *lk.busy)
        tT = V(c, tt(t_.v[:, :, :], v2(lk), b3(eye[:, :]), ALU.add), tL, *t_.busy)
        lk.busy = [tT]
        tm = c.po.do(tt(m_.v[:, :, :], NT, b3(lvl(5)), ALU.mult), tTT, tL)
        yield
        for l in range(5, -1, -1):
            b, b2 = xb[x].take(), yb2[x].take()
            tX = part_matmuls(c, [(b.v[:, u * P:(u + 1) * P], m_.v[:, u, :], t_.v[:, u, :]) for u in range(2)],
                              tm, tT, *b.busy)
            tx = c.ac.do(act(x_.v[:, :, :], v2(b), ACT.Copy), tX, *x_.busy)
            b.busy = [tx]
            if l:
                tm = c.po.do(tt(m_.v[:, :, :], NT, b3(lvl(l - 1)), ALU.mult), tX)
            yield
            items = [(b2.v[:, u * P:(u + 1) * P], x_.v[:, u, :], tt_.v[:, u, :]) for u in range(2)]
            if l:
                items += [(b2.v[:, (2 + u) * P:(3 + u) * P], tt_.v[:, u, :], x_.v[:, u, :]) for u in range(2)]
            tb2 = part_matmuls(c, items, tx, tTT, *b2.busy)
            x_.busy = [tb2]
            if l:
                tT = V(c, tt(t_.v[:, :, :], t_.v[:, :, :], v2(b2, 256), ALU.add), tb2, tT)
                tTT = V(c, tt(tt_.v[:, :, :], tt_.v[:, :, :], v2(b2), ALU.add), tTT)
                b2.busy = [tTT]
            else:
                tTT = V(c, tt(FT.v[:, :, :], tt_.v[:, :, :], v2(b2), ALU.add), tb2, tTT, *FT.busy)
                b2.busy = [tTT]
                t_.busy, tt_.busy, m_.busy = [tX], [tTT, tb2], [tX]
            yield
        res.update(M=M, FT=FT, tM=tM, tT=tTT, d=d, n=n)

    def chain(g, carry):
        d, n = g["d"], g["n"]
        M, FT, AR, VZ, p = g["M"], g["FT"], d["AR"], d["VZ"], d["p"]
        ns = slice(n * P, (n + 1) * P)
        bank, out = sq1.take(), sq2.take()
        S_, tS = carry.get("S"), carry.get("tS")
        al, rh = AR.v[:, n, 0, :], AR.v[:, n, 1, :]
        items = [(bank.v[:, 0:P], M.v[:, hh, 256:384], VZ.v[:, n, hh, :]) for hh in range(2)]
        if n:
            items.append((bank.v[:, 0:P], al, S_.v[:, :]))
        t = mm_group(c, bank, items, *g["tM"], *d["tz"], d["tar"], tS, *bank.busy)
        R, U = rz.take(), uz.take()
        t = c.ac.do(act(own_columns(R), bank.v[:, 0:P].rearrange("p (a b) -> p a b", a=2), ACT.Copy), t, zero, *R.busy)
        yield
        t = mm_group(c, bank, [(bank.v[:, P:2 * P], FT.v[:, hh, :], R.v[:, hh, :]) for hh in range(2)],
                     t, g["tT"])
        R.busy = [t]
        tU = c.ac.do(act(own_columns(U), bank.v[:, P:2 * P].rearrange("p (a b) -> p a b", a=2), ACT.Copy), t, zero, *U.busy)
        bank.busy = [tU]
        yield
        if n < NS - 1:
            t = mm_group(c, bank, [
                (bank.v[:, 2 * P:3 * P], d["KA"].v[:, ns], VZ.v[:, n, hh, :]) for hh in range(2)] + [
                (bank.v[:, 2 * P:3 * P], d["BE"].v[:, ns], U.v[:, hh, :]) for hh in range(2)], tU, d["tks"])
            nx = st.take()
            if n:
                t = V(c, tt(nx.v[:, :], bank.v[:, 2 * P:3 * P], S_.v[:, :], ALU.add), t, tS, *nx.busy)
                tS2 = V(c, stt(nx.v[:, :], nx.v[:, :], d["G"].v[:, n:n + 1], heads2[:, :], ALU.mult, ALU.mult),
                        t, d["tG"])
            else:
                tS2 = V(c, stt(nx.v[:, :], bank.v[:, 2 * P:3 * P], d["G"].v[:, n:n + 1], heads2[:, :],
                               ALU.mult, ALU.mult), t, d["tG"], *nx.busy)
            bank.busy = [tS2]
            carry["S"], carry["tS"] = nx, tS2
        yo = out.v[:, 0:P]
        items = [(yo, M.v[:, hh, 384:512], VZ.v[:, n, hh, :]) for hh in range(2)]
        items += [(yo, M.v[:, hh, P:2 * P], U.v[:, hh, :]) for hh in range(2)]
        if n:
            items.append((yo, rh, S_.v[:, :]))
        t = mm_group(c, out, items, tU, *out.busy)
        U.busy = [t]
        if n:
            S_.busy = [t, tS2] if n < NS - 1 else [t]
        ty = t
        M.busy, FT.busy = [ty], [ty]
        AR.busy = [ty]
        yield
        y, gt = yb.take(), gb.take()
        tg = gt.chan.dma(c.sp, gt.v[:, :], z[ns, 1024 + p * P:1024 + (p + 1) * P], ztok, *gt.busy)
        t = c.ac.do(act(y.v[:, :], yo, ACT.Copy), ty, *y.busy)
        out.busy = [t]
        tc = t
        for hh in range(2):
            es = slice(64 * hh, 64 * hh + 64)
            t = V(c, lambda e, hh=hh, es=es: e.bn_stats(stats[:, hh, :], y.v[:, es]), tc, carry.get("ty"))
        for hh in range(2):
            t = V(c, lambda e, hh=hh: e.bn_aggr(mv[:, hh, :], stats[:, hh, :]), t)
        t = V(c, ts(mv[:, :, 1], mv[:, :, 1], LNX_EPS, None, ALU.add), t)
        t = c.ac.do(act(mv[:, :, 1], mv[:, :, 1], ACT.Sqrt), t)
        yield
        t = V(c, lambda e: e.reciprocal(mv[:, :, 1], mv[:, :, 1]), t)
        for hh in range(2):
            es = slice(64 * hh, 64 * hh + 64)
            t = V(c, ts(y.v[:, es], y.v[:, es], mv[:, hh, 0:1], mv[:, hh, 1:2], ALU.subtract, ALU.mult), t)
        carry["ty"] = t
        ln = d["ln"]
        t = c.po.do(tt(y.v[:, :], y.v[:, :], ln.v[:, 0, :], ALU.mult), t, d["tln"])
        t = c.po.do(tt(y.v[:, :], y.v[:, :], ln.v[:, 1, :], ALU.add), t)
        ln.busy = [t]
        yield
        for hh in range(2):
            es = slice(64 * hh, 64 * hh + 64)
            t2 = V(c, stt(y.v[:, es], VZ.v[:, n, hh, es], d["bo"].v[:, 2 * n + hh:2 * n + hh + 1], y.v[:, es],
                          ALU.mult, ALU.add), t, d["tbo"])
        t = c.po.do(tt(y.v[:, :], y.v[:, :], gt.v[:, :], ALU.mult), t2, tg)
        yield
        gt.busy, d["bo"].busy = [t], [t2]
        VZ.busy = [t2, ty]
        t = transposes(c, out.v, [y.v[:, :]], t, *out.busy)
        y.busy = [t]
        th = c.ac.do(act(c.XH[:, p, ns], out.v[:, 0:P], ACT.Copy), t)
        tl = V(c, tt(c.XL[:, p, ns], out.v[:, 0:P], f32(c.XH[:, p, ns]), ALU.subtract), th, t)
        out.busy = [tl, th]
        c.xt[n] = [th, tl]
        yield
        d["KA"].busy, d["BE"].busy, d["G"].busy = [ty], [ty], [ty]

    data = [{"last_use": []} for _ in range(8)]
    inverses = [[{} for _ in range(NS)] for _ in range(8)]
    done = [0]

    def inverse_line(x):
        for p in range(8):
            while "AR" not in data[p]:
                yield
            if p == 0:
                for _ in range(7 * x):
                    yield
            for n in range(x, NS, 2):
                yield from inverse(data[p], n, inverses[p][n])

    def chain_line():
        for p in range(8):
            for n in range(NS):
                while not inverses[p][n]:
                    yield
                yield from chain(inverses[p][n], carry)
            done[0] += 1

    def factor_line():
        for p in range(8):
            while done[0] < p - 1:
                yield
            for _ in prepare(p, data[p]):
                yield
                yield
            if p:
                while len(data[p - 1]["last_use"]) < NS:
                    yield
                data[p - 1]["ka"].busy = data[p - 1]["be"].busy = data[p - 1]["last_use"]
            yield from factors(data[p])

    alternate(inverse_line(0), inverse_line(1), chain_line(), factor_line())


def own_columns(s):
    return s.v[:, :, :].rearrange("p a b -> p (a b)").rearrange("p (a b) -> p a b", a=2)[:, :, 0:64]


def forget_sums(c, w, b_f):
    ready = w.get(4)
    cc = {n: c.keep.enter_context(c.nc.sbuf_tensor(f"c_{n}", [P, S], R32, side="right"))
          for n in ("ph", "pl", "mh", "ml")}
    fl, a, one = c.sb("fl", [P, S]), c.sb("fa", [P, S]), c.sb("fb", [P, 1])
    mm = c.psum(range(2))
    r = slice(96, 128)
    tb0 = V(c, lambda e: e.memset(one[r, :], 0.0))
    tb0 = c.chan().dma(c.sp, one[112:128, :], b_f.rearrange("(a n) -> a n", n=1), tb0)
    ts_ = []
    for sh in range(2):
        b = mm.take()
        t = feat_tile(c, b, 0, sh, ready)
        cs = slice(512 * sh, 512 * (sh + 1))
        ts_.append(c.ac.do(act(fl[r, cs], b.v[r, :], ACT.Identity, bias=one[r, :]), t, tb0))
        b.busy = ts_[-1:]
    t = c.ac.do(act(a[r, :], fl[r, :], ACT.Abs), *ts_)
    t = c.ac.do(act(a[r, :], a[r, :], ACT.Exp, scale=-1.0), t)
    t = c.ac.do(act(a[r, :], a[r, :], ACT.Ln, bias=1.0), t)
    t = V(c, stt(a[r, :], fl[r, :], 0.0, a[r, :], ALU.min, ALU.subtract), t)
    t = V(c, lambda e: e.tensor_tensor_scan(fl[r, :], a[r, :], a[r, :], 0.0, ALU.add, ALU.bypass), t)
    tp = V(c, cp(cc["ph"][r, :], fl[r, :]), t)
    t1 = V(c, tt(cc["pl"][r, :], fl[r, :], f32(cc["ph"][r, :]), ALU.subtract), tp)
    t2 = V(c, ts(cc["mh"][r, :], f32(cc["ph"][r, :]), -1.0, None, ALU.mult), tp)
    t3 = V(c, ts(cc["ml"][r, :], f32(cc["pl"][r, :]), -1.0, None, ALU.mult), t1)
    return cc, [t1, t2, t3]


def fox(c, z, zt, ztok, cc, ctok):
    c.phase()
    neg, t0 = c.const("neg")
    negr = c.sb("negr", [P, P], R32)
    idr = c.sb("idr", [P, P], R32)
    t0 = [V(c, cp(negr[:, :], neg[:, :]), t0), V(c, cp(idr[:, :], c.ident[:, :]), c.tid)]
    raw = c.buf("raw", [P, S], 2)
    qk = [{n: c.buf(f"{n}{hh}", [P, S], 1, R32).take() for n in ("qh", "ql", "kh", "kl")} for hh in range(2)]
    for x in qk:
        x["chans"] = [c.chan(), c.chan(), c.chan(), c.chan()]
    vh, vl = (c.buf(n, [P, S], 2, R32) for n in ("vh", "vl"))
    gg = c.buf("gg", [P, S], 2)
    ws = c.buf("w", [P, S], 2)
    wts = [(c.buf(f"WH{n}", [P, 4 * (n + 1), 512], 1, R32).take(), c.buf(f"WL{n}", [P, 4 * (n + 1), 512], 1, R32).take())
           for n in range(2)]
    sts, dgs = c.buf("st", [P, 6], 4), c.buf("dg", [P, P], 3)
    mix = c.buf("mix", [P, 512], 1)
    sring = Ring([Slot((c.banks[0], c.banks[1])), Slot((c.banks[2], c.banks[3]))])
    tb, ob = c.psum([4, 5, 6]), c.psum([7])

    w0, w1 = ws.slots
    t1 = [V(c, lambda e: e.memset(w0.v[:, :], 0.0)), c.po.do(lambda e: e.memset(w1.v[:, :], 1.0))]
    zeroed = []
    for hh in range(2):
        other = slice(64 * (1 - hh), 64 * (1 - hh) + 64)
        for n in ("qh", "ql", "kh", "kl"):
            zeroed.append(V(c, cp(qk[hh][n].v[other, :], w0.v[other, :]), *t1))
        at = 64 * (1 - hh)
        zeroed.append(V(c, cp(qk[hh]["qh"].v[at:at + 2, :], w1.v[at:at + 2, :]), *t1, c.ve.last))
        ch = c.chan()
        zeroed.append(ch.dma(c.sp, f32(qk[hh]["kh"].v[at + 2:at + 4, :]), w1.v[at:at + 2, :], *zeroed))
    w0.busy = w1.busy = zeroed

    def load(pair, hh, d):
        x = qk[hh]
        hr, at, head = slice(64 * hh, 64 * hh + 64), 64 * (1 - hh), 2 * pair + hh
        row = slice(112 + head, 113 + head)
        toks, got = [], []
        for base in (0, 1024):
            b = raw.take()
            r0 = base + pair * P + 64 * hh
            got.append((b, b.chan.dma(c.sp, b.v[hr, :], zt[r0:r0 + 64, :], ztok, *b.busy)))
        for n, (dst, r, name) in enumerate((("qh", 2, "ph"), ("qh", 3, "pl"), ("kh", 0, "mh"), ("kh", 1, "ml"))):
            toks.append(x["chans"][n].dma(c.sp, f32(x[dst].v[at + r:at + r + 1, :]), f32(cc[name][row, :]), ctok,
                                          *zeroed, *x[dst].busy))
        yield
        for (hi, lo, scale), (b, t) in zip((("qh", "ql", 0.125), ("kh", "kl", 1.0)), list(got)):
            h, l = x[hi], x[lo]
            th = c.ac.do(act(h.v[hr, :], b.v[hr, :], ACT.Copy, scale=scale), t, *h.busy)
            tl = V(c, stt(l.v[hr, :], b.v[hr, :], scale, f32(h.v[hr, :]), ALU.mult, ALU.subtract), th, *l.busy)
            b.busy = [tl]
            toks += [th, tl]
            if hi == "kh":
                d.update(x=x, tq=toks)
            elif hh == 0:
                b, g = raw.take(), gg.take()
                t = b.chan.dma(c.sp, b.v[:, :].rearrange("p (a e) -> p a e", a=NS),
                               z[:, pair * P:(pair + 1) * P].rearrange("(a p) e -> p a e", p=P), *b.busy)
                got.append((b, t))
                d["g"] = (g, g.chan.dma(c.sp, g.v[:, :], zt[2048 + pair * P:2048 + (pair + 1) * P, :], *g.busy))
            yield
        if hh == 0:
            (b, t), h, l = got[2], vh.take(), vl.take()
            th = c.ac.do(act(h.v[:, :], b.v[:, :], ACT.Copy), t, *h.busy)
            tl = V(c, tt(l.v[:, :], b.v[:, :], f32(h.v[:, :]), ALU.subtract), th, *l.busy)
            b.busy = [tl]
            d["v"] = (h, l, [th, tl])
            yield

    def scores(x):
        half, qb, d = x["half"], x["qb"], x["d"]
        q = d["x"]
        qs = slice(qb * P, (qb + 1) * P)
        sr = x["sr"] = sring.take()
        tot = x["tot"] = (qb + 1) * P
        for part in range(half + 1):
            n = min(512, tot - 512 * part)
            bank, kc = sr.v[part], slice(512 * part, 512 * part + n)
            for j, (u, v) in enumerate((("qh", "kh"), ("ql", "kh"), ("qh", "kl"))):
                fn = lambda e, bank=bank, u=q[u], v=q[v], n=n, kc=kc, j=j: e.matmul(
                    bank[:, 0:n], u.v[:, qs], v.v[:, kc], start=(j == 0), stop=(j == 2))
                if j == 1 and part == half:
                    c.pe.go(lambda e, bank=bank, n=n: e.matmul(
                        bank[:, n - P:n], idr[:, :], negr[:, :], start=False, stop=False, skip_group_check=True), t0)
                if j < 2:
                    c.pe.go(fn, sr.busy, d["tq"])
                else:
                    t = c.pe.do(fn)
        x["ts"] = t
        for n in ("qh", "ql", "kh", "kl"):
            q[n].busy = [t]

    def exps(x):
        half, sr, tot = x["half"], x["sr"], x["tot"]
        w, st = ws.take(), sts.take()
        x["w"], x["st"] = w, st
        parts = [(p_, min(512, tot - 512 * p_)) for p_ in range(half + 1)]
        for p_, n in parts:
            t = V(c, lambda e, p_=p_, n=n: e.tensor_reduce(st.v[:, p_:p_ + 1], sr.v[p_][:, 0:n], AX, ALU.max,
                                                           negate=True), x["ts"], *st.busy)
        m = st.v[:, 0:1]
        if half:
            m = st.v[:, 2:3]
            t = V(c, tt(m, st.v[:, 0:1], st.v[:, 1:2], ALU.min), t)
        te = [c.ac.do(act(w.v[:, 512 * p_:512 * p_ + n], sr.v[p_][:, 0:n], ACT.Exp, bias=m,
                          accum_out=st.v[:, 3 + p_:4 + p_]), t, *w.busy) for p_, n in parts]
        sr.busy = te
        x["te"] = te

    def normed(x):
        w, st, te, tot = x["w"], x["st"], x["te"], x["tot"]
        t = te[0]
        if x["half"]:
            t = V(c, tt(st.v[:, 3:4], st.v[:, 3:4], st.v[:, 4:5], ALU.add), *te)
        t = V(c, lambda e: e.reciprocal(st.v[:, 5:6], st.v[:, 3:4]), t)
        dg = x["dg"] = dgs.take()
        x["tn"] = V(c, ts(dg.v[:, :], c.ident[:, :], st.v[:, 5:6], None, ALU.mult), t, c.tid, *dg.busy)
        st.busy = [x["tn"]]

    def turned(x):
        half, qb, w, dg = x["half"], x["qb"], x["w"], x["dg"]
        WH = wts[half][0]
        x["low"] = []
        for g4 in range(half + 1):
            kbs = list(range(4 * g4, min(4 * g4 + 4, qb + 1)))
            bt, nb = tb.take(), len(kbs)
            t = part_matmuls(c, [(bt.v[:, j * P:(j + 1) * P], w.v[:, kb * P:(kb + 1) * P], dg.v[:, :])
                                 for j, kb in enumerate(kbs)], x["tn"], *x["te"], *bt.busy)
            src = bt.v[:, 0:nb * P].rearrange("p (a b) -> p a b", a=nb)
            part = (slice(0, P), slice(4 * g4, 4 * g4 + nb), slice((qb - 4 * half) * P, (qb - 4 * half + 1) * P))
            th = c.ac.do(act(WH.v[part], src, ACT.Copy), t, *WH.busy)
            bt.busy = [th]
            x["low"].append((bt, src, part, th))
        w.busy = dg.busy = [t]

    def lowered(x, g4):
        WH, WL = wts[x["half"]]
        if g4 < len(x["low"]):
            bt, src, part, th = x["low"][g4]
            x["tw"] = V(c, tt(WL.v[part], src, f32(WH.v[part]), ALU.subtract), th, *WL.busy)
            bt.busy = [th, x["tw"]]

    def weighted(x):
        pair, hh, half, d = x["pair"], x["hh"], x["half"], x["d"]
        (vH, vL, tv), (g, tg) = d["v"], d["g"]
        WH, WL = wts[half]
        hr = slice(64 * hh, 64 * hh + 64)
        o, mx = ob.take(), mix.take()
        kbs = list(range(4 * half + 3, -1, -1))
        for kb in kbs:
            off = max(0, kb - 4 * half) * P
            for j, (u, y) in enumerate(((vH, WH), (vL, WH), (vH, WL))):
                last = kb == 0 and j == 2
                fn = lambda e, u=u, y=y, kb=kb, off=off, j=j, last=last: e.matmul(
                    o.v[:, off:512], u.v[:, kb * P:(kb + 1) * P], y.v[:, kb, off:512],
                    start=(kb == kbs[0] and j == 0), stop=last, skip_group_check=True)
                if last:
                    to = c.pe.do(fn)
                else:
                    c.pe.go(fn, x["tw"], tv, *o.busy)
        WH.busy, WL.busy, vH.busy, vL.busy = [to], [to], [to], [to]
        qc = slice(512 * half, 512 * (half + 1))
        t = V(c, tt(mx.v[hr, :], o.v[hr, :], g.v[hr, qc], ALU.mult), to, tg, *mx.busy)
        o.busy, g.busy = [t], [t]
        th = c.ac.do(act(c.XH[hr, pair, qc], mx.v[hr, :], ACT.Copy), t)
        tl = V(c, tt(c.XL[hr, pair, qc], mx.v[hr, :], f32(c.XH[hr, pair, qc]), ALU.subtract), th, t)
        mx.busy = [tl, th]
        for s in range(4 * half, 4 * half + 4):
            c.xt[s] = [th, tl]

    steps = [dict(pair=p, hh=hh, half=qb // 4, qb=qb) for p in range(8) for hh in range(2) for qb in range(8)]
    heads = {(p, hh): {} for p in range(8) for hh in range(2)}
    for _ in load(0, 0, heads[0, 0]):
        pass
    ahead = iter(())
    at = lambda n: steps[n] if 0 <= n < len(steps) else None
    for n in range(len(steps) + 4):
        x, x1, x2, x3, x4 = (at(n - lag) for lag in range(5))
        if x:
            x["d"] = heads[x["pair"], x["hh"]]
            scores(x)
        if x3:
            lowered(x3, 0)
        if x2:
            turned(x2)
        if x:
            exps(x)
        if x3:
            lowered(x3, 1)
        if x1:
            normed(x1)
        if x4 and x4["qb"] % 4 == 3:
            weighted(x4)
        if x and x["qb"] == 2:
            if x["hh"]:
                x["d"]["v"], x["d"]["g"] = (heads[x["pair"], 0][name] for name in ("v", "g"))
            head = 2 * x["pair"] + x["hh"] + 1
            ahead = load(head // 2, head % 2, heads[head // 2, head % 2]) if head < 16 else iter(())
        next(ahead, None)


def layer_fox(c, i):
    c.phase()
    c.keep = ExitStack()
    z, zt = c.scratch["z"], c.scratch["zt"]
    c.stage = c.buf("stage", [P, 512], 3)
    win = i["att_w_in_2"][0]
    w = Weights(c, [win[:, 512 * b:512 * (b + 1)] for b in range(4)] + [win[:, 3984:4112]] +
                [win[:, 512 * b:512 * (b + 1)] for b in range(4, 8)], raw=3)
    modes = ["feat"] * 4 + ["seq"] * 2 + ["feat"] * 2
    dst = []
    for b in range(8):
        if 4 <= b < 6:
            dst.append(lambda j, at=512 * (b - 4): z[j * P:(j + 1) * P, at:at + 512])
        else:
            at = 512 * b if b < 4 else 2048 + 512 * (b - 6)
            dst.append(lambda j, at=at: zt[at + (j % 4) * P:at + (j % 4 + 1) * P, (j // 4) * 512:(j // 4 + 1) * 512])
    tok = project(c, None, modes[:4], dst[:4], w)
    cc, ct = forget_sums(c, w, i["att_b_f_2"][0])
    tok += project(c, None, modes[4:], dst[4:], w, first=5, silu=(2, 3))
    fox(c, z, zt, tok, cc, ct)
    c.drop = c.keep


def hgrn(c, z, zt, ztok, rec_lb, out_gain):
    c.phase()
    levels, t0 = c.const("levels")
    reset, t1 = c.const("reset")
    lv = levels[:, :].bitcast(I32).rearrange("p (l t) -> p l t", l=8)
    ogt = c.sb("og", [P, 1])
    t2 = c.chan().dma(c.sp, ogt[:, :], out_gain.rearrange("(n a) -> n a", a=1))
    lb = c.sb("lb", [P, 4, 8])
    lr = c.sb("lr", [16, P])
    t = c.chan().dma(c.sp, lr[:, :], rec_lb.rearrange("l (h p) -> (l h) p", p=P))
    tb = c.psum([6, 7])
    b = tb.take()
    t = c.pe.do(lambda e: e.transpose(b.v[:, 0:16], lr[:, :], c.ident[0:16, 0:16]), t, c.tid)
    t = V(c, cp(lb[:, 0:2, :], b.v[:, 0:16].rearrange("p (l h) -> p l h", l=2)), t)
    b.busy = [t]
    t = V(c, tt(lb[:, 2, :], lb[:, 0, :], lb[:, 1, :], ALU.max), t)
    t = V(c, tt(lb[:, 0:2, :], lb[:, 0:2, :], lb[:, 2, :].unsqueeze(1).to_broadcast([P, 2, 8]), ALU.subtract), t)
    t = c.ac.do(act(lb[:, 0:2, :], lb[:, 0:2, :], ACT.Exp), t)
    t = V(c, tt(lb[:, 2, :], lb[:, 0, :], lb[:, 1, :], ALU.add), t)
    t = V(c, lambda e: e.reciprocal(lb[:, 2, :], lb[:, 2, :]), t)
    t = V(c, tt(lb[:, 0:2, :], lb[:, 0:2, :], lb[:, 2, :].unsqueeze(1).to_broadcast([P, 2, 8]), ALU.mult), t)
    tlb = t
    names = ("q", "f", "b", "k", "v", "g", "acc", "ke", "o")
    rings = {n: c.buf(n, [P, S], 2) for n in names}
    ds, q2, k2 = c.buf("D", [P, S], 3), c.buf("q2", [P, S], 3), c.buf("k2", [P, S], 3)
    state = c.buf("state", [P, P], 4)
    sts = c.buf("st", [P, 2, NS], 2)
    sring = Ring([Slot((c.banks[0], c.banks[1])), Slot((c.banks[2], c.banks[3]))])
    obs = c.psum([4, 5])
    junk = c.sb("junk", [P, P])
    r3 = lambda t: t[:, :].rearrange("p (a e) -> p a e", a=NS)

    def head(h):
        q, f, bb, k, v, g, acc, ke, o = (rings[n].take() for n in names)
        st_ = sts.take()
        rows = lambda n: zt[n + h * P:n + (h + 1) * P, :]
        cols = lambda n: z[:, n + h * P:n + (h + 1) * P].rearrange("(a p) e -> p a e", p=P)
        tf = f.chan.dma(c.sp, f.v[:, :], rows(1024), ztok, *f.busy)
        tq = q.chan.dma(c.sp, q.v[:, :], rows(0), *q.busy)
        tv = v.chan.dma(c.sp, r3(v.v), cols(0), *v.busy)
        tg = g.chan.dma(c.sp, r3(g.v), cols(1024), *g.busy)
        tacc = c.po.do(lambda e: e.memset(acc.v[:, :], 0.0), *acc.busy)
        yield
        tk = c.ac.do(act(k.v[:, :], f.v[:, :], ACT.Sigmoid, scale=-1.0), tf, *k.busy)
        t = c.ac.do(act(f.v[:, :], f.v[:, :], ACT.Sigmoid), tk)
        yield
        tk = V(c, ts(k.v[:, :], k.v[:, :], lb[:, 0, h:h + 1], None, ALU.mult), tk, tlb)
        t = V(c, ts(f.v[:, :], f.v[:, :], lb[:, 0, h:h + 1], lb[:, 1, h:h + 1], ALU.mult, ALU.add), t, tlb)
        t = c.ac.do(act(f.v[:, :], f.v[:, :], ACT.Ln), t)
        tb_ = V(c, lambda e: e.tensor_tensor_scan(bb.v[:, :], reset[:, :], f.v[:, :], 0.0, ALU.mult, ALU.add),
                t, t1, *bb.busy)
        f.busy = [tb_]
        yield

        def decays(l):
            m = 64 >> l
            d = ds.take()
            bv = bb.v[:, :].rearrange("p (n a m) -> p n a m", a=2, m=m)
            dv = d.v[:, :].rearrange("p (n a m) -> p n a m", a=2, m=m)
            ref = bv[:, :, 0, m - 1:m].to_broadcast([P, S // (2 * m), m])
            V(c, tt(dv[:, :, 0, :], ref, bv[:, :, 0, :], ALU.subtract), tb_, *d.busy)
            t = V(c, tt(dv[:, :, 1, :], bv[:, :, 1, :], ref, ALU.subtract))
            return d, c.ac.do(act(d.v[:, :], d.v[:, :], ACT.Exp), t)

        def scored(l, sr, tm, tacc):
            for half in range(2):
                dst = acc.v[:, 512 * half:512 * (half + 1)].rearrange("p (a t) -> p a t", a=4)
                src = sr.v[half][:, :].rearrange("p (a t) -> p a t", a=4)
                if l < 3:
                    m = 64 >> l
                    for x in range(1 << l):
                        r, cs = slice(2 * m * x, 2 * m * x + m), slice(2 * m * x + m, 2 * m * (x + 1))
                        t = c.ac.do(act(dst[r, :, cs], src[r, :, cs], ACT.Copy), tm, tacc)
                else:
                    mask = lv[:, l, :].unsqueeze(1).to_broadcast([P, 4, P])
                    t = V(c, lambda e, dst=dst, mask=mask, src=src: e.copy_predicated(dst, mask, src), tm, tacc, t0)
            sr.busy = [t]
            return t

        nxt = decays(0)
        held = None

        def products(a, b2, ta, tk2):
            sr = sring.take()
            tm = part_matmuls(c, [(sr.v[n // 4][:, (n % 4) * P:(n % 4 + 1) * P], b2.v[:, n * P:(n + 1) * P],
                                   a.v[:, n * P:(n + 1) * P]) for n in range(NS)], ta, tk2, *sr.busy)
            if a is not q:
                a.busy, b2.busy = [tm], [tm]
            return sr, tm

        for l in range(8):
            yield
            if held is not None:
                sr, tm = products(*held)
            if l < 7:
                d, t = nxt
                a, b2 = q2.take(), k2.take()
                ta = V(c, tt(a.v[:, :], q.v[:, :], d.v[:, :], ALU.mult), t, tq, *a.busy)
                tk2 = c.po.do(tt(b2.v[:, :], k.v[:, :], d.v[:, :], ALU.mult), t, tk, *b2.busy)
                d.busy = [ta, tk2]
                if l < 6:
                    nxt = decays(l + 1)
            else:
                a, b2, ta, tk2 = q, k, tq, tk
            if held is not None:
                tacc = scored(l - 1, sr, tm, tacc)
            held = (a, b2, ta, tk2)
        sr, tm = products(*held)
        d, e2 = ds.take(), ds.take()
        t = c.ac.do(act(d.v[:, :], bb.v[:, :], ACT.Exp), tb_, *d.busy)
        te2 = V(c, tt(r3(e2.v), r3(bb.v)[:, :, P - 1:P].to_broadcast([P, NS, P]), r3(bb.v), ALU.subtract), *e2.busy)
        bb.busy = [te2, t]
        te2 = c.ac.do(act(e2.v[:, :], e2.v[:, :], ACT.Exp), te2)
        tacc = scored(7, sr, tm, tacc)
        ta = V(c, tt(q.v[:, :], q.v[:, :], d.v[:, :], ALU.mult), t, tm)
        a = q
        ex = st_.v[:, 0, :]
        te = V(c, cp(ex, r3(d.v)[:, :, P - 1]), t, *st_.busy)
        d.busy = [ta, te]
        tk2 = c.po.do(tt(k.v[:, :], k.v[:, :], e2.v[:, :], ALU.mult), te2, tm)
        e2.busy = [tk2]
        yield
        tke = []
        for half in range(2):
            b = tb.take()
            t = transposes(c, b.v, [k.v[:, (4 * half + j) * P:(4 * half + j + 1) * P] for j in range(4)], tk2, *b.busy)
            b.busy = [c.ac.do(act(ke.v[:, 512 * half:512 * (half + 1)], b.v[:, :], ACT.Copy), t, *ke.busy)]
            tke += b.busy
        k.busy = [t]
        st, tst = None, None
        for n in range(NS):
            if n:
                yield
            ns = slice(n * P, (n + 1) * P)
            ob = obs.take()
            oc, kc = slice(0, P), slice(P, 2 * P)
            tkv = mm_group(c, ob, [(ob.v[:, kc], ke.v[:, ns], v.v[:, ns])], *tke, tv, *ob.busy)
            items = [(ob.v[:, oc], acc.v[:, ns], v.v[:, ns])]
            if n:
                items.append((ob.v[:, oc], a.v[:, ns], st.v[:, :]))
            to = mm_group(c, ob, items, tacc, tv, ta, tst)
            nx = state.take()
            if n:
                t = V(c, stt(nx.v[:, :], st.v[:, :], ex[:, n:n + 1], ob.v[:, kc], ALU.mult, ALU.add), to, tkv, te, tst,
                      *nx.busy)
                st.busy = [t, to]
            else:
                t = V(c, cp(nx.v[:, :], ob.v[:, kc]), to, tkv, *nx.busy)
            st, tst = nx, t
            t2_ = c.ac.do(act(o.v[:, ns], ob.v[:, oc], ACT.Copy), to, tst, *o.busy)
            tss = c.ac.do(act(junk[:, :], ob.v[:, oc], ACT.Square, accum_out=st_.v[:, 1, n:n + 1]), to, tst,
                          *st_.busy, c.ac.last)
            ob.busy = [tss, tst]
        st.busy = [tst]
        q.busy, ke.busy, v.busy, acc.busy = [to, ta], [tkv], [to], [to]
        ss = st_.v[:, 1, :]
        t = V(c, ts(ss, ss, 1.0 / P, RMS_EPS, ALU.mult, ALU.add), tss)
        t = c.ac.do(act(ss, ss, ACT.Sqrt), t)
        yield
        t = V(c, lambda e: e.reciprocal(ss, ss), t)
        for n in range(NS):
            ns = slice(n * P, (n + 1) * P)
            t_ = V(c, stt(o.v[:, ns], o.v[:, ns], ss[:, n:n + 1], g.v[:, ns], ALU.mult, ALU.mult), t, t2_, tg)
        t = t_
        st_.busy, g.busy = [t, tst], [t]
        yield
        for half in range(2):
            b = tb.take()
            tt_ = transposes(c, b.v, [o.v[:, (4 * half + j) * P:(4 * half + j + 1) * P] for j in range(4)], t, *b.busy)
            hs = slice(512 * half, 512 * (half + 1))
            th = c.ac.do(act(c.XH[:, h, hs], b.v[:, :], ACT.Copy, scale=ogt[:, 0:1]), tt_, t2)
            tl = V(c, stt(c.XL[:, h, hs], b.v[:, :], ogt[:, 0:1], f32(c.XH[:, h, hs]), ALU.mult, ALU.subtract), th, tt_, t2)
            b.busy = [th, tl]
            for s in range(4 * half, 4 * half + 4):
                c.xt[s] = [th, tl]
        o.busy = [tt_]

    staggered([head(h) for h in range(8)], 8)


def layer_hgrn(c, i):
    c.phase()
    z, zt = c.scratch["z"], c.scratch["zt"]
    c.stage = c.buf("stage", [P, 512], 4)
    win = i["rec_w_in_2"][0]
    modes = ["feat"] * 4 + ["seq"] * 4
    dst = []
    for b in range(8):
        if b >= 4:
            dst.append(lambda j, at=512 * (b - 4): z[j * P:(j + 1) * P, at:at + 512])
        else:
            dst.append(lambda j, at=512 * b: zt[at + (j % 4) * P:at + (j % 4 + 1) * P, (j // 4) * 512:(j // 4 + 1) * 512])
    tok = project(c, [win[:, 512 * b:512 * (b + 1)] for b in range(8)], modes, dst, silu=(6, 7))
    hgrn(c, z, zt, tok, i["rec_lb_2"], i["rec_out_norm_2"][0])


def program(nc, i, consts, out, where, layers=(0, 1, 2, 3)):
    scratch = {
        "h": nc.dram_tensor("sc_h", [S, D], F32, kind="Internal").ap(),
        "z": nc.dram_tensor("sc_z", [S, 4096], F32, kind="Internal").ap(),
        "zt": nc.dram_tensor("sc_zt", [4096, S], F32, kind="Internal").ap(),
    }
    with ExitStack() as ctx:
        c = Ctx(nc, ctx, consts, where, scratch)
        pre = {0: i["norm_gain"][0], 1: i["norm_gain"][1], 2: i["norm_pre_2"][0], 3: i["norm_pre_2"][1]}
        w = start(c, i["x"][0], pre[layers[0]], column_blocks(i["even_w_in"][0]))
        for n, l in enumerate(layers):
            nxt = layers[n + 1] if n + 1 < len(layers) else None
            kw = {"next_gain": None if nxt is None else pre[nxt], "out": out if nxt is None else None}
            if l == 0:
                layer_even(c, i, w)
                layer_end(c, i["even_w_out"][0], i["p"][0, 0], i["ple_proj"][0], i["ple_gate"][0], **kw)
            elif l == 1:
                layer_odd(c, i)
                layer_end(c, i["odd_w_out"][0], i["p"][1, 0], i["ple_proj"][1], i["ple_gate"][1],
                          mid_gain=i["final_gain"], **kw)
            elif l == 2:
                layer_fox(c, i)
                layer_end(c, i["att_w_out_2"][0], i["p_2"][0, 0], i["ple_w_proj_2"][0], i["ple_w_gate_2"][0],
                          post_gain=i["norm_post_2"][0], **kw)
            else:
                layer_hgrn(c, i)
                layer_end(c, i["rec_w_out_2"][0], i["p_2"][1, 0], i["ple_w_proj_2"][1], i["ple_w_gate_2"][1],
                          post_gain=i["norm_post_2"][1], **kw)
        c.phase()
        c.stack.close()
        block = ctx.enter_context(nc.Block())
        block.sync(lambda e: c.sp.run(e))
        block.tensor(lambda e: c.pe.run(e))
        block.vector(lambda e: c.ve.run(e))
        block.scalar(lambda e: c.ac.run(e))
        block.gpsimd(lambda e: c.po.run(e))


_INS = ["x", "p", "norm_gain", "final_gain", "ple_proj", "ple_gate", "even_w_in", "even_w_out", "ret_gn_gain",
        "odd_mu", "odd_w_in", "odd_w_out", "rwkv_w0", "rwkv_w1", "rwkv_w2", "rwkv_a0", "rwkv_a1", "rwkv_a2",
        "rwkv_k_k", "rwkv_k_a", "rwkv_r_k", "rwkv_lnx_gain", "rwkv_lnx_bias", "p_2", "norm_pre_2", "norm_post_2",
        "att_w_in_2", "att_b_f_2", "att_w_out_2", "rec_w_in_2", "rec_lb_2", "rec_out_norm_2", "rec_w_out_2",
        "ple_w_proj_2", "ple_w_gate_2"]


def kernel(**inputs):
    import concourse.bacc as _bacc
    from concourse.bass_utils import run_bass_kernel_spmd as _run

    nc = _bacc.Bacc("TRN2", target_bir_lowering=False, num_devices=1)
    arrays, args = {}, {}
    for name in _INS:
        a = np.ascontiguousarray(inputs[name])
        arrays[f"in_{name}"] = a
        args[name] = nc.dram_tensor(f"in_{name}", a.shape, mybir.dt.from_np(a.dtype), kind="ExternalInput").ap()
    table, where = shape_constants()
    arrays["consts"] = table
    consts = nc.dram_tensor("consts", table.shape, F32, kind="ExternalInput").ap()
    out = nc.dram_tensor("out_0", (1, S, D), F32, kind="ExternalOutput").ap()
    program(nc, args, consts, out[0], where)
    r = _run(nc, [arrays], core_ids=[0])
    return r.results[0]["out_0"]
```
